# Optimizing a Trainium2 kernel written in Bass

```python
import math
import jax, jax.numpy as jnp
from jax import lax
import numpy as np

D_MODEL = 1024
BATCH = 1
SEQ = 256
DEPTH = 2

FOX_HEADS = 8
FOX_HEAD_DIM = 64
FOX_WIDTH = FOX_HEADS * FOX_HEAD_DIM
Q_BLOCK = 128
CONV_CHANNELS = D_MODEL // 2
CONV_WIDTH = 31
MLSTM_HEADS = 8
MLSTM_HEAD_DIM = 128
MLSTM_WIDTH = MLSTM_HEADS * MLSTM_HEAD_DIM
MLSTM_CONV_WIDTH = 4
MLSTM_CHUNK = 64
D_FF = 2816
N_EXPERTS = 8
TOP_K = 2
D_FF_EXPERT = 3584
EPS = 1e-6

IN0_WIDTH = 3 * FOX_WIDTH + FOX_HEADS + 2 * CONV_CHANNELS
IN1_WIDTH = 3 * MLSTM_WIDTH + 2 * MLSTM_HEADS

kernel_name = "fox_conformer_mlstm_moe_hybrid"

def rms_norm(x, g):
    xf = x.astype(jnp.float32)
    y = xf * lax.rsqrt(jnp.mean(xf * xf, axis=-1, keepdims=True) + EPS)
    return (y * g.astype(jnp.float32)).astype(x.dtype)

def layer_norm(x, g, b):
    xf = x.astype(jnp.float32)
    mu = jnp.mean(xf, axis=-1, keepdims=True)
    var = jnp.mean(jnp.square(xf - mu), axis=-1, keepdims=True)
    y = (xf - mu) * lax.rsqrt(var + EPS)
    return (y * g.astype(jnp.float32) + b.astype(jnp.float32)).astype(x.dtype)

def causal_depthwise_conv(x, w, b):
    width, ch = w.shape
    y = lax.conv_general_dilated(
        x, w[:, None, :].astype(x.dtype), window_strides=(1,), padding=[(width - 1, 0)],
        dimension_numbers=("NWC", "WIO", "NWC"), feature_group_count=ch)
    return y + b.astype(x.dtype)

def swiglu(h, w_gate, w_up, w_down):
    return (jax.nn.silu(h @ w_gate) * (h @ w_up)) @ w_down

def forgetting_attention(q, k, v, log_f):
    b_, h_, s_, dh = q.shape
    nb = s_ // Q_BLOCK
    c = jnp.cumsum(log_f, axis=-1)
    scale = dh ** -0.5
    qb = q.reshape(b_, h_, nb, Q_BLOCK, dh).transpose(2, 0, 1, 3, 4)
    cb = c.reshape(b_, h_, nb, Q_BLOCK).transpose(2, 0, 1, 3)
    key_pos = jnp.arange(s_)

    def one_block(args):
        q_blk, c_blk, blk = args
        logits = jnp.einsum("bhqd,bhkd->bhqk", q_blk, k,
                            preferred_element_type=jnp.float32) * scale
        logits = logits + (c_blk[..., :, None] - c[..., None, :])
        q_pos = blk * Q_BLOCK + jnp.arange(Q_BLOCK)
        logits = jnp.where(key_pos[None, :] <= q_pos[:, None], logits, -jnp.inf)
        p = jax.nn.softmax(logits, axis=-1)
        return jnp.einsum("bhqk,bhkd->bhqd", p.astype(v.dtype), v)

    out = lax.map(one_block, (qb, cb, jnp.arange(nb)))
    return out.transpose(1, 2, 0, 3, 4).reshape(b_, h_, s_, dh)

def mlstm_chunkwise(q, k, v, log_i, log_f):
    b_, h_, s_, dk = q.shape
    dv = v.shape[-1]
    L = MLSTM_CHUNK
    nc = s_ // L

    def chunks(t):
        return jnp.moveaxis(t.reshape(b_, h_, nc, L, *t.shape[3:]), 2, 0)

    qc = chunks(q.astype(jnp.float32))
    kc = chunks(k.astype(jnp.float32))
    vc = chunks(v.astype(jnp.float32))
    ic, fc = chunks(log_i), chunks(log_f)
    bcum = jnp.cumsum(fc, axis=-1)
    gtot = bcum[..., -1]
    a_end = gtot[..., None] - bcum + ic
    tri = jnp.tril(jnp.ones((L, L), dtype=bool))
    dmat = jnp.where(tri, bcum[..., :, None] - bcum[..., None, :] + ic[..., None, :], -jnp.inf)

    def step(carry, xs):
        C, n, m = carry
        q_, k_, v_, b_c, g_c, a_c, d_c = xs
        inter = b_c + m[..., None]
        m_t = jnp.maximum(inter, jnp.max(d_c, axis=-1))
        w_inter = jnp.exp(inter - m_t)
        w_intra = jnp.exp(d_c - m_t[..., None]) * jnp.einsum("bhld,bhsd->bhls", q_, k_)
        num = (w_inter[..., None] * jnp.einsum("bhvd,bhld->bhlv", C, q_)
               + jnp.einsum("bhls,bhsv->bhlv", w_intra, v_))
        nq = w_inter * jnp.einsum("bhd,bhld->bhl", n, q_) + jnp.sum(w_intra, axis=-1)
        h = num / jnp.maximum(jnp.abs(nq), jnp.exp(-m_t))[..., None]
        m_new = jnp.maximum(g_c + m, jnp.max(a_c, axis=-1))
        decay = jnp.exp(g_c + m - m_new)
        w_in = jnp.exp(a_c - m_new[..., None])
        C_new = decay[..., None, None] * C + jnp.einsum("bhs,bhsv,bhsd->bhvd", w_in, v_, k_)
        n_new = decay[..., None] * n + jnp.einsum("bhs,bhsd->bhd", w_in, k_)
        return (C_new, n_new, m_new), h

    init = (jnp.zeros((b_, h_, dv, dk), jnp.float32),
            jnp.zeros((b_, h_, dk), jnp.float32),
            jnp.zeros((b_, h_), jnp.float32))
    _, hs = lax.scan(step, init, (qc, kc, vc, bcum, gtot, a_end, dmat))
    return jnp.moveaxis(hs, 0, 2).reshape(b_, h_, s_, dv)

def even_mixer(h, w_in, b_f, dw_w, dw_b, cln_g, cln_b, w_out):
    b_, s_, _ = h.shape
    proj = h @ w_in
    q, k, v, f_pre, glu_in = jnp.split(
        proj, [FOX_WIDTH, 2 * FOX_WIDTH, 3 * FOX_WIDTH, 3 * FOX_WIDTH + FOX_HEADS], axis=-1)

    def heads(t):
        return t.reshape(b_, s_, FOX_HEADS, FOX_HEAD_DIM).transpose(0, 2, 1, 3)

    log_f = jax.nn.log_sigmoid((f_pre + b_f).astype(jnp.float32)).transpose(0, 2, 1)
    att = forgetting_attention(heads(q), heads(k), heads(v), log_f)
    att = att.transpose(0, 2, 1, 3).reshape(b_, s_, FOX_WIDTH)

    a, gate = jnp.split(glu_in, 2, axis=-1)
    u = a * jax.nn.sigmoid(gate)
    u = causal_depthwise_conv(u, dw_w, dw_b)
    u = jax.nn.silu(layer_norm(u, cln_g, cln_b))

    return jnp.concatenate([att, u], axis=-1) @ w_out

def odd_mixer(h, w_in, b_i, b_f, conv_w, conv_b, wq_head, wk_head, hnorm_g, w_out):
    b_, s_, _ = h.shape
    proj = h @ w_in
    u, v, o, i_pre, f_pre = jnp.split(
        proj, [MLSTM_WIDTH, 2 * MLSTM_WIDTH, 3 * MLSTM_WIDTH, 3 * MLSTM_WIDTH + MLSTM_HEADS], axis=-1)
    u = jax.nn.silu(causal_depthwise_conv(u, conv_w, conv_b))
    u = u.reshape(b_, s_, MLSTM_HEADS, MLSTM_HEAD_DIM)
    q = jnp.einsum("bshd,hde->bhse", u, wq_head)
    k = jnp.einsum("bshd,hde->bhse", u, wk_head) * (MLSTM_HEAD_DIM ** -0.5)
    vh = v.reshape(b_, s_, MLSTM_HEADS, MLSTM_HEAD_DIM).transpose(0, 2, 1, 3)
    log_i = (i_pre + b_i).astype(jnp.float32).transpose(0, 2, 1)
    log_f = jax.nn.log_sigmoid((f_pre + b_f).astype(jnp.float32)).transpose(0, 2, 1)
    h_tilde = mlstm_chunkwise(q, k, vh, log_i, log_f)
    h_tilde = h_tilde.transpose(0, 2, 1, 3).astype(h.dtype)
    og = jax.nn.sigmoid(o).reshape(b_, s_, MLSTM_HEADS, MLSTM_HEAD_DIM)
    hc = og * h_tilde
    hc = rms_norm(hc, hnorm_g.reshape(MLSTM_HEADS, MLSTM_HEAD_DIM))
    return hc.reshape(b_, s_, MLSTM_WIDTH) @ w_out

def moe_swiglu(h, router, e_gate, e_up, e_down):
    logits = (h @ router).astype(jnp.float32)
    top_vals, top_idx = lax.top_k(logits, TOP_K)
    gates = jax.nn.softmax(top_vals, axis=-1)
    combine = jnp.sum(jax.nn.one_hot(top_idx, N_EXPERTS, dtype=jnp.float32) * gates[..., None],
                      axis=-2).astype(h.dtype)
    y = jnp.zeros_like(h)
    for e in range(N_EXPERTS):
        y = y + combine[..., e:e + 1] * swiglu(h, e_gate[e], e_up[e], e_down[e])
    return y

def setup_inputs(seed: int = 0) -> dict:
    key = jax.random.key(seed)
    ks = iter(jax.random.split(key, 32))

    def nrm(shape, scale):
        return jax.random.normal(next(ks), shape, jnp.float32) * scale

    def gain(n):
        return 1.0 + nrm((n,), 0.02)

    D = D_MODEL
    return {
        "x": nrm((BATCH, SEQ, D), 1.0),
        "l0_norm1_g": gain(D),
        "l0_w_in": nrm((D, IN0_WIDTH), D ** -0.5),
        "l0_b_f": 2.0 + nrm((FOX_HEADS,), 0.5),
        "l0_dw_w": nrm((CONV_WIDTH, CONV_CHANNELS), CONV_WIDTH ** -0.5),
        "l0_dw_b": nrm((CONV_CHANNELS,), 0.02),
        "l0_cln_g": gain(CONV_CHANNELS),
        "l0_cln_b": nrm((CONV_CHANNELS,), 0.02),
        "l0_w_out": nrm((FOX_WIDTH + CONV_CHANNELS, D), (FOX_WIDTH + CONV_CHANNELS) ** -0.5),
        "l0_norm2_g": gain(D),
        "l0_w_gate": nrm((D, D_FF), D ** -0.5),
        "l0_w_up": nrm((D, D_FF), D ** -0.5),
        "l0_w_down": nrm((D_FF, D), D_FF ** -0.5),
        "l1_norm1_g": gain(D),
        "l1_w_in": nrm((D, IN1_WIDTH), D ** -0.5),
        "l1_b_i": nrm((MLSTM_HEADS,), 0.1),
        "l1_b_f": 3.0 + nrm((MLSTM_HEADS,), 0.5),
        "l1_conv_w": nrm((MLSTM_CONV_WIDTH, MLSTM_WIDTH), MLSTM_CONV_WIDTH ** -0.5),
        "l1_conv_b": nrm((MLSTM_WIDTH,), 0.02),
        "l1_wq_head": nrm((MLSTM_HEADS, MLSTM_HEAD_DIM, MLSTM_HEAD_DIM), MLSTM_HEAD_DIM ** -0.5),
        "l1_wk_head": nrm((MLSTM_HEADS, MLSTM_HEAD_DIM, MLSTM_HEAD_DIM), MLSTM_HEAD_DIM ** -0.5),
        "l1_hnorm_g": gain(MLSTM_WIDTH),
        "l1_w_out": nrm((MLSTM_WIDTH, D), MLSTM_WIDTH ** -0.5),
        "l1_norm2_g": gain(D),
        "l1_router": nrm((D, N_EXPERTS), D ** -0.5),
        "l1_e_gate": nrm((N_EXPERTS, D, D_FF_EXPERT), D ** -0.5),
        "l1_e_up": nrm((N_EXPERTS, D, D_FF_EXPERT), D ** -0.5),
        "l1_e_down": nrm((N_EXPERTS, D_FF_EXPERT, D), D_FF_EXPERT ** -0.5),
        "final_norm_g": gain(D),
    }

def reference(x, l0_norm1_g, l0_w_in, l0_b_f, l0_dw_w, l0_dw_b, l0_cln_g, l0_cln_b, l0_w_out,
              l0_norm2_g, l0_w_gate, l0_w_up, l0_w_down,
              l1_norm1_g, l1_w_in, l1_b_i, l1_b_f, l1_conv_w, l1_conv_b, l1_wq_head, l1_wk_head,
              l1_hnorm_g, l1_w_out, l1_norm2_g, l1_router, l1_e_gate, l1_e_up, l1_e_down,
              final_norm_g):
    for layer in range(DEPTH):
        if layer % 2 == 0:
            x = x + even_mixer(rms_norm(x, l0_norm1_g), l0_w_in, l0_b_f, l0_dw_w, l0_dw_b,
                               l0_cln_g, l0_cln_b, l0_w_out)
            x = x + swiglu(rms_norm(x, l0_norm2_g), l0_w_gate, l0_w_up, l0_w_down)
        else:
            x = x + odd_mixer(rms_norm(x, l1_norm1_g), l1_w_in, l1_b_i, l1_b_f, l1_conv_w,
                              l1_conv_b, l1_wq_head, l1_wk_head, l1_hnorm_g, l1_w_out)
            x = x + moe_swiglu(rms_norm(x, l1_norm2_g), l1_router, l1_e_gate, l1_e_up, l1_e_down)
    return rms_norm(x, final_norm_g)


_drawn_inputs = setup_inputs


def setup_inputs(seed=0):
    import zlib

    import numpy as np

    out = dict(_drawn_inputs(seed))
    spreads = {}
    factors = {'l1_b_i': 64.0,
     'l1_hnorm_g': 2.86,
     'final_norm_g': 7.426,
     'l0_cln_b': 2.674,
     'l1_norm2_g': 6.124}
    for name, (base, spread) in spreads.items():
        noise = np.random.default_rng([zlib.crc32(name.encode()), seed]).standard_normal(out[name].shape)
        drawn = base * np.exp(spread * noise) if base else spread * noise
        out[name] = __import__('jax').numpy.asarray(drawn.astype(out[name].dtype))
    for name, factor in factors.items():
        out[name] = (out[name] * factor).astype(out[name].dtype)
    return out
```

```python
from contextlib import ExitStack

import concourse.bass as bass
from concourse import mybir

ALU = mybir.AluOpType
ACT = mybir.ActivationFunctionType
AX_X = mybir.AxisListType.X
F32 = mybir.dt.float32
I32 = mybir.dt.int32

P = 128
EPS = 1e-6
NEG = -1e30
CAP = 80
RING = 7
TILE = 512
COLS = 4096


def bass_hybrid_trunk(nc, x, l0_norm1_g, l0_w_in, l0_b_f, l0_dw_w, l0_dw_b, l0_cln_g, l0_cln_b, l0_w_out,
                      l0_norm2_g, l0_w_gate, l0_w_up, l0_w_down, l1_norm1_g, l1_w_in, l1_b_i, l1_b_f,
                      l1_conv_w, l1_conv_b, l1_wq_head, l1_wk_head, l1_hnorm_g, l1_w_out, l1_norm2_g,
                      l1_router, l1_e_gate, l1_e_up, l1_e_down, final_norm_g, out):
    _, T, D = x.shape
    TT = T // P
    KD = D // P
    H = l0_b_f.shape[0]
    DH = 64
    FW = H * DH
    CC = l0_dw_w.shape[1]
    NC4 = CC // P
    TAPS = l0_dw_w.shape[0]
    TAPS1 = l1_conv_w.shape[0]
    DFF = l0_w_gate.shape[1]
    NF = DFF // P
    NE, _, DFE = l1_e_gate.shape
    GROUPS = DFE // TILE
    CPG = TILE // P
    CH = GROUPS * CPG
    ROUNDS = -(-T // CAP)
    assert TT == 2 and KD == 8 and H == 8 and NE == 8 and (3 * GROUPS) % RING == 0

    def wide(w, c0, n):
        return w[:, c0:c0 + n].rearrange("(k p) n -> p k n", p=P)

    front = []
    for c0 in (3 * FW + H, 3 * FW + H + CC, 0, FW, 2 * FW):
        front.append([(wide(l0_w_in, c0, TILE), 0, TILE)])
    for half in range(2):
        front.append([(wide(l0_w_out, half * TILE, TILE), 0, TILE)])
    PAIRS = DFF // 256
    for p in range(PAIRS):
        front.append([(wide(l0_w_gate, p * 256, 256), 0, 256), (wide(l0_w_up, p * 256, 256), KD * 256, 256)])
    DOWNS = -(-NF // 4)
    for t in range(DOWNS):
        n = min(4, NF - 4 * t)
        front.append([(l0_w_down[t * 512:t * 512 + n * P, :].rearrange("(k p) n -> p k n", p=P), 0, D)])
    for c0 in range(0, 3 * D, TILE):
        front.append([(wide(l1_w_in, c0, TILE), 0, TILE)])
    front.append([(l1_wq_head.rearrange("h d e -> d h e"), 0, P), (l1_wk_head.rearrange("h d e -> d h e"), H * P, P)])
    for half in range(2):
        front.append([(wide(l1_w_out, half * TILE, TILE), 0, TILE)])
    T_GLU, T_Q, T_K, T_V, T_OUT0, T_PAIR = 0, 2, 3, 4, 5, 7
    T_DOWN = T_PAIR + PAIRS
    T_U = T_DOWN + DOWNS
    T_V1, T_O1, T_QK1, T_OUT1 = T_U + 2, T_U + 4, T_U + 6, T_U + 7
    FRONT = T_OUT1 + 2
    assert FRONT == len(front)

    with ExitStack() as ctx:
        def sb(name, shape, dt=F32):
            return ctx.enter_context(nc.sbuf_tensor(name, shape, dt))

        def sem(name):
            return ctx.enter_context(nc.semaphore(name))

        ring = sb("ring", [P, RING, COLS])
        xres = sb("xres", [P, TT, D])
        xn = sb("xn", [P, TT, D])
        hT = sb("hT", [P, KD, T])
        work = sb("work", [P, 13880])
        ident = sb("ident", [P, P])
        upper = sb("upper", [P, P])
        ones = sb("ones", [P, P])
        ch_mean = sb("ch_mean", [P, P])
        mask_qk = sb("mask_qk", [P, P])
        mask_kq = sb("mask_kq", [P, P])
        neg_sel = sb("neg_sel", [H, H, P])
        slot_no = sb("slot_no", [P, CAP])
        pick_order = sb("pick_order", [P, TT, NE])
        minus_half = sb("minus_half", [P, T])
        rows1 = sb("rows1", [P, P])
        rows2 = sb("rows2", [P, P])
        prm = sb("prm", [P, P])
        dww = sb("dww", [P, P])
        wf = sb("wf", [P, KD, H])
        wif = sb("wif", [P, KD, 2 * H])
        wr = sb("wr", [P, KD, NE])
        bf0 = sb("bf0", [P, TT, H])
        bif1 = sb("bif1", [P, TT, 2 * H])
        small = sb("small", [P, 40, TT * H])
        cT = sb("cT", [H, T])
        aT = sb("aT", [H, T])
        GT = sb("GT", [H, T])
        ss = sb("ss", [P, 8, TT])
        cur = sb("cur", [P, 2, TT])
        flag = sb("flag", [P, 2], I32)

        def region(start, *dims):
            n = 1
            for d in dims:
                n *= d
            v = work[:, start:start + n]
            if len(dims) == 2:
                v = v.rearrange("p (a b) -> p a b", a=dims[0])
            if len(dims) == 3:
                v = v.rearrange("p (a b c) -> p a b c", a=dims[0], b=dims[1])
            return v

        qT0 = region(0, NC4, T)
        kT0 = region(1024, NC4, T)
        v0 = region(2048, TT, FW)
        PAD0 = TAPS - 1
        upad = region(3072, NC4, T + PAD0)
        conv = region(4216, NC4, T)
        lnc = region(5240, NC4, T)
        lnsq = region(6264, NC4, T)
        catT = region(7288, KD, T)
        probs = region(9336, 2, 3 * P)
        probsT = region(10104, 2, 3 * P)
        att = region(10872, TT, FW)
        glu_sg = region(11896, NC4, T)
        lnvar = region(12920, T)
        lnrstd = region(13176, T)
        hid = region(0, NF, T)
        dsg = region(NF * T, 4, T)
        PAD1 = TAPS1 - 1
        upad1 = region(0, KD, T + PAD1)
        uT = region(2072, KD, T)
        qT1 = region(4120, KD, T)
        kT1 = region(6168, KD, T)
        v_aug = region(8216, TT, H, P + 1)
        og = region(10280, TT, D)
        dec = region(12328, 2, 3 * P)
        wts = region(13096, 2, 3 * P)
        num = region(0, TT, H, P + 1)
        hc = region(4120, TT, D)
        hsq = region(6168, TT, D)
        catT1 = region(2072, KD, T)
        xT = region(0, KD, CAP)
        hidE = region(640, 4, CAP)
        sil = region(960, 4, CAP)
        yT = region(1280, KD, CAP)
        ye = region(1920, D)
        disp = region(2944, TT, CAP)
        comb = region(3104, TT, CAP)
        combT = region(3264, T)
        gain_bc = region(3520, KD, CAP)
        gfin = region(4160, D)

        ps = [ctx.enter_context(nc.psum_tensor(f"bank{b}", [P, 512], F32)) for b in range(8)]

        G_NORM = [0, 8, 16, 24]
        C_DWB, C_CLNG, C_CLNB, C_CB1, C_HN, C_CW1 = 32, 36, 40, 44, 52, 60
        N_ROWS1 = C_CW1 + TAPS1 * KD
        N_ROWS2 = TAPS * NC4

        def S(i):
            return small[:, i, :]

        def S3(i):
            return small[:, i, :].rearrange("p (t h) -> p t h", t=TT)

        landed = [sem(f"landed{i}") for i in range(RING)]
        tiles_used = sem("tiles_used")
        x_in = sem("x_in")
        params_in = sem("params_in")
        small_in = sem("small_in")
        gfin_in = sem("gfin_in")
        ident_ready = sem("ident_ready")
        const_ready = sem("const_ready")
        pool_chain = sem("pool_chain")
        dve_chain = sem("dve_chain")
        act_chain = sem("act_chain")
        prm_T = sem("prm_T")
        prm_ready = sem("prm_ready")
        sq_done = sem("sq_done")
        var_ready = sem("var_ready")
        rstd_ready = sem("rstd_ready")
        xn_ready = sem("xn_ready")
        xT_ready = sem("xT_ready")
        hT_act = sem("hT_act")
        hT_dve = sem("hT_dve")
        gate_pre = sem("gate_pre")
        absz_ready = sem("absz_ready")
        ln_ready = sem("ln_ready")
        logf_ready = sem("logf_ready")
        cum_ready = sem("cum_ready")
        cum_copied = sem("cum_copied")
        cumT_ready = sem("cumT_ready")
        cT_ready = sem("cT_ready")
        glu_ready = sem("glu_ready")
        sg_ready = sem("sg_ready")
        u_ready = sem("u_ready")
        conv_tap = sem("conv_tap")
        qk_ready = sem("qk_ready")
        qk_copied = sem("qk_copied")
        v_ready = sem("v_ready")
        v_copied = sem("v_copied")
        ln_mean = sem("ln_mean")
        lnc_ready = sem("lnc_ready")
        lnsq_ready = sem("lnsq_ready")
        ln_var = sem("ln_var")
        lnvar_ready = sem("lnvar_ready")
        lnrstd_ready = sem("lnrstd_ready")
        ln_scaled = sem("ln_scaled")
        convT_ready = sem("convT_ready")
        scores_ready = sem("scores_ready")
        max_ready = sem("max_ready")
        exp_ready = sem("exp_ready")
        pT_ready = sem("pT_ready")
        pT_copied = sem("pT_copied")
        pv_ready = sem("pv_ready")
        att_ready = sem("att_ready")
        attT_ready = sem("attT_ready")
        attT_copied = sem("attT_copied")
        proj_ready = sem("proj_ready")
        res_added = sem("res_added")
        gu_ready = sem("gu_ready")
        dsg_ready = sem("dsg_ready")
        hid_ready = sem("hid_ready")
        pads_ready = sem("pads_ready")
        u1_ready = sem("u1_ready")
        u1_copied = sem("u1_copied")
        conv1_tap = sem("conv1_tap")
        uT_ready = sem("uT_ready")
        v1_ready = sem("v1_ready")
        v1_copied = sem("v1_copied")
        o1_ready = sem("o1_ready")
        og_ready = sem("og_ready")
        qk1_ready = sem("qk1_ready")
        qk1_copied = sem("qk1_copied")
        gT_ready = sem("gT_ready")
        gt_back = sem("gt_back")
        m_ready = sem("m_ready")
        enm_ready = sem("enm_ready")
        st_ready = sem("st_ready")
        ex_ready = sem("ex_ready")
        dec_ready = sem("dec_ready")
        w_ready = sem("w_ready")
        num_ready = sem("num_ready")
        num_copied = sem("num_copied")
        hc_ready = sem("hc_ready")
        hsq_ready = sem("hsq_ready")
        hvar_ready = sem("hvar_ready")
        hrstd_ready = sem("hrstd_ready")
        hn_ready = sem("hn_ready")
        hcT_ready = sem("hcT_ready")
        hcT_act = sem("hcT_act")
        hcT_dve = sem("hcT_dve")
        logits_ready = sem("logits_ready")
        diff_ready = sem("diff_ready")
        e2_ready = sem("e2_ready")
        mask_ready = sem("mask_ready")
        pos_ready = sem("pos_ready")
        flag_ready = sem("flag_ready")
        gain_ready = sem("gain_ready")
        cur_ready = sem("cur_ready")
        round_ready = sem("round_ready")
        route_ready = sem("route_ready")
        disp_done = sem("disp_done")
        xTe_ready = sem("xTe_ready")
        combT_done = sem("combT_done")
        combT_ready = sem("combT_ready")
        egu_ready = sem("egu_ready")
        sil_ready = sem("sil_ready")
        hidE_ready = sem("hidE_ready")
        yT_done = sem("yT_done")
        yT_dve = sem("yT_dve")
        yT_act = sem("yT_act")
        yt_done = sem("yt_done")
        ye_dve = sem("ye_dve")
        ye_act = sem("ye_act")
        y_done = sem("y_done")
        y_added = sem("y_added")
        moe_done = sem("moe_done")
        fin_ready = sem("fin_ready")
        stored = sem("stored")

        def slot(t):
            return t % RING

        def tile(t, k, n):
            return ring[:, slot(t), 0:k * n].rearrange("p (k n) -> p k n", k=k)

        slot_count = [0] * RING
        landed_at = []
        for t, parts in enumerate(front):
            slot_count[slot(t)] += 16 * len(parts)
            landed_at.append(slot_count[slot(t)])
        PER_PASS = 3 * GROUPS * 16 // RING

        def expert_tile(j):
            s = (FRONT + j) % RING
            return s, slot_count[s] + 16 * (j // RING + 1)

        block = ctx.enter_context(nc.Block())

        @block.sync
        def _(sp):
            for t in range(TT):
                sp.dma_start(xres[:, t, :], x[0, t * P:(t + 1) * P, :]).then_inc(x_in, 16)
            for t, parts in enumerate(front):
                if t >= RING:
                    sp.wait_ge(tiles_used, t - RING + 1)
                for src, off, n in parts:
                    k = src.shape[1]
                    dst = ring[:, slot(t), off:off + k * n].rearrange("p (k n) -> p k n", k=k)
                    sp.dma_start(dst, src).then_inc(landed[slot(t)], 16)

            def load_expert(it, e):
                for g in range(GROUPS):
                    for kind, w in enumerate((l1_e_gate, l1_e_up, l1_e_down)):
                        j = 3 * g + kind
                        s, _ = expert_tile(j)
                        sp.wait_ge(tiles_used, it * (3 * GROUPS) + (FRONT + j - RING + 1))
                        row = w[bass.ds(e, 1), :, :].rearrange("a r c -> (a r) c")
                        if kind < 2:
                            src = row[:, g * TILE:(g + 1) * TILE].rearrange("(k p) n -> p k n", p=P)
                            dst = ring[:, s, :].rearrange("p (k n) -> p k n", k=KD)
                        else:
                            src = row[g * TILE:(g + 1) * TILE, :].rearrange("(k p) n -> p k n", p=P)
                            dst = ring[:, s, :].rearrange("p (k n) -> p k n", k=CPG)
                        sp.dma_start(dst, src).then_inc(landed[s], 16)

            with sp.Fori(0, NE) as e:
                load_expert(e, e)
            sp.wait_ge(flag_ready, 1)
            most = sp.value_load(flag[0:1, 0:1], min_val=0, max_val=T)
            with sp.If(most > CAP):
                with sp.Fori(1, ROUNDS) as r:
                    with sp.Fori(0, NE) as e:
                        load_expert(r * NE + e, e)
            for t in range(TT):
                sp.wait_ge(fin_ready, t + 1)
                sp.dma_start(out[0, t * P:(t + 1) * P, :], xn[:, t, :]).then_inc(stored, 16)
            sp.wait_ge(stored, 16 * TT)

        @block.gpsimd
        def _(pool):
            pool.memset(ident[:, :], 0.0).then_inc(pool_chain, 1)
            pool.wait_ge(pool_chain, 1)
            pool.affine_select(out=ident[:, :], in_=ident[:, :], compare_op=ALU.not_equal, fill=1.0, base=0,
                               pattern=[[-1, P]], channel_multiplier=1).then_inc(ident_ready, 1)
            pool.memset(minus_half[:, :], -0.5).then_inc(pool_chain, 1)
            pool.memset(upper[:, :], 1.0).then_inc(pool_chain, 1)
            pool.memset(mask_qk[:, :], 0.0).then_inc(pool_chain, 1)
            pool.memset(mask_kq[:, :], 0.0).then_inc(pool_chain, 1)
            pool.memset(neg_sel[:, :, :], 0.0).then_inc(pool_chain, 1)
            pool.memset(ones[:, :], 1.0).then_inc(pool_chain, 1)
            pool.memset(ch_mean[:, :], 1.0 / CC).then_inc(pool_chain, 1)
            pool.memset(upad[:, :, 0:PAD0], 0.0).then_inc(pool_chain, 1)
            pool.iota(slot_no[:, :], pattern=[[1, CAP]], base=0, channel_multiplier=0,
                      allow_small_or_imprecise_dtypes=True).then_inc(pool_chain, 1)
            pool.iota(pick_order[:, :, :], pattern=[[0, TT], [-1, NE]], base=NE, channel_multiplier=0,
                      allow_small_or_imprecise_dtypes=True).then_inc(pool_chain, 1)
            pool.wait_ge(pool_chain, 11)
            pool.affine_select(out=upper[:, :], in_=upper[:, :], compare_op=ALU.is_ge, fill=0.0, base=0,
                               pattern=[[1, P]], channel_multiplier=-1).then_inc(const_ready, 1)
            pool.affine_select(out=mask_qk[:, :], in_=mask_qk[:, :], compare_op=ALU.is_ge, fill=NEG, base=0,
                               pattern=[[-1, P]], channel_multiplier=1).then_inc(const_ready, 1)
            pool.affine_select(out=mask_kq[:, :], in_=mask_kq[:, :], compare_op=ALU.is_ge, fill=NEG, base=0,
                               pattern=[[1, P]], channel_multiplier=-1).then_inc(const_ready, 1)
            pool.affine_select(out=neg_sel[:, :, :], in_=neg_sel[:, :, :], compare_op=ALU.not_equal, fill=-1.0,
                               base=0, pattern=[[-1, H], [0, P]], channel_multiplier=1).then_inc(const_ready, 1)

            def rstd_of_norm(i):
                pool.wait_ge(var_ready, i + 1)
                pool.tensor_tensor(ss[:, 2, :], ss[:, 1, :], minus_half[:, 0:TT], ALU.pow).then_inc(rstd_ready, 1)

            rstd_of_norm(0)
            pool.wait_ge(lnvar_ready, 1)
            pool.tensor_tensor(lnrstd, lnvar, minus_half[:, :], ALU.pow).then_inc(lnrstd_ready, 1)
            rstd_of_norm(1)
            pool.wait_ge(res_added, 8)
            pool.memset(upad1[:, :, 0:PAD1], 0.0).then_inc(pads_ready, 1)
            pool.memset(v_aug[:, :, :, P:P + 1], 1.0).then_inc(pads_ready, 1)
            rstd_of_norm(2)
            pool.wait_ge(hvar_ready, 1)
            pool.tensor_tensor(S(33), S(32), minus_half[:, 0:TT * H], ALU.pow).then_inc(hrstd_ready, 1)
            rstd_of_norm(3)
            rstd_of_norm(4)

        @block.scalar
        def _(act):
            def row(dst, src):
                act.dma_start(dst, src.rearrange("(r p) -> r p", p=P)).then_inc(params_in, 16)

            for i, g in enumerate((l0_norm1_g, l0_norm2_g, l1_norm1_g, l1_norm2_g)):
                row(rows1[G_NORM[i]:G_NORM[i] + KD, :], g)
            row(rows1[C_DWB:C_DWB + NC4, :], l0_dw_b)
            row(rows1[C_CLNG:C_CLNG + NC4, :], l0_cln_g)
            row(rows1[C_CLNB:C_CLNB + NC4, :], l0_cln_b)
            row(rows1[C_CB1:C_CB1 + KD, :], l1_conv_b)
            row(rows1[C_HN:C_HN + KD, :], l1_hnorm_g)
            row(rows1[C_CW1:N_ROWS1, :], l1_conv_w.rearrange("t c -> (t c)"))
            row(rows2[0:N_ROWS2, :], l0_dw_w.rearrange("t c -> (t c)"))
            act.dma_start(wf[:, :, :], wide(l0_w_in, 3 * FW, H)).then_inc(small_in, 16)
            act.dma_start(wif[:, :, :], wide(l1_w_in, 3 * D, 2 * H)).then_inc(small_in, 16)
            act.dma_start(wr[:, :, :], wide(l1_router, 0, NE)).then_inc(small_in, 16)
            for t in range(TT):
                act.dma_start(bf0[:, t, :], l0_b_f.partition_broadcast(P)).then_inc(small_in, 16)
                act.dma_start(bif1[:, t, 0:H], l1_b_i.partition_broadcast(P)).then_inc(small_in, 16)
                act.dma_start(bif1[:, t, H:2 * H], l1_b_f.partition_broadcast(P)).then_inc(small_in, 16)

            def norm_squares(i):
                if i == 0:
                    act.wait_ge(x_in, 16 * TT)
                elif i < 4:
                    act.wait_ge(res_added, 4 * i)
                else:
                    act.wait_ge(moe_done, 1)
                for t in range(TT):
                    act.activation(xn[:, t, :], xres[:, t, :], ACT.Square,
                                   accum_out=ss[:, 0, t:t + 1]).then_inc(sq_done, 1)

            def norm_gains(i):
                for b in (0, 2):
                    act.wait_ge(xT_ready, 4 * i + b + 1)
                    for k in (2 * b, 2 * b + 1):
                        act.activation(hT[:, k, :], ps[4 + b][:, (k % 2) * T:(k % 2 + 1) * T], ACT.Copy,
                                       scale=prm[:, G_NORM[i] + k:G_NORM[i] + k + 1]).then_inc(hT_act, 1)

            def log_sigmoid_part(i, az, e, l):
                act.wait_ge(absz_ready, i + 1)
                act.activation(S(e), S(az), ACT.Exp).then_inc(act_chain, 1)
                act.wait_ge(act_chain, i + 1)
                act.activation(S(l), S(e), ACT.Ln, bias=1.0).then_inc(ln_ready, 1)

            norm_squares(0)
            act.wait_ge(prm_ready, 2)
            norm_gains(0)
            log_sigmoid_part(0, 1, 2, 3)
            for c in range(NC4):
                act.wait_ge(glu_ready, c + 1)
                act.activation(glu_sg[:, c, :], ps[1 + c][:, T:2 * T], ACT.Sigmoid).then_inc(sg_ready, 1)
            for c in range(NC4):
                act.wait_ge(qk_ready, c + 1)
                b = (5, 6, 7, 0)[c]
                act.activation(qT0[:, c, :], ps[b][:, 0:T], ACT.Copy, scale=DH ** -0.5).then_inc(qk_copied, 1)
                act.activation(kT0[:, c, :], ps[b][:, T:2 * T], ACT.Copy).then_inc(qk_copied, 1)
            for t in range(TT):
                act.wait_ge(v_ready, t + 1)
                act.activation(v0[:, t, :], ps[1 + t][:, :], ACT.Copy).then_inc(v_copied, 1)
            for h in range(H):
                act.wait_ge(max_ready, h + 1)
                if h >= 2:
                    act.wait_ge(pT_ready, h - 1)
                b = (0, 5)[h % 2]
                act.activation(probs[:, h % 2, 0:P], ps[b][:, 0:P], ACT.Exp, bias=S3(5)[:, 0, h:h + 1],
                               accum_out=S3(6)[:, 0, h:h + 1]).then_inc(exp_ready, 1)
                act.activation(probs[:, h % 2, P:3 * P], ps[b][:, P:3 * P], ACT.Exp, bias=S3(5)[:, 1, h:h + 1],
                               accum_out=S3(6)[:, 1, h:h + 1]).then_inc(exp_ready, 1)
                if h == 1:
                    act.wait_ge(lnc_ready, 1)
                    act.activation(lnsq, lnc, ACT.Square).then_inc(lnsq_ready, 1)
            act.wait_ge(ln_scaled, 1)
            for c in range(NC4):
                act.activation(catT[:, NC4 + c, :], conv[:, c, :], ACT.Silu, scale=prm[:, C_CLNG + c:C_CLNG + c + 1],
                               bias=prm[:, C_CLNB + c:C_CLNB + c + 1]).then_inc(convT_ready, 1)
            act.wait_ge(attT_ready, 1)
            act.activation(catT[:, 0:2, :].rearrange("p a b -> p (a b)"), ps[0][:, :], ACT.Copy).then_inc(attT_copied, 1)
            norm_squares(1)
            norm_gains(1)
            for c in range(NF):
                act.wait_ge(gu_ready, c + 1)
                if c >= 4:
                    act.wait_ge(hid_ready, c - 3)
                act.activation(dsg[:, c % 4, :], ps[c % 4][:, 0:T], ACT.Silu).then_inc(dsg_ready, 1)
            norm_squares(2)
            norm_gains(2)
            act.wait_ge(pads_ready, 2)
            for c in range(KD // 2):
                act.wait_ge(u1_ready, c + 1)
                act.activation(upad1[:, 2 * c:2 * c + 2, PAD1:PAD1 + T],
                               ps[1 + c][:, :].rearrange("p (a b) -> p a b", a=2), ACT.Copy).then_inc(u1_copied, 1)
            log_sigmoid_part(1, 11, 12, 13)
            for n in range(4):
                act.wait_ge(v1_ready, n + 1)
                half, t = n // 2, n % 2
                act.activation(v_aug[:, t, 4 * half:4 * half + 4, 0:P],
                               ps[(5, 6, 7, 1)[n]][:, :].rearrange("p (h d) -> p h d", h=4), ACT.Copy).then_inc(v1_copied, 1)
            for c in range(KD):
                act.wait_ge(conv1_tap, (TAPS1 - 1) * KD + c + 1)
                act.activation(uT[:, c, :], uT[:, c, :], ACT.Silu,
                               bias=prm[:, C_CB1 + c:C_CB1 + c + 1]).then_inc(uT_ready, 1)
            for n in range(4):
                act.wait_ge(o1_ready, n + 1)
                half, t = n // 2, n % 2
                act.activation(og[:, t, half * 512:half * 512 + 512], ps[2 + n][:, :], ACT.Sigmoid).then_inc(og_ready, 1)
            for h in range(H):
                act.wait_ge(qk1_ready, h + 1)
                b = (6, 7, 1, 2)[h % 4]
                act.activation(qT1[:, h, :], ps[b][:, 0:T], ACT.Copy).then_inc(qk1_copied, 1)
                act.activation(kT1[:, h, :], ps[b][:, T:2 * T], ACT.Copy, scale=P ** -0.5).then_inc(qk1_copied, 1)
            act.wait_ge(m_ready, 1)
            act.activation(S(21), S(20), ACT.Exp, scale=-1.0).then_inc(enm_ready, 1)

            def num_copy(h):
                act.wait_ge(num_ready, h + 1)
                act.activation(num[:, :, h, :], ps[5 + h % 2][:, :].rearrange("p (t d) -> p t d", t=TT)[:, :, 0:P + 1],
                               ACT.Copy).then_inc(num_copied, 1)

            for h in range(H):
                act.wait_ge(ex_ready, h + 1)
                if h >= 2:
                    act.wait_ge(w_ready, h - 1)
                act.activation(dec[:, h % 2, 0:2 * P], ps[3 + h % 2][:, 0:2 * P], ACT.Exp,
                               bias=S3(16)[:, 0, h:h + 1]).then_inc(act_chain, 1)
                act.activation(dec[:, h % 2, 2 * P:3 * P], ps[3 + h % 2][:, 2 * P:3 * P], ACT.Exp,
                               bias=S3(16)[:, 1, h:h + 1]).then_inc(dec_ready, 1)
                if h >= 1:
                    num_copy(h - 1)
            num_copy(H - 1)
            act.wait_ge(hc_ready, 1)
            for t in range(TT):
                act.activation(hsq[:, t, :], hc[:, t, :], ACT.Square).then_inc(hsq_ready, 1)
            for b in (0, 2):
                act.wait_ge(hcT_ready, b + 1)
                for k in (2 * b, 2 * b + 1):
                    act.activation(catT1[:, k, :], ps[4 + b][:, (k % 2) * T:(k % 2 + 1) * T], ACT.Copy,
                                   scale=prm[:, C_HN + k:C_HN + k + 1]).then_inc(hcT_act, 1)
            norm_squares(3)
            act.wait_ge(xn_ready, 8)
            act.dma_start(gfin, final_norm_g.partition_broadcast(P)).then_inc(gfin_in, 16)
            norm_gains(3)
            act.wait_ge(diff_ready, 1)
            act.activation(ss[:, 4, :], ss[:, 3, :], ACT.Exp).then_inc(e2_ready, 1)

            def expert(it):
                act.wait_ge(combT_done, it + 1)
                act.activation(combT[0:CAP, :], ps[5][0:CAP, 0:T], ACT.Copy).then_inc(combT_ready, 1)
                for c in range(CH):
                    act.wait_ge(egu_ready, it * CH + (c + 1))
                    if c >= 4:
                        act.wait_ge(hidE_ready, it * CH + (c - 3))
                    act.activation(sil[:, c % 4, :], ps[c % 2][:, 0:CAP], ACT.Silu).then_inc(sil_ready, 1)
                act.wait_ge(yT_done, it + 1)
                act.activation(yT[:, 4:8, :].rearrange("p a b -> p (a b)"), ps[3][:, 0:4 * CAP],
                               ACT.Copy).then_inc(yT_act, 1)
                act.wait_ge(yt_done, it * 2 + 2)
                act.activation(ye[0:CAP, 512:1024], ps[5][0:CAP, :], ACT.Copy).then_inc(ye_act, 1)

            with act.Fori(0, NE) as e:
                expert(e)
            act.wait_ge(flag_ready, 1)
            most = act.value_load(flag[0:1, 0:1], min_val=0, max_val=T)
            with act.If(most > CAP):
                with act.Fori(1, ROUNDS) as r:
                    with act.Fori(0, NE) as e:
                        expert(r * NE + e)
            norm_squares(4)

        @block.vector
        def _(dve):
            links = [0]

            def link(ins):
                links[0] += 1
                ins.then_inc(dve_chain, 1)
                dve.wait_ge(dve_chain, links[0])

            def bc(ap, n):
                return ap.unsqueeze(2).broadcast_to([ap.shape[0], ap.shape[1], n])

            def norm_scale(i):
                dve.wait_ge(sq_done, 2 * i + 2)
                dve.tensor_scalar(ss[:, 1, :], ss[:, 0, :], 1.0 / D, EPS, ALU.mult, ALU.add).then_inc(var_ready, 1)
                dve.wait_ge(rstd_ready, i + 1)
                if i == 4:
                    return
                for t in range(TT):
                    dve.tensor_scalar(xn[:, t, :], xres[:, t, :], ss[:, 2, t:t + 1], None, ALU.mult).then_inc(xn_ready, 1)

            def norm_gains(i):
                for b in (1, 3):
                    dve.wait_ge(xT_ready, 4 * i + b + 1)
                    for k in (2 * b, 2 * b + 1):
                        dve.tensor_scalar(hT[:, k, :], ps[4 + b][:, (k % 2) * T:(k % 2 + 1) * T],
                                          prm[:, G_NORM[i] + k:G_NORM[i] + k + 1], None, ALU.mult).then_inc(hT_dve, 1)

            def add_residual(stage, banks):
                for n in range(4):
                    dve.wait_ge(proj_ready, 4 * stage + n + 1)
                    half, t = n // 2, n % 2
                    v = xres[:, t, half * 512:(half + 1) * 512]
                    dve.tensor_tensor(v, v, ps[banks[n]][:, :], ALU.add).then_inc(res_added, 1)

            def neg_abs(i, z, az):
                dve.scalar_tensor_tensor(out=S(az), in0=S(z), scalar=-1.0, in1=S(z), op0=ALU.mult,
                                         op1=ALU.min).then_inc(absz_ready, 1)

            def log_f(i, z, l, lf):
                dve.wait_ge(ln_ready, i + 1)
                dve.scalar_tensor_tensor(out=S(lf), in0=S(z), scalar=0.0, in1=S(l), op0=ALU.min,
                                         op1=ALU.subtract).then_inc(logf_ready, 1)

            dve.wait_ge(prm_T, 1)
            dve.tensor_copy(prm[:, 0:N_ROWS1], ps[7][:, 0:N_ROWS1]).then_inc(prm_ready, 1)
            dve.tensor_copy(dww[:, 0:N_ROWS2], ps[7][:, P:P + N_ROWS2]).then_inc(prm_ready, 1)
            norm_scale(0)
            dve.wait_ge(prm_ready, 2)
            norm_gains(0)
            dve.wait_ge(small_in, 16 * 9)
            dve.wait_ge(gate_pre, 1)
            link(dve.tensor_tensor(S3(0), ps[0][:, 0:TT * H].rearrange("p (t h) -> p t h", t=TT), bf0[:, :, :], ALU.add))
            neg_abs(0, 0, 1)
            log_f(0, 0, 3, 4)

            def glu(c):
                if c == 0:
                    dve.wait_ge(pool_chain, 11)
                dve.wait_ge(sg_ready, c + 1)
                dve.tensor_tensor(upad[:, c, PAD0:PAD0 + T], ps[1 + c][:, 0:T], glu_sg[:, c, :], ALU.mult).then_inc(u_ready, 1)

            glu(0)
            dve.wait_ge(cum_ready, 1)
            dve.tensor_copy(S(7), ps[0][:, 16:16 + TT * H]).then_inc(cum_copied, 1)
            glu(1)
            glu(2)
            dve.wait_ge(cumT_ready, 1)
            dve.tensor_copy(cT[:, :], ps[0][0:H, 64:64 + T]).then_inc(cT_ready, 1)
            glu(3)
            dve.wait_ge(u_ready, NC4)
            for j in range(TAPS):
                for c in range(NC4):
                    w = dww[:, j * NC4 + c:j * NC4 + c + 1]
                    if j == 0:
                        dve.tensor_scalar(conv[:, c, :], upad[:, c, 0:T], w, prm[:, C_DWB + c:C_DWB + c + 1],
                                          ALU.mult, ALU.add).then_inc(conv_tap, 1)
                    else:
                        dve.wait_ge(conv_tap, NC4 * (j - 1) + c + 1)
                        dve.scalar_tensor_tensor(out=conv[:, c, :], in0=upad[:, c, j:j + T], scalar=w,
                                                 in1=conv[:, c, :], op0=ALU.mult, op1=ALU.add).then_inc(conv_tap, 1)
            dve.wait_ge(conv_tap, NC4 * TAPS)
            dve.wait_ge(ln_mean, 1)
            dve.tensor_tensor(lnc, conv, ps[3][:, 0:T].unsqueeze(1).broadcast_to([P, NC4, T]),
                              ALU.subtract).then_inc(lnc_ready, 1)

            def fox_max(h):
                dve.wait_ge(scores_ready, h + 1)
                b = (0, 5)[h % 2]
                dve.tensor_reduce(S3(5)[:, 0, h:h + 1], ps[b][:, 0:P], AX_X, ALU.max, negate=True).then_inc(dve_chain, 1)
                dve.tensor_reduce(S3(5)[:, 1, h:h + 1], ps[b][:, P:3 * P], AX_X, ALU.max, negate=True).then_inc(max_ready, 1)
                links[0] += 1

            def fox_pT(h):
                dve.wait_ge(pT_ready, h + 1)
                if h >= 2:
                    dve.wait_ge(pv_ready, h - 1)
                dve.tensor_copy(probsT[:, h % 2, :], ps[6 + h % 2][:, 0:3 * P]).then_inc(pT_copied, 1)

            for h in range(H + 1):
                if h < H:
                    fox_max(h)
                if h >= 1:
                    fox_pT(h - 1)
                if h == 5:
                    dve.wait_ge(ln_var, 1)
                    dve.tensor_scalar(lnvar, ps[4][:, 0:T], EPS, None, ALU.add).then_inc(lnvar_ready, 1)
                if h == 7:
                    dve.wait_ge(lnrstd_ready, 1)
                    dve.tensor_tensor(conv, lnc, lnrstd.unsqueeze(1).broadcast_to([P, NC4, T]), ALU.mult).then_inc(ln_scaled, 1)
            dve.wait_ge(exp_ready, 2 * H)
            link(dve.reciprocal(S(8), S(6)))
            dve.wait_ge(pv_ready, H)
            for t in range(TT):
                dve.tensor_tensor(att[:, t, :].rearrange("p (h d) -> p h d", h=H),
                                  ps[1 + t][:, :].rearrange("p (h d) -> p h d", h=H), bc(S3(8)[:, t, :], DH),
                                  ALU.mult).then_inc(att_ready, 1)
            dve.wait_ge(attT_ready, 2)
            dve.tensor_copy(catT[:, 2:4, :].rearrange("p a b -> p (a b)"), ps[5][:, :]).then_inc(attT_copied, 1)
            add_residual(0, (0, 1, 2, 3))
            norm_scale(1)
            norm_gains(1)
            for c in range(NF):
                dve.wait_ge(dsg_ready, c + 1)
                dve.tensor_tensor(hid[:, c, :], ps[c % 4][:, T:2 * T], dsg[:, c % 4, :], ALU.mult).then_inc(hid_ready, 1)
            add_residual(1, (4, 5, 6, 7))
            norm_scale(2)
            norm_gains(2)
            dve.wait_ge(gate_pre, 2)
            gates = ps[0][:, 0:2 * TT * H].rearrange("p (t g) -> p t g", t=TT)
            link(dve.tensor_tensor(S3(9), gates[:, :, 0:H], bif1[:, :, 0:H], ALU.add))
            link(dve.tensor_tensor(S3(10), gates[:, :, H:2 * H], bif1[:, :, H:2 * H], ALU.add))
            neg_abs(1, 10, 11)
            for c in range(KD // 2):
                dve.wait_ge(u1_copied, c + 1)
            for j in range(TAPS1):
                for c in range(KD):
                    w = prm[:, C_CW1 + j * KD + c:C_CW1 + j * KD + c + 1]
                    if j == 0:
                        dve.tensor_scalar(uT[:, c, :], upad1[:, c, 0:T], w, None, ALU.mult).then_inc(conv1_tap, 1)
                    else:
                        dve.wait_ge(conv1_tap, KD * (j - 1) + c + 1)
                        dve.scalar_tensor_tensor(out=uT[:, c, :], in0=upad1[:, c, j:j + T], scalar=w,
                                                 in1=uT[:, c, :], op0=ALU.mult, op1=ALU.add).then_inc(conv1_tap, 1)
            log_f(1, 10, 13, 14)
            dve.wait_ge(cum_ready, 2)
            link(dve.tensor_copy(S(15), ps[0][:, 64:64 + TT * H]))
            dve.tensor_tensor(S(16), S(9), S(15), ALU.subtract).then_inc(cum_copied, 1)
            dve.wait_ge(cumT_ready, 2)
            link(dve.tensor_copy(aT[:, :], ps[0][0:H, 128:128 + T]))
            dve.tensor_tensor_scan(GT[:, :], aT[:, :], aT[:, :], 0.0, ALU.max, ALU.max).then_inc(gT_ready, 1)
            dve.wait_ge(gt_back, 1)
            dve.tensor_tensor(S(20), S(15), ps[0][:, 400:400 + TT * H], ALU.add).then_inc(m_ready, 1)
            for h in range(H):
                dve.wait_ge(dec_ready, h + 1)
                if h >= 2:
                    dve.wait_ge(num_ready, h - 1)
                dve.tensor_tensor(wts[:, h % 2, :], ps[1 + h % 2][:, 0:3 * P], dec[:, h % 2, :], ALU.mult).then_inc(w_ready, 1)
            dve.wait_ge(num_copied, H)
            dve.wait_ge(enm_ready, 1)
            nq = num[:, :, :, P:P + 1].rearrange("p t h o -> p t (h o)")
            link(dve.tensor_copy(S3(22), nq))
            link(dve.scalar_tensor_tensor(out=S(23), in0=S(22), scalar=-1.0, in1=S(22), op0=ALU.mult, op1=ALU.max))
            link(dve.tensor_tensor(S(24), S(23), S(21), ALU.max))
            link(dve.reciprocal(S(25), S(24)))
            dve.wait_ge(og_ready, 4)
            for t in range(TT):
                v = hc[:, t, :].rearrange("p (h d) -> p h d", h=H)
                link(dve.tensor_tensor(v, num[:, t, :, 0:P], bc(S3(25)[:, t, :], P), ALU.mult))
            dve.tensor_tensor(hc, hc, og, ALU.mult).then_inc(hc_ready, 1)
            dve.wait_ge(hsq_ready, 2)
            link(dve.tensor_reduce(S(31), hsq.rearrange("p t (h d) -> p (t h) d", h=H), AX_X, ALU.add))
            dve.tensor_scalar(S(32), S(31), 1.0 / P, EPS, ALU.mult, ALU.add).then_inc(hvar_ready, 1)
            dve.wait_ge(hrstd_ready, 1)
            dve.wait_ge(hc_ready, 1)
            for t in range(TT):
                v = hc[:, t, :].rearrange("p (h d) -> p h d", h=H)
                dve.tensor_tensor(v, v, bc(S3(33)[:, t, :], P), ALU.mult).then_inc(hn_ready, 1)
            for b in (1, 3):
                dve.wait_ge(hcT_ready, b + 1)
                for k in (2 * b, 2 * b + 1):
                    dve.tensor_scalar(catT1[:, k, :], ps[4 + b][:, (k % 2) * T:(k % 2 + 1) * T],
                                      prm[:, C_HN + k:C_HN + k + 1], None, ALU.mult).then_inc(hcT_dve, 1)
            add_residual(2, (0, 1, 2, 3))
            norm_scale(3)
            norm_gains(3)
            for k in range(KD):
                dve.tensor_scalar(gain_bc[:, k, :], slot_no[:, :], 0.0, prm[:, G_NORM[3] + k:G_NORM[3] + k + 1],
                                  ALU.mult, ALU.add).then_inc(gain_ready, 1)
            dve.wait_ge(gain_ready, KD)
            dve.tensor_copy(cur[:, 0, :], ss[:, 2, :]).then_inc(y_added, 4)
            dve.wait_ge(logits_ready, 1)
            L, p1, oh1, l2, p2, oh2, t1, t2 = 0, 1, 2, 3, 4, 5, 6, 7
            link(dve.tensor_copy(S(L), ps[0][:, 0:TT * NE]))

            def first_max(l, p, oh, top):
                link(dve.tensor_reduce(top, S3(l), AX_X, ALU.max))
                link(dve.tensor_tensor(S3(p), S3(l), bc(top, NE), ALU.is_equal))
                link(dve.tensor_tensor(S3(p), S3(p), pick_order[:, :, :], ALU.mult))
                link(dve.tensor_reduce(ss[:, 7, :], S3(p), AX_X, ALU.max))
                link(dve.tensor_tensor(S3(oh), S3(p), bc(ss[:, 7, :], NE), ALU.is_equal))

            first_max(L, p1, oh1, ss[:, 5, :])
            link(dve.scalar_tensor_tensor(out=S(l2), in0=S(oh1), scalar=NEG, in1=S(L), op0=ALU.mult, op1=ALU.add))
            first_max(l2, p2, oh2, ss[:, 6, :])
            dve.tensor_tensor(S(8), S(oh1), S(oh2), ALU.add).then_inc(mask_ready, 1)
            dve.tensor_tensor(ss[:, 3, :], ss[:, 6, :], ss[:, 5, :], ALU.subtract).then_inc(diff_ready, 1)
            dve.wait_ge(e2_ready, 1)
            link(dve.tensor_scalar(ss[:, 5, :], ss[:, 4, :], 1.0, None, ALU.add))
            link(dve.reciprocal(ss[:, 6, :], ss[:, 5, :]))
            link(dve.tensor_tensor(ss[:, 7, :], ss[:, 4, :], ss[:, 6, :], ALU.mult))
            link(dve.tensor_tensor(S3(t1), S3(oh1), bc(ss[:, 6, :], NE), ALU.mult))
            link(dve.tensor_tensor(S3(t2), S3(oh2), bc(ss[:, 7, :], NE), ALU.mult))
            link(dve.tensor_tensor(S(9), S(t1), S(t2), ALU.add))
            dve.wait_ge(pos_ready, 1)
            link(dve.tensor_tensor(S(10), ps[0][:, 64:64 + TT * NE], S(8), ALU.mult))
            link(dve.tensor_scalar(S(11), S(10), -1.0, None, ALU.add))
            link(dve.tensor_reduce(ss[:, 3, 0:1], ps[0][:, 96:96 + NE], AX_X, ALU.max))
            dve.tensor_copy(flag[:, 0:1], ss[:, 3, 0:1]).then_inc(flag_ready, 1)

            def expert(it, e, r=None):
                if r is not None:
                    dve.wait_ge(round_ready, r)
                dve.tensor_copy(cur[:, 0, :].unsqueeze(2), S3(11)[:, :, bass.ds(e, 1)]).then_inc(cur_ready, 1)
                dve.tensor_copy(cur[:, 1, :].unsqueeze(2), S3(9)[:, :, bass.ds(e, 1)]).then_inc(cur_ready, 1)
                dve.wait_ge(cur_ready, it * 2 + 2)
                for t in range(TT):
                    dve.tensor_scalar(disp[:, t, :], slot_no[:, :], cur[:, 0, t:t + 1], None,
                                      ALU.is_equal).then_inc(route_ready, 1)
                    dve.tensor_scalar(comb[:, t, :], slot_no[:, :], cur[:, 0, t:t + 1], cur[:, 1, t:t + 1],
                                      ALU.is_equal, ALU.mult).then_inc(route_ready, 1)
                for b in range(2):
                    dve.wait_ge(disp_done, it * 2 + (b + 1))
                    dve.tensor_tensor(xT[:, 4 * b:4 * b + 4, :], ps[6 + b][:, 0:4 * CAP].rearrange("p (k s) -> p k s", k=4),
                                      gain_bc[:, 4 * b:4 * b + 4, :], ALU.mult).then_inc(xTe_ready, 1)
                for c in range(CH):
                    dve.wait_ge(sil_ready, it * CH + (c + 1))
                    dve.tensor_tensor(hidE[:, c % 4, :], ps[c % 2][:, CAP:2 * CAP], sil[:, c % 4, :],
                                      ALU.mult).then_inc(hidE_ready, 1)
                dve.wait_ge(yT_done, it + 1)
                dve.tensor_copy(yT[:, 0:4, :].rearrange("p a b -> p (a b)"), ps[2][:, 0:4 * CAP]).then_inc(yT_dve, 1)
                dve.wait_ge(yt_done, it * 2 + 1)
                dve.tensor_copy(ye[0:CAP, 0:512], ps[4][0:CAP, :]).then_inc(ye_dve, 1)
                for n in range(4):
                    dve.wait_ge(y_done, it * 4 + (n + 1))
                    t, half = n // 2, n % 2
                    v = xres[:, t, half * 512:(half + 1) * 512]
                    dve.tensor_tensor(v, v, ps[(6, 7, 2, 3)[n]][:, :], ALU.add).then_inc(y_added, 1)

            dve.wait_ge(dve_chain, links[0])
            with dve.Fori(0, NE) as e:
                expert(e, e)
            dve.wait_ge(flag_ready, 1)
            most = dve.value_load(flag[0:1, 0:1], min_val=0, max_val=T)
            with dve.If(most > CAP):
                with dve.Fori(1, ROUNDS) as r:
                    dve.wait_ge(cur_ready, r * (2 * NE))
                    dve.tensor_scalar(S(11), S(11), -float(CAP), None, ALU.add).then_inc(round_ready, 1)
                    with dve.Fori(0, NE) as e:
                        expert(r * NE + e, e, r)
                dve.wait_ge(y_added, ROUNDS * NE * 4 + 4)
            dve.wait_ge(y_added, NE * 4 + 4)
            dve.tensor_copy(flag[:, 1:2], flag[:, 0:1]).then_inc(moe_done, 1)
            norm_scale(4)
            dve.wait_ge(gfin_in, 16)
            for t in range(TT):
                dve.scalar_tensor_tensor(out=xn[:, t, :], in0=xres[:, t, :], scalar=ss[:, 2, t:t + 1], in1=gfin,
                                         op0=ALU.mult, op1=ALU.mult).then_inc(fin_ready, 1)

        @block.tensor
        def _(pe):
            def arrived(t):
                pe.wait_ge(landed[slot(t)], landed_at[t])

            def turn(src, ready, i, done, frees=False):
                for b in range(4):
                    for k in (2 * b, 2 * b + 1):
                        for t in range(TT):
                            if b == 0 and k == 0:
                                pe.wait_ge(ready, 2 * i + t + 1)
                            last = pe.transpose(ps[4 + b][:, (k % 2) * T + t * P:(k % 2) * T + (t + 1) * P],
                                                src[:, t, k * P:(k + 1) * P], ident[:, :])
                            if frees and k == 0 and t == 0:
                                last.then_inc(tiles_used, 1)
                    last.then_inc(done, 1)

            def hT_wait(i):
                pe.wait_ge(hT_act, 4 * i + 4)
                pe.wait_ge(hT_dve, 4 * i + 4)

            def feature_major(o, w, c, frees=False):
                for k in range(KD):
                    last = pe.matmul(o, w[:, k, c * P:(c + 1) * P], hT[:, k, :], start=(k == 0), stop=(k == KD - 1))
                    if k == 0 and frees:
                        last.then_inc(tiles_used, 1)
                return last

            def token_major(o, w, t, src=hT, frees=False):
                for k in range(KD):
                    last = pe.matmul(o, src[:, k, t * P:(t + 1) * P], w[:, k, :], start=(k == 0), stop=(k == KD - 1))
                    if k == 0 and frees:
                        last.then_inc(tiles_used, 1)
                return last

            def cumulate(o, src):
                pe.matmul(o[:, 0:H], upper[:, :], src[:, 0, :], start=True, stop=True)
                pe.matmul(o[:, H:2 * H], ones[:, :], src[:, 0, :], start=True, stop=False)
                return pe.matmul(o[:, H:2 * H], upper[:, :], src[:, 1, :], start=False, stop=True)

            def out_proj(stage, t0, src, banks):
                for n in range(4):
                    half, t = n // 2, n % 2
                    if t == 0:
                        arrived(t0 + half)
                    w = tile(t0 + half, KD, TILE)
                    token_major(ps[banks[n]][:, :], w, t, src, frees=(n == 2)).then_inc(proj_ready, 1)

            pe.wait_ge(ident_ready, 1)
            pe.wait_ge(params_in, 16 * 11)
            pe.transpose(ps[7][:, 0:N_ROWS1], rows1[0:N_ROWS1, :], ident[0:N_ROWS1, 0:N_ROWS1])
            pe.transpose(ps[7][:, P:P + N_ROWS2], rows2[0:N_ROWS2, :], ident[0:N_ROWS2, 0:N_ROWS2]).then_inc(prm_T, 1)
            pe.wait_ge(prm_ready, 2)
            turn(xn, xn_ready, 0, xT_ready)
            pe.wait_ge(small_in, 16 * 9)
            hT_wait(0)
            token_major(ps[0][:, 0:H], wf, 0)
            token_major(ps[0][:, H:2 * H], wf, 1).then_inc(gate_pre, 1)
            arrived(T_GLU)
            arrived(T_GLU + 1)
            for c in range(NC4):
                feature_major(ps[1 + c][:, 0:T], tile(T_GLU, KD, TILE), c)
                feature_major(ps[1 + c][:, T:2 * T], tile(T_GLU + 1, KD, TILE), c,
                              frees=(c == NC4 - 1)).then_inc(glu_ready, 1)
                if c == 0:
                    pe.wait_ge(const_ready, 4)
                    pe.wait_ge(pool_chain, 11)
                    pe.wait_ge(logf_ready, 1)
                    cumulate(ps[0][:, 16:16 + 2 * H], S3(4)).then_inc(cum_ready, 1)
                if c == 2:
                    pe.wait_ge(cum_copied, 1)
                    pe.transpose(ps[0][0:H, 64:64 + P], S3(7)[:, 0, :], ident[:, :])
                    pe.transpose(ps[0][0:H, 64 + P:64 + T], S3(7)[:, 1, :], ident[:, :]).then_inc(cumT_ready, 1)
            arrived(T_Q)
            arrived(T_K)
            for c in range(NC4):
                b = (5, 6, 7, 0)[c]
                if b == 0:
                    pe.wait_ge(cT_ready, 1)
                feature_major(ps[b][:, 0:T], tile(T_Q, KD, TILE), c, frees=(c == 0))
                feature_major(ps[b][:, T:2 * T], tile(T_K, KD, TILE), c, frees=(c == NC4 - 1)).then_inc(qk_ready, 1)
            arrived(T_V)
            for t in range(TT):
                pe.wait_ge(u_ready, t + 1)
                token_major(ps[1 + t][:, :], tile(T_V, KD, TILE), t, frees=(t == 0)).then_inc(v_ready, 1)
            pe.wait_ge(conv_tap, NC4 * TAPS)
            pe.wait_ge(u_ready, NC4)
            for c in range(NC4):
                last = pe.matmul(ps[3][:, 0:T], ch_mean[:, :], conv[:, c, :], start=(c == 0), stop=(c == NC4 - 1))
                if c == 0:
                    last.then_inc(tiles_used, 1)
            last.then_inc(ln_mean, 1)

            def scores(h):
                lo, c, b = DH * (h % 2), h // 2, (0, 5)[h % 2]
                if h >= 2:
                    pe.wait_ge(exp_ready, 2 * (h - 1))
                for t, o in ((0, ps[b][:, 0:P]), (1, ps[b][:, P:3 * P])):
                    n = (t + 1) * P
                    pe.matmul(o, qT0[lo:lo + DH, c, t * P:(t + 1) * P], kT0[lo:lo + DH, c, 0:n], start=True, stop=False)
                    pe.matmul(o, neg_sel[:, h, :], cT[:, 0:n], start=False, stop=False)
                    last = pe.matmul(o[:, n - P:n], ident[:, :], mask_qk[:, :], start=False, stop=True)
                last.then_inc(scores_ready, 1)

            def turn_probs(h):
                pe.wait_ge(exp_ready, 2 * h + 2)
                if h >= 2:
                    pe.wait_ge(pT_copied, h - 1)
                for j in range(3):
                    last = pe.transpose(ps[6 + h % 2][:, j * P:(j + 1) * P], probs[:, h % 2, j * P:(j + 1) * P], ident[:, :])
                last.then_inc(pT_ready, 1)

            def values(h):
                pe.wait_ge(pT_copied, h + 1)
                cols = slice(h * DH, (h + 1) * DH)
                pe.matmul(ps[1][:, cols], probsT[:, h % 2, 0:P], v0[:, 0, cols], start=True, stop=True)
                pe.matmul(ps[2][:, cols], probsT[:, h % 2, P:2 * P], v0[:, 0, cols], start=True, stop=False)
                pe.matmul(ps[2][:, cols], probsT[:, h % 2, 2 * P:3 * P], v0[:, 1, cols], start=False,
                          stop=True).then_inc(pv_ready, 1)

            pe.wait_ge(qk_copied, 2 * NC4)
            pe.wait_ge(v_copied, TT)
            for i in range(H + 2):
                if i < H:
                    scores(i)
                if i == 4:
                    pe.wait_ge(lnsq_ready, 1)
                    for c in range(NC4):
                        last = pe.matmul(ps[4][:, 0:T], ch_mean[:, :], lnsq[:, c, :], start=(c == 0), stop=(c == NC4 - 1))
                    last.then_inc(ln_var, 1)
                if 1 <= i <= H:
                    turn_probs(i - 1)
                if i >= 2:
                    values(i - 2)
            pe.wait_ge(att_ready, TT)
            for j in range(FW // P):
                for t in range(TT):
                    last = pe.transpose(ps[(0, 5)[j // 2]][:, (j % 2) * T + t * P:(j % 2) * T + (t + 1) * P],
                                        att[:, t, j * P:(j + 1) * P], ident[:, :])
                if j % 2:
                    last.then_inc(attT_ready, 1)
            pe.wait_ge(attT_copied, 2)
            pe.wait_ge(convT_ready, NC4)
            out_proj(0, T_OUT0, catT, (0, 1, 2, 3))
            turn(xn, xn_ready, 1, xT_ready, frees=True)
            hT_wait(1)
            for c in range(NF):
                t = T_PAIR + c // 2
                if c % 2 == 0:
                    arrived(t)
                if c >= 4:
                    pe.wait_ge(hid_ready, c - 3)
                w = tile(t, 2 * KD, 256)
                feature_major(ps[c % 4][:, 0:T], w[:, 0:KD, :], c % 2, frees=(c % 2 == 0 and c > 0))
                feature_major(ps[c % 4][:, T:2 * T], w[:, KD:2 * KD, :], c % 2).then_inc(gu_ready, 1)
            for f in range(NF):
                if f % 4 == 0:
                    arrived(T_DOWN + f // 4)
                pe.wait_ge(hid_ready, f + 1)
                w = tile(T_DOWN + f // 4, 4, D)
                for n in range(4):
                    half, t = n // 2, n % 2
                    last = pe.matmul(ps[4 + n][:, :], hid[:, f, t * P:(t + 1) * P], w[:, f % 4, half * 512:(half + 1) * 512],
                                     start=(f == 0), stop=(f == NF - 1))
                    if f % 4 == 0 and n == 0:
                        last.then_inc(tiles_used, 1)
                    if f == NF - 1:
                        last.then_inc(proj_ready, 1)
            turn(xn, xn_ready, 2, xT_ready, frees=True)
            hT_wait(2)
            token_major(ps[0][:, 0:2 * H], wif, 0)
            token_major(ps[0][:, 2 * H:4 * H], wif, 1).then_inc(gate_pre, 1)
            for c in range(KD):
                if c % 4 == 0:
                    arrived(T_U + c // 4)
                last = feature_major(ps[1 + c // 2][:, (c % 2) * T:(c % 2 + 1) * T], tile(T_U + c // 4, KD, TILE), c % 4,
                                     frees=(c == 4))
                if c % 2:
                    last.then_inc(u1_ready, 1)
            for n in range(4):
                half, t = n // 2, n % 2
                if t == 0:
                    arrived(T_V1 + half)
                if n == 3:
                    pe.wait_ge(u1_copied, 1)
                token_major(ps[(5, 6, 7, 1)[n]][:, :], tile(T_V1 + half, KD, TILE), t, frees=(t == 0)).then_inc(v1_ready, 1)
            pe.wait_ge(logf_ready, 2)
            cumulate(ps[0][:, 64:64 + 2 * H], S3(14)).then_inc(cum_ready, 1)
            for n in range(4):
                half, t = n // 2, n % 2
                if t == 0:
                    arrived(T_O1 + half)
                if n == 0:
                    pe.wait_ge(u1_copied, 4)
                if n == 3:
                    pe.wait_ge(v1_copied, 1)
                token_major(ps[2 + n][:, :], tile(T_O1 + half, KD, TILE), t, frees=(t == 0)).then_inc(o1_ready, 1)
                if n == 1:
                    pe.wait_ge(cum_copied, 2)
                    for tt in range(TT):
                        last = pe.transpose(ps[0][0:H, P + tt * P:P + (tt + 1) * P], S3(16)[:, tt, :], ident[:, :])
                    last.then_inc(cumT_ready, 1)
            pe.wait_ge(gT_ready, 1)
            for t in range(TT):
                last = pe.transpose(ps[0][:, 400 + t * H:400 + (t + 1) * H], GT[:, t * P:(t + 1) * P], ident[0:H, 0:H])
            last.then_inc(gt_back, 1)
            arrived(T_QK1)
            w = tile(T_QK1, 2 * H, P)
            pe.wait_ge(v1_copied, 4)
            for h in range(H):
                b = (6, 7, 1, 2)[h % 4]
                pe.wait_ge(uT_ready, h + 1)
                if h == 3:
                    pe.wait_ge(og_ready, 1)
                if h >= 4:
                    pe.wait_ge(qk1_copied, 2 * (h - 3))
                last = pe.matmul(ps[b][:, 0:T], w[:, h, :], uT[:, h, :], start=True, stop=True)
                if h == 0:
                    last.then_inc(tiles_used, 1)
                pe.matmul(ps[b][:, T:2 * T], w[:, H + h, :], uT[:, h, :], start=True, stop=True).then_inc(qk1_ready, 1)

            def decay_and_scores(h):
                s, e = ps[1 + h % 2], ps[3 + h % 2]
                if h >= 2:
                    pe.wait_ge(w_ready, h - 1)
                last = pe.matmul(s[:, 0:T], kT1[:, h, 0:P], qT1[:, h, :], start=True, stop=True)
                if h == 0:
                    last.then_inc(tiles_used, 1)
                pe.matmul(s[:, T:T + P], kT1[:, h, P:T], qT1[:, h, P:T], start=True, stop=True)
                pe.matmul(e[:, 0:T], neg_sel[:, h, :], GT[:, :], start=True, stop=False)
                pe.matmul(e[:, 0:P], ident[:, :], mask_kq[:, :], start=False, stop=True)
                pe.matmul(e[:, T:T + P], neg_sel[:, h, :], GT[:, P:T], start=True, stop=False)
                pe.matmul(e[:, T:T + P], ident[:, :], mask_kq[:, :], start=False, stop=True).then_inc(ex_ready, 1)

            def numerators(h):
                o = ps[5 + h % 2]
                pe.wait_ge(w_ready, h + 1)
                if h >= 2:
                    pe.wait_ge(num_copied, h - 1)
                pe.matmul(o[:, 0:P + 1], wts[:, h % 2, 0:P], v_aug[:, 0, h, :], start=True, stop=True)
                pe.matmul(o[:, T:T + P + 1], wts[:, h % 2, P:T], v_aug[:, 0, h, :], start=True, stop=False)
                pe.matmul(o[:, T:T + P + 1], wts[:, h % 2, T:T + P], v_aug[:, 1, h, :], start=False,
                          stop=True).then_inc(num_ready, 1)

            pe.wait_ge(qk1_copied, 2 * H)
            pe.wait_ge(og_ready, 4)
            for i in range(H + 1):
                if i < H:
                    decay_and_scores(i)
                if i >= 1:
                    numerators(i - 1)
            turn(hc, hn_ready, 0, hcT_ready)
            pe.wait_ge(hcT_act, 4)
            pe.wait_ge(hcT_dve, 4)
            out_proj(2, T_OUT1, catT1, (0, 1, 2, 3))
            turn(xn, xn_ready, 3, xT_ready, frees=True)
            hT_wait(3)
            token_major(ps[0][:, 0:NE], wr, 0)
            token_major(ps[0][:, NE:2 * NE], wr, 1).then_inc(logits_ready, 1)
            pe.wait_ge(mask_ready, 1)
            cumulate(ps[0][:, 64:64 + 2 * NE], S3(8))
            pe.matmul(ps[0][:, 96:96 + NE], ones[:, :], S3(8)[:, 0, :], start=True, stop=False)
            pe.matmul(ps[0][:, 96:96 + NE], ones[:, :], S3(8)[:, 1, :], start=False, stop=True).then_inc(pos_ready, 1)

            def expert(it):
                pe.wait_ge(y_added, it * 4 + 4)
                pe.wait_ge(route_ready, it * 4 + 4)
                for k in range(KD):
                    o = ps[6 + k // 4][:, (k % 4) * CAP:(k % 4 + 1) * CAP]
                    for t in range(TT):
                        last = pe.matmul(o, xn[:, t, k * P:(k + 1) * P], disp[:, t, :], start=(t == 0), stop=(t == TT - 1))
                    if k % 4 == 3:
                        last.then_inc(disp_done, 1)
                for t in range(TT):
                    last = pe.transpose(ps[5][0:CAP, t * P:(t + 1) * P], comb[:, t, :], ident[:, :])
                last.then_inc(combT_done, 1)
                pe.wait_ge(xTe_ready, it * 2 + 2)

                def down(c):
                    s, count = expert_tile(3 * (c // CPG) + 2)
                    w = ring[:, s, :].rearrange("p (k n) -> p k n", k=CPG)
                    if c % CPG == 0:
                        pe.wait_ge(landed[s], it * PER_PASS + count)
                    pe.wait_ge(hidE_ready, it * CH + (c + 1))
                    for k in range(KD):
                        last = pe.matmul(ps[2 + k // 4][:, (k % 4) * CAP:(k % 4 + 1) * CAP], w[:, c % CPG, k * P:(k + 1) * P],
                                         hidE[:, c % 4, :], start=(c == 0 and k % 4 == 0), stop=(c == CH - 1),
                                         skip_group_check=True)
                        if c % CPG == CPG - 2 and k == 0:
                            last.then_inc(tiles_used, 1)
                    return last

                for c in range(CH):
                    g, j = c // CPG, c % CPG
                    for kind in range(2):
                        s, count = expert_tile(3 * g + kind)
                        if j == 0:
                            pe.wait_ge(landed[s], it * PER_PASS + count)
                        if kind == 0 and c >= 2:
                            pe.wait_ge(hidE_ready, it * CH + (c - 1))
                        w = ring[:, s, :].rearrange("p (k n) -> p k n", k=KD)
                        for k in range(KD):
                            last = pe.matmul(ps[c % 2][:, kind * CAP:(kind + 1) * CAP], w[:, k, j * P:(j + 1) * P],
                                             xT[:, k, :], start=(k == 0), stop=(k == KD - 1))
                            if k == 0 and ((kind == 1 and j == CPG - 1) or (kind == 0 and j == 1 and g > 0)):
                                last.then_inc(tiles_used, 1)
                    last.then_inc(egu_ready, 1)
                    if c >= 1:
                        down(c - 1)
                down(CH - 1).then_inc(yT_done, 1)
                for k in range(KD):
                    if k == 0:
                        pe.wait_ge(yT_dve, it + 1)
                    if k == 4:
                        pe.wait_ge(yT_act, it + 1)
                    last = pe.transpose(ps[4 + k // 4][0:CAP, (k % 4) * P:(k % 4 + 1) * P], yT[:, k, :], ident[:, :])
                    if k == 0:
                        last.then_inc(tiles_used, 1)
                    if k % 4 == 3:
                        last.then_inc(yt_done, 1)
                pe.wait_ge(combT_ready, it + 1)
                for n in range(4):
                    t, half = n // 2, n % 2
                    if n == 0:
                        pe.wait_ge(ye_dve, it + 1)
                    if n == 1:
                        pe.wait_ge(ye_act, it + 1)
                    pe.matmul(ps[(6, 7, 2, 3)[n]][:, :], combT[0:CAP, t * P:(t + 1) * P],
                              ye[0:CAP, half * 512:(half + 1) * 512], start=True, stop=True).then_inc(y_done, 1)

            with pe.Fori(0, NE) as e:
                expert(e)
            pe.wait_ge(flag_ready, 1)
            most = pe.value_load(flag[0:1, 0:1], min_val=0, max_val=T)
            with pe.If(most > CAP):
                with pe.Fori(1, ROUNDS) as r:
                    with pe.Fori(0, NE) as e:
                        expert(r * NE + e)


_INS = ['x', 'l0_norm1_g', 'l0_w_in', 'l0_b_f', 'l0_dw_w', 'l0_dw_b', 'l0_cln_g', 'l0_cln_b', 'l0_w_out',
        'l0_norm2_g', 'l0_w_gate', 'l0_w_up', 'l0_w_down', 'l1_norm1_g', 'l1_w_in', 'l1_b_i', 'l1_b_f',
        'l1_conv_w', 'l1_conv_b', 'l1_wq_head', 'l1_wk_head', 'l1_hnorm_g', 'l1_w_out', 'l1_norm2_g',
        'l1_router', 'l1_e_gate', 'l1_e_up', 'l1_e_down', 'final_norm_g']


def kernel(**inputs):
    import numpy as _np
    import concourse.bacc as _bacc
    from concourse import mybir as _mybir
    from concourse.bass_utils import run_bass_kernel_spmd as _run

    nc = _bacc.Bacc("TRN2", target_bir_lowering=False, num_devices=1)
    arrays, args = {}, []
    for name in _INS:
        a = _np.ascontiguousarray(inputs[name])
        arrays[f"in_{name}_dram"] = a
        args.append(nc.dram_tensor(f"in_{name}_dram", a.shape, _mybir.dt.from_np(a.dtype), kind="ExternalInput").ap())
    out = nc.dram_tensor("out_dram", inputs["x"].shape, _mybir.dt.float32, kind="ExternalOutput").ap()
    bass_hybrid_trunk(nc, *args, out)
    r = _run(nc, [arrays], core_ids=[0])
    return r.results[0]["out_dram"]
```

```python
from contextlib import ExitStack

import concourse.bass as bass
from concourse import mybir

ALU = mybir.AluOpType
ACT = mybir.ActivationFunctionType
AX_X = mybir.AxisListType.X
F32 = mybir.dt.float32
F32R = mybir.dt.float32r
I32 = mybir.dt.int32

P = 128
EPS = 1e-6
NEG = -1e30
CAP = 128
RING = 6
SPLITS = 3
TILE = 512
ARENA = 19200
COLS = 4096


def bass_hybrid_trunk(nc, x, l0_norm1_g, l0_w_in, l0_b_f, l0_dw_w, l0_dw_b, l0_cln_g, l0_cln_b, l0_w_out,
                      l0_norm2_g, l0_w_gate, l0_w_up, l0_w_down, l1_norm1_g, l1_w_in, l1_b_i, l1_b_f,
                      l1_conv_w, l1_conv_b, l1_wq_head, l1_wk_head, l1_hnorm_g, l1_w_out, l1_norm2_g,
                      l1_router, l1_e_gate, l1_e_up, l1_e_down, final_norm_g, out):
    _, T, D = x.shape
    TT = T // P
    KD = D // P
    H = l0_b_f.shape[0]
    DH = 64
    FW = H * DH
    CC = l0_dw_w.shape[1]
    NC4 = CC // P
    TAPS = l0_dw_w.shape[0]
    TAPS1 = l1_conv_w.shape[0]
    DFF = l0_w_gate.shape[1]
    NF = DFF // P
    NE, _, DFE = l1_e_gate.shape
    GROUPS = DFE // TILE
    CPG = TILE // P
    CH = GROUPS * CPG
    ROUNDS = -(-T // CAP)
    assert TT == 2 and KD == 8 and H == 8 and NE == 8 and 6 * GROUPS % RING == 0 and 6 * GROUPS % SPLITS == 0

    def wide(w, c0, n):
        return w[:, c0:c0 + n].rearrange("(k p) n -> p k n", p=P)

    front = []
    for c0 in (3 * FW + H, 3 * FW + H + CC, 0, FW, 2 * FW):
        front.append([(wide(l0_w_in, c0, TILE), 0, TILE)])
    for half in range(2):
        front.append([(wide(l0_w_out, half * TILE, TILE), 0, TILE)])
    PAIRS = DFF // 256
    for p in range(PAIRS):
        front.append([(wide(l0_w_gate, p * 256, 256), 0, 256), (wide(l0_w_up, p * 256, 256), KD * 256, 256)])
    DOWNS = -(-NF // 4)
    for t in range(DOWNS):
        n = min(4, NF - 4 * t)
        front.append([(l0_w_down[t * 512:t * 512 + n * P, :].rearrange("(k p) n -> p k n", p=P), 0, D)])
    for c0 in range(0, 3 * D, TILE):
        front.append([(wide(l1_w_in, c0, TILE), 0, TILE)])
    front.append([(l1_wq_head.rearrange("h d e -> d h e"), 0, P), (l1_wk_head.rearrange("h d e -> d h e"), H * P, P)])
    for half in range(2):
        front.append([(wide(l1_w_out, half * TILE, TILE), 0, TILE)])
    T_GLU, T_Q, T_K, T_V, T_OUT0, T_PAIR = 0, 2, 3, 4, 5, 7
    T_DOWN = T_PAIR + PAIRS
    T_U = T_DOWN + DOWNS
    T_V1, T_O1, T_QK1, T_OUT1 = T_U + 2, T_U + 4, T_U + 6, T_U + 7
    FRONT = T_OUT1 + 2
    assert FRONT == len(front)

    with ExitStack() as ctx:
        def sb(name, shape, dt=F32):
            return ctx.enter_context(nc.sbuf_tensor(name, shape, dt))

        def sem(name):
            return ctx.enter_context(nc.semaphore(name))

        ring = sb("ring", [P, RING, COLS])
        xres = sb("xres", [P, TT, D])
        xn = sb("xn", [P, TT, D])
        hT = sb("hT", [P, KD, T])
        arena_at = nc.sbuf_base
        arena = sb("arena", [P, ARENA])

        class Phase:
            def __init__(self):
                self.at = 0

            def __call__(self, name, shape, dt=F32):
                words = 1
                for n in shape[1:]:
                    words *= n
                t = nc.alloc_sbuf_tensor_at(name, shape, dt, offset=arena_at + 4 * self.at)
                self.at += words
                assert self.at <= ARENA, name
                return t

        layers, moe = Phase(), Phase()
        work = layers("work", [P, 13864])
        ident = sb("ident", [P, P])
        upper = sb("upper", [P, P])
        ones = sb("ones", [P, P])
        ch_mean = layers("ch_mean", [P, P])
        mask_qk = layers("mask_qk", [P, P])
        mask_kq = layers("mask_kq", [P, P])
        neg_sel = layers("neg_sel", [H, H, P])
        slot_no = sb("slot_no", [P, CAP])
        pick_order = sb("pick_order", [P, TT, NE])
        minus_half = sb("minus_half", [P, TT * H])
        rows1 = layers("rows1", [P, P])
        rows2 = layers("rows2", [P, P])
        prm = sb("prm", [P, P])
        dww = layers("dww", [P, P])
        wf = layers("wf", [P, KD, H])
        wif = layers("wif", [P, KD, 2 * H])
        wr = sb("wr", [P, KD, NE])
        bf0 = sb("bf0", [P, H])
        bif1 = sb("bif1", [P, 2 * H])
        small = sb("small", [P, 40, TT * H])
        cT = layers("cT", [H, T])
        aT = layers("aT", [H, T])
        GT = layers("GT", [H, T])
        ss = sb("ss", [P, 8, TT])
        cur = sb("cur", [P, 2, TT])
        flag = sb("flag", [P, 2], I32)

        def region(start, *dims):
            n = 1
            for d in dims:
                n *= d
            v = work[:, start:start + n]
            if len(dims) == 2:
                v = v.rearrange("p (a b) -> p a b", a=dims[0])
            if len(dims) == 3:
                v = v.rearrange("p (a b c) -> p a b c", a=dims[0], b=dims[1])
            return v

        qT0 = region(0, NC4, T)
        kT0 = region(1024, NC4, T)
        v0 = region(2048, TT, FW)
        PAD0 = TAPS - 1
        upad = region(3072, NC4, T + PAD0)
        conv = region(4216, NC4, T)
        lnc = region(5240, NC4, T)
        lnsq = region(6264, NC4, T)
        catT = region(7288, KD, T)
        probs = region(9336, 2, 3 * P)
        probsT = region(10104, 2, 3 * P)
        att = region(10872, TT, FW)
        glu_sg = region(11896, NC4, T)
        lnvar = region(12920, T)
        lnrstd = region(13176, T)
        hid = region(0, NF, T)
        dsg = region(NF * T, 4, T)
        PAD1 = TAPS1 - 1
        upad1 = region(0, KD, T + PAD1)
        uT = region(2072, KD, T)
        qT1 = region(4120, KD, T)
        kT1 = region(6168, KD, T)
        v_aug = region(8216, TT, H, P + 1)
        og = region(10280, TT, D)
        dec = region(12328, 2, 3 * P)
        wts = region(13096, 2, 3 * P)
        num = region(0, TT, H, P + 1)
        hc = region(4120, TT, D)
        hsq = region(6168, TT, D)
        catT1 = region(2072, KD, T)
        HALF = COLS // 2
        w_hi = moe("w_hi", [P, SPLITS, HALF], F32R)
        w_lo = moe("w_lo", [P, SPLITS, HALF], F32R)
        x_hi = moe("x_hi", [P, KD, CAP], F32R)
        x_lo = moe("x_lo", [P, KD, CAP], F32R)
        h_hi = moe("h_hi", [P, 2, TILE], F32R)
        h_lo = moe("h_lo", [P, 2, TILE], F32R)
        ye = moe("ye", [P, D])
        disp = moe("disp", [P, TT, CAP])
        comb = moe("comb", [P, TT, CAP])
        combT = moe("combT", [P, T])
        gfin = moe("gfin", [P, D])
        xT = hT[:, 0:4, :].rearrange("p a b -> p (a b)").rearrange("p (k s) -> p k s", k=KD)
        sil = hT[:, 4:6, :].rearrange("p a b -> p (a b)")
        htok = hT[:, 6:8, :].rearrange("p a b -> p (a b)")

        ps = [ctx.enter_context(nc.psum_tensor(f"bank{b}", [P, 512], F32)) for b in range(8)]

        G_NORM = [0, 8, 16, 24]
        C_DWB, C_CLNG, C_CLNB, C_CB1, C_HN, C_CW1 = 32, 36, 40, 44, 52, 60
        N_ROWS1 = C_CW1 + TAPS1 * KD
        N_ROWS2 = TAPS * NC4

        def S(i):
            return small[:, i, :]

        def S3(i):
            return small[:, i, :].rearrange("p (t h) -> p t h", t=TT)

        landed = [sem(f"landed{i}") for i in range(RING)]
        tiles_used = sem("tiles_used")
        x_in = sem("x_in")
        params_in = sem("params_in")
        small_in = sem("small_in")
        gfin_in = sem("gfin_in")
        ident_ready = sem("ident_ready")
        const_ready = sem("const_ready")
        pool_chain = sem("pool_chain")
        dve_chain = sem("dve_chain")
        act_chain = sem("act_chain")
        prm_T = sem("prm_T")
        prm_ready = sem("prm_ready")
        sq_done = sem("sq_done")
        var_ready = sem("var_ready")
        rstd_ready = sem("rstd_ready")
        xn_ready = sem("xn_ready")
        xT_ready = sem("xT_ready")
        hT_act = sem("hT_act")
        hT_dve = sem("hT_dve")
        gate_pre = sem("gate_pre")
        absz_ready = sem("absz_ready")
        ln_ready = sem("ln_ready")
        logf_ready = sem("logf_ready")
        cum_ready = sem("cum_ready")
        cum_copied = sem("cum_copied")
        cumT_ready = sem("cumT_ready")
        cT_ready = sem("cT_ready")
        glu_ready = sem("glu_ready")
        sg_ready = sem("sg_ready")
        u_ready = sem("u_ready")
        conv_tap = sem("conv_tap")
        qk_ready = sem("qk_ready")
        qk_copied = sem("qk_copied")
        v_ready = sem("v_ready")
        v_copied = sem("v_copied")
        ln_mean = sem("ln_mean")
        lnc_ready = sem("lnc_ready")
        lnsq_ready = sem("lnsq_ready")
        ln_var = sem("ln_var")
        lnvar_ready = sem("lnvar_ready")
        lnstd_ready = sem("lnstd_ready")
        ln_scaled = sem("ln_scaled")
        convT_ready = sem("convT_ready")
        scores_ready = sem("scores_ready")
        max_ready = sem("max_ready")
        exp_ready = sem("exp_ready")
        pT_ready = sem("pT_ready")
        pT_copied = sem("pT_copied")
        pv_ready = sem("pv_ready")
        att_ready = sem("att_ready")
        attT_ready = sem("attT_ready")
        attT_copied = sem("attT_copied")
        proj_ready = sem("proj_ready")
        res_added = sem("res_added")
        gu_ready = sem("gu_ready")
        dsg_ready = sem("dsg_ready")
        hid_ready = sem("hid_ready")
        pads_ready = sem("pads_ready")
        u1_ready = sem("u1_ready")
        u1_copied = sem("u1_copied")
        conv1_tap = sem("conv1_tap")
        uT_ready = sem("uT_ready")
        v1_ready = sem("v1_ready")
        v1_copied = sem("v1_copied")
        o1_ready = sem("o1_ready")
        og_ready = sem("og_ready")
        qk1_ready = sem("qk1_ready")
        qk1_copied = sem("qk1_copied")
        gT_ready = sem("gT_ready")
        gt_back = sem("gt_back")
        m_ready = sem("m_ready")
        enm_ready = sem("enm_ready")
        st_ready = sem("st_ready")
        ex_ready = sem("ex_ready")
        dec_ready = sem("dec_ready")
        w_ready = sem("w_ready")
        num_ready = sem("num_ready")
        num_copied = sem("num_copied")
        hc_ready = sem("hc_ready")
        hsq_ready = sem("hsq_ready")
        hvar_ready = sem("hvar_ready")
        hrstd_ready = sem("hrstd_ready")
        hn_ready = sem("hn_ready")
        hcT_ready = sem("hcT_ready")
        hcT_act = sem("hcT_act")
        hcT_dve = sem("hcT_dve")
        logits_ready = sem("logits_ready")
        diff_ready = sem("diff_ready")
        e2_ready = sem("e2_ready")
        mask_ready = sem("mask_ready")
        pos_ready = sem("pos_ready")
        flag_ready = sem("flag_ready")
        cur_ready = sem("cur_ready")
        round_ready = sem("round_ready")
        route_ready = sem("route_ready")
        hi_ready = sem("hi_ready")
        lo_ready = sem("lo_ready")
        split_used = sem("split_used")
        disp_done = sem("disp_done")
        xTe_ready = sem("xTe_ready")
        xhi_ready = sem("xhi_ready")
        xlo_ready = sem("xlo_ready")
        combT_done = sem("combT_done")
        combT_ready = sem("combT_ready")
        g_done = sem("g_done")
        sil_ready = sem("sil_ready")
        u_done = sem("u_done")
        htok_ready = sem("htok_ready")
        hidT_done = sem("hidT_done")
        hhi_ready = sem("hhi_ready")
        hlo_ready = sem("hlo_ready")
        ysum_done = sem("ysum_done")
        ye_dve = sem("ye_dve")
        ye_act = sem("ye_act")
        y_done = sem("y_done")
        y_added = sem("y_added")
        moe_done = sem("moe_done")
        fin_ready = sem("fin_ready")
        stored = sem("stored")

        def slot(t):
            return t % RING

        def tile(t, k, n):
            return ring[:, slot(t), 0:k * n].rearrange("p (k n) -> p k n", k=k)

        slot_count = [0] * RING
        landed_at = []
        for t, parts in enumerate(front):
            slot_count[slot(t)] += 16 * len(parts)
            landed_at.append(slot_count[slot(t)])
        NT = 3 * GROUPS
        PER_PAIR = 2 * NT * 16 // RING

        order = [(0, 0), (1, 0)]
        for g in range(1, GROUPS):
            order += [(0, g), (1, g), (2, g - 1)]
        order.append((2, GROUPS - 1))

        def expert_tile(q, n):
            j = q * NT + n
            s = (FRONT + j) % RING
            return s, slot_count[s] + 16 * (j // RING + 1)

        def half_tile(s, h):
            return ring[:, s, h * HALF:(h + 1) * HALF]

        block = ctx.enter_context(nc.Block())

        @block.sync
        def _(sp):
            for t in range(TT):
                sp.dma_start(xres[:, t, :], x[0, t * P:(t + 1) * P, :]).then_inc(x_in, 16)
            for dst, w in ((wf, wide(l0_w_in, 3 * FW, H)), (wif, wide(l1_w_in, 3 * D, 2 * H)), (wr, wide(l1_router, 0, NE))):
                sp.dma_start(dst[:, :, :], w).then_inc(small_in, 16)
            sp.wait_ge(params_in, 16 * 11)
            sp.wait_ge(small_in, 16 * 6)
            for t, parts in enumerate(front):
                if t >= RING:
                    sp.wait_ge(tiles_used, t - RING + 1)
                for src, off, n in parts:
                    k = src.shape[1]
                    dst = ring[:, slot(t), off:off + k * n].rearrange("p (k n) -> p k n", k=k)
                    sp.dma_start(dst, src).then_inc(landed[slot(t)], 16)

            def load_expert(pair, q, e):
                for n, (kind, g) in enumerate(order):
                    j = q * NT + n
                    s, _ = expert_tile(q, n)
                    if j < RING:
                        sp.wait_ge(tiles_used, FRONT + j - RING + 1)
                    sp.wait_ge(lo_ready, pair * (4 * NT) + (2 * j + 2))
                    w = (l1_e_gate, l1_e_up, l1_e_down)[kind]
                    row = w[bass.ds(e, 1), :, :].rearrange("a r c -> (a r) c")
                    if kind < 2:
                        src = row[:, g * TILE:(g + 1) * TILE]
                    else:
                        src = row[g * TILE:(g + 1) * TILE, :]
                    k = src.shape[0] // P
                    sp.dma_start(ring[:, s, :].rearrange("p (k n) -> p k n", k=k),
                                 src.rearrange("(k p) n -> p k n", p=P)).then_inc(landed[s], 16)

            with sp.Fori(0, NE // 2) as i:
                for q in range(2):
                    load_expert(i, q, i * 2 + q)
            sp.wait_ge(flag_ready, 1)
            most = sp.value_load(flag[0:1, 0:1], min_val=0, max_val=T)
            with sp.If(most > CAP):
                with sp.Fori(1, ROUNDS) as r:
                    with sp.Fori(0, NE // 2) as i:
                        for q in range(2):
                            load_expert(r * (NE // 2) + i, q, i * 2 + q)
            for t in range(TT):
                sp.wait_ge(fin_ready, t + 1)
                sp.dma_start(out[0, t * P:(t + 1) * P, :], xn[:, t, :]).then_inc(stored, 16)
            sp.wait_ge(stored, 16 * TT)

        @block.gpsimd
        def _(pool):
            pool.memset(ident[:, :], 0.0).then_inc(pool_chain, 1)
            pool.wait_ge(pool_chain, 1)
            pool.affine_select(out=ident[:, :], in_=ident[:, :], compare_op=ALU.not_equal, fill=1.0, base=0,
                               pattern=[[-1, P]], channel_multiplier=1).then_inc(ident_ready, 1)
            pool.memset(minus_half[:, :], -0.5).then_inc(pool_chain, 1)
            pool.memset(upper[:, :], 1.0).then_inc(pool_chain, 1)
            pool.memset(mask_qk[:, :], 0.0).then_inc(pool_chain, 1)
            pool.memset(mask_kq[:, :], 0.0).then_inc(pool_chain, 1)
            pool.memset(neg_sel[:, :, :], 0.0).then_inc(pool_chain, 1)
            pool.memset(ones[:, :], 1.0).then_inc(pool_chain, 1)
            pool.memset(ch_mean[:, :], 1.0 / CC).then_inc(pool_chain, 1)
            pool.memset(upad[:, :, 0:PAD0], 0.0).then_inc(pool_chain, 1)
            pool.iota(slot_no[:, :], pattern=[[1, CAP]], base=0, channel_multiplier=0,
                      allow_small_or_imprecise_dtypes=True).then_inc(pool_chain, 1)
            pool.iota(pick_order[:, :, :], pattern=[[0, TT], [-1, NE]], base=NE, channel_multiplier=0,
                      allow_small_or_imprecise_dtypes=True).then_inc(pool_chain, 1)
            pool.wait_ge(pool_chain, 11)
            pool.affine_select(out=upper[:, :], in_=upper[:, :], compare_op=ALU.is_ge, fill=0.0, base=0,
                               pattern=[[1, P]], channel_multiplier=-1).then_inc(const_ready, 1)
            pool.affine_select(out=mask_qk[:, :], in_=mask_qk[:, :], compare_op=ALU.is_ge, fill=NEG, base=0,
                               pattern=[[-1, P]], channel_multiplier=1).then_inc(const_ready, 1)
            pool.affine_select(out=mask_kq[:, :], in_=mask_kq[:, :], compare_op=ALU.is_ge, fill=NEG, base=0,
                               pattern=[[1, P]], channel_multiplier=-1).then_inc(const_ready, 1)
            pool.affine_select(out=neg_sel[:, :, :], in_=neg_sel[:, :, :], compare_op=ALU.not_equal, fill=-1.0,
                               base=0, pattern=[[-1, H], [0, P]], channel_multiplier=1).then_inc(const_ready, 1)

            def rstd_of_norm(i):
                pool.wait_ge(var_ready, i + 1)
                pool.tensor_tensor(ss[:, 2, :], ss[:, 1, :], minus_half[:, 0:TT], ALU.pow).then_inc(rstd_ready, 1)

            rstd_of_norm(0)
            rstd_of_norm(1)
            pool.wait_ge(res_added, 8)
            pool.memset(upad1[:, :, 0:PAD1], 0.0).then_inc(pads_ready, 1)
            pool.memset(v_aug[:, :, :, P:P + 1], 1.0).then_inc(pads_ready, 1)
            rstd_of_norm(2)
            pool.wait_ge(hvar_ready, 1)
            pool.tensor_tensor(S(33), S(32), minus_half[:, 0:TT * H], ALU.pow).then_inc(hrstd_ready, 1)
            rstd_of_norm(3)
            rstd_of_norm(4)

        @block.scalar
        def _(act):
            def row(dst, src):
                act.dma_start(dst, src.rearrange("(r p) -> r p", p=P)).then_inc(params_in, 16)

            for i, g in enumerate((l0_norm1_g, l0_norm2_g, l1_norm1_g, l1_norm2_g)):
                row(rows1[G_NORM[i]:G_NORM[i] + KD, :], g)
            row(rows1[C_DWB:C_DWB + NC4, :], l0_dw_b)
            row(rows1[C_CLNG:C_CLNG + NC4, :], l0_cln_g)
            row(rows1[C_CLNB:C_CLNB + NC4, :], l0_cln_b)
            row(rows1[C_CB1:C_CB1 + KD, :], l1_conv_b)
            row(rows1[C_HN:C_HN + KD, :], l1_hnorm_g)
            row(rows1[C_CW1:N_ROWS1, :], l1_conv_w.rearrange("t c -> (t c)"))
            row(rows2[0:N_ROWS2, :], l0_dw_w.rearrange("t c -> (t c)"))
            act.dma_start(bf0[:, :], l0_b_f.partition_broadcast(P)).then_inc(small_in, 16)
            act.dma_start(bif1[:, 0:H], l1_b_i.partition_broadcast(P)).then_inc(small_in, 16)
            act.dma_start(bif1[:, H:2 * H], l1_b_f.partition_broadcast(P)).then_inc(small_in, 16)

            def norm_squares(i):
                if i == 0:
                    act.wait_ge(x_in, 16 * TT)
                elif i < 4:
                    act.wait_ge(res_added, 4 * i)
                else:
                    act.wait_ge(moe_done, 1)
                for t in range(TT):
                    act.activation(xn[:, t, :], xres[:, t, :], ACT.Square,
                                   accum_out=ss[:, 0, t:t + 1]).then_inc(sq_done, 1)

            def norm_gains(i):
                for b in (0, 2):
                    act.wait_ge(xT_ready, 4 * i + b + 1)
                    for k in (2 * b, 2 * b + 1):
                        act.activation(hT[:, k, :], ps[4 + b][:, (k % 2) * T:(k % 2 + 1) * T], ACT.Copy,
                                       scale=prm[:, G_NORM[i] + k:G_NORM[i] + k + 1]).then_inc(hT_act, 1)

            def log_sigmoid_part(i, az, e, l):
                act.wait_ge(absz_ready, i + 1)
                act.activation(S(e), S(az), ACT.Exp).then_inc(act_chain, 1)
                act.wait_ge(act_chain, i + 1)
                act.activation(S(l), S(e), ACT.Ln, bias=1.0).then_inc(ln_ready, 1)

            norm_squares(0)
            act.wait_ge(prm_ready, 2)
            norm_gains(0)
            log_sigmoid_part(0, 1, 2, 3)
            for c in range(NC4):
                act.wait_ge(glu_ready, c + 1)
                act.activation(glu_sg[:, c, :], ps[1 + c][:, T:2 * T], ACT.Sigmoid).then_inc(sg_ready, 1)
            for c in range(NC4):
                act.wait_ge(qk_ready, c + 1)
                b = (5, 6, 7, 0)[c]
                act.activation(qT0[:, c, :], ps[b][:, 0:T], ACT.Copy, scale=DH ** -0.5).then_inc(qk_copied, 1)
                act.activation(kT0[:, c, :], ps[b][:, T:2 * T], ACT.Copy).then_inc(qk_copied, 1)
            for t in range(TT):
                act.wait_ge(v_ready, t + 1)
                act.activation(v0[:, t, :], ps[1 + t][:, :], ACT.Copy).then_inc(v_copied, 1)
            for h in range(H):
                act.wait_ge(max_ready, h + 1)
                if h >= 2:
                    act.wait_ge(pT_ready, h - 1)
                b = (0, 5)[h % 2]
                act.activation(probs[:, h % 2, 0:P], ps[b][:, 0:P], ACT.Exp, bias=S3(5)[:, 0, h:h + 1],
                               accum_out=S3(6)[:, 0, h:h + 1]).then_inc(exp_ready, 1)
                act.activation(probs[:, h % 2, P:3 * P], ps[b][:, P:3 * P], ACT.Exp, bias=S3(5)[:, 1, h:h + 1],
                               accum_out=S3(6)[:, 1, h:h + 1]).then_inc(exp_ready, 1)
                if h == 5:
                    act.wait_ge(lnc_ready, 1)
                    act.activation(lnsq, lnc, ACT.Square).then_inc(lnsq_ready, 1)
            act.wait_ge(lnvar_ready, 1)
            act.activation(lnrstd, lnvar, ACT.Sqrt).then_inc(lnstd_ready, 1)
            act.wait_ge(ln_scaled, 1)
            for c in range(NC4):
                act.activation(catT[:, NC4 + c, :], conv[:, c, :], ACT.Silu, scale=prm[:, C_CLNG + c:C_CLNG + c + 1],
                               bias=prm[:, C_CLNB + c:C_CLNB + c + 1]).then_inc(convT_ready, 1)
            act.wait_ge(attT_ready, 1)
            act.activation(catT[:, 0:2, :].rearrange("p a b -> p (a b)"), ps[0][:, :], ACT.Copy).then_inc(attT_copied, 1)
            norm_squares(1)
            norm_gains(1)
            for c in range(NF):
                act.wait_ge(gu_ready, c + 1)
                if c >= 4:
                    act.wait_ge(hid_ready, c - 3)
                act.activation(dsg[:, c % 4, :], ps[c % 4][:, 0:T], ACT.Silu).then_inc(dsg_ready, 1)
            norm_squares(2)
            norm_gains(2)
            act.wait_ge(pads_ready, 2)
            for c in range(KD // 2):
                act.wait_ge(u1_ready, c + 1)
                act.activation(upad1[:, 2 * c:2 * c + 2, PAD1:PAD1 + T],
                               ps[1 + c][:, :].rearrange("p (a b) -> p a b", a=2), ACT.Copy).then_inc(u1_copied, 1)
            log_sigmoid_part(1, 11, 12, 13)
            for n in range(4):
                act.wait_ge(v1_ready, n + 1)
                half, t = n // 2, n % 2
                act.activation(v_aug[:, t, 4 * half:4 * half + 4, 0:P],
                               ps[(5, 6, 7, 1)[n]][:, :].rearrange("p (h d) -> p h d", h=4), ACT.Copy).then_inc(v1_copied, 1)
            for c in range(KD):
                act.wait_ge(conv1_tap, (TAPS1 - 1) * KD + c + 1)
                act.activation(uT[:, c, :], uT[:, c, :], ACT.Silu,
                               bias=prm[:, C_CB1 + c:C_CB1 + c + 1]).then_inc(uT_ready, 1)
            for n in range(4):
                act.wait_ge(o1_ready, n + 1)
                half, t = n // 2, n % 2
                act.activation(og[:, t, half * 512:half * 512 + 512], ps[2 + n][:, :], ACT.Sigmoid).then_inc(og_ready, 1)
            for h in range(H):
                act.wait_ge(qk1_ready, h + 1)
                b = (6, 7, 1, 2)[h % 4]
                act.activation(qT1[:, h, :], ps[b][:, 0:T], ACT.Copy).then_inc(qk1_copied, 1)
                act.activation(kT1[:, h, :], ps[b][:, T:2 * T], ACT.Copy, scale=P ** -0.5).then_inc(qk1_copied, 1)
            act.wait_ge(m_ready, 1)
            act.activation(S(21), S(20), ACT.Exp, scale=-1.0).then_inc(enm_ready, 1)

            def num_copy(h):
                act.wait_ge(num_ready, h + 1)
                act.activation(num[:, :, h, :], ps[5 + h % 2][:, :].rearrange("p (t d) -> p t d", t=TT)[:, :, 0:P + 1],
                               ACT.Copy).then_inc(num_copied, 1)

            for h in range(H):
                act.wait_ge(ex_ready, h + 1)
                if h >= 2:
                    act.wait_ge(w_ready, h - 1)
                act.activation(dec[:, h % 2, 0:2 * P], ps[3 + h % 2][:, 0:2 * P], ACT.Exp,
                               bias=S3(16)[:, 0, h:h + 1]).then_inc(act_chain, 1)
                act.activation(dec[:, h % 2, 2 * P:3 * P], ps[3 + h % 2][:, 2 * P:3 * P], ACT.Exp,
                               bias=S3(16)[:, 1, h:h + 1]).then_inc(dec_ready, 1)
                if h >= 1:
                    num_copy(h - 1)
            num_copy(H - 1)
            act.wait_ge(hc_ready, 1)
            for t in range(TT):
                act.activation(hsq[:, t, :], hc[:, t, :], ACT.Square).then_inc(hsq_ready, 1)
            for b in (0, 2):
                act.wait_ge(hcT_ready, b + 1)
                for k in (2 * b, 2 * b + 1):
                    act.activation(catT1[:, k, :], ps[4 + b][:, (k % 2) * T:(k % 2 + 1) * T], ACT.Copy,
                                   scale=prm[:, C_HN + k:C_HN + k + 1]).then_inc(hcT_act, 1)
            norm_squares(3)
            act.wait_ge(xn_ready, 8)
            act.dma_start(gfin[:, :], final_norm_g.partition_broadcast(P)).then_inc(gfin_in, 16)
            norm_gains(3)
            act.wait_ge(diff_ready, 1)
            act.activation(ss[:, 4, :], ss[:, 3, :], ACT.Exp).then_inc(e2_ready, 1)

            def expert(pair, q):
                def count(sem, n, per):
                    act.wait_ge(sem, pair * (2 * per) + (q * per + n))

                def hi(u):
                    s, at = expert_tile(q, u // 2)
                    if u % 2 == 0:
                        act.wait_ge(landed[s], pair * PER_PAIR + at)
                    count(split_used, u + 1, 2 * NT)
                    act.activation(w_hi[:, u % SPLITS, :], half_tile(s, u % 2), ACT.Copy).then_inc(hi_ready, 1)

                for u in range(SPLITS - 1):
                    hi(u)
                for b in range(2):
                    count(xTe_ready, b + 1, 2)
                    act.activation(x_hi[:, 4 * b:4 * b + 4, :], xT[:, 4 * b:4 * b + 4, :], ACT.Copy).then_inc(xhi_ready, 1)
                count(combT_done, 1, 1)
                act.activation(combT[0:CAP, :], ps[7][0:CAP, 0:T], ACT.Copy).then_inc(combT_ready, 1)
                for u in range(2 * NT):
                    if u + SPLITS - 1 < 2 * NT:
                        hi(u + SPLITS - 1)
                    kind, g = order[u // 2]
                    if kind == 0 and u % 2:
                        count(g_done, g + 1, GROUPS)
                        if g > 0:
                            count(htok_ready, g, GROUPS)
                        act.activation(sil, ps[0][:, :], ACT.Silu).then_inc(sil_ready, 1)
                    if u % 2 == 0 and u >= 4 and order[u // 2 - 1][0] == 1:
                        gt = order[u // 2 - 1][1]
                        count(hidT_done, gt + 1, GROUPS)
                        act.activation(h_hi[:, gt % 2, :], ps[4][:, :], ACT.Copy).then_inc(hhi_ready, 1)
                count(ysum_done, 1, 1)
                act.activation(ye[0:CAP, 512:1024], ps[3][0:CAP, :], ACT.Copy).then_inc(ye_act, 1)

            with act.Fori(0, NE // 2) as i:
                for q in range(2):
                    expert(i, q)
            act.wait_ge(flag_ready, 1)
            most = act.value_load(flag[0:1, 0:1], min_val=0, max_val=T)
            with act.If(most > CAP):
                with act.Fori(1, ROUNDS) as r:
                    with act.Fori(0, NE // 2) as i:
                        for q in range(2):
                            expert(r * (NE // 2) + i, q)
            norm_squares(4)

        @block.vector
        def _(dve):
            links = [0]

            def link(ins):
                links[0] += 1
                ins.then_inc(dve_chain, 1)
                dve.wait_ge(dve_chain, links[0])

            def bc(ap, n):
                return ap.unsqueeze(2).broadcast_to([ap.shape[0], ap.shape[1], n])

            def both(ap):
                return ap.unsqueeze(1).broadcast_to([ap.shape[0], TT, ap.shape[1]])

            def norm_scale(i):
                dve.wait_ge(sq_done, 2 * i + 2)
                dve.tensor_scalar(ss[:, 1, :], ss[:, 0, :], 1.0 / D, EPS, ALU.mult, ALU.add).then_inc(var_ready, 1)
                dve.wait_ge(rstd_ready, i + 1)
                if i == 4:
                    return
                for t in range(TT):
                    dve.tensor_scalar(xn[:, t, :], xres[:, t, :], ss[:, 2, t:t + 1], None, ALU.mult).then_inc(xn_ready, 1)

            def norm_gains(i):
                for b in (1, 3):
                    dve.wait_ge(xT_ready, 4 * i + b + 1)
                    for k in (2 * b, 2 * b + 1):
                        dve.tensor_scalar(hT[:, k, :], ps[4 + b][:, (k % 2) * T:(k % 2 + 1) * T],
                                          prm[:, G_NORM[i] + k:G_NORM[i] + k + 1], None, ALU.mult).then_inc(hT_dve, 1)

            def add_residual(stage, banks):
                for n in range(4):
                    dve.wait_ge(proj_ready, 4 * stage + n + 1)
                    half, t = n // 2, n % 2
                    v = xres[:, t, half * 512:(half + 1) * 512]
                    dve.tensor_tensor(v, v, ps[banks[n]][:, :], ALU.add).then_inc(res_added, 1)

            def neg_abs(i, z, az):
                dve.scalar_tensor_tensor(out=S(az), in0=S(z), scalar=-1.0, in1=S(z), op0=ALU.mult,
                                         op1=ALU.min).then_inc(absz_ready, 1)

            def log_f(i, z, l, lf):
                dve.wait_ge(ln_ready, i + 1)
                dve.scalar_tensor_tensor(out=S(lf), in0=S(z), scalar=0.0, in1=S(l), op0=ALU.min,
                                         op1=ALU.subtract).then_inc(logf_ready, 1)

            dve.wait_ge(prm_T, 1)
            dve.tensor_copy(prm[:, 0:N_ROWS1], ps[7][:, 0:N_ROWS1]).then_inc(prm_ready, 1)
            dve.tensor_copy(dww[:, 0:N_ROWS2], ps[7][:, P:P + N_ROWS2]).then_inc(prm_ready, 1)
            norm_scale(0)
            dve.wait_ge(prm_ready, 2)
            norm_gains(0)
            dve.wait_ge(small_in, 16 * 6)
            dve.wait_ge(gate_pre, 1)
            link(dve.tensor_tensor(S3(0), ps[0][:, 0:TT * H].rearrange("p (t h) -> p t h", t=TT), both(bf0[:, :]), ALU.add))
            neg_abs(0, 0, 1)
            log_f(0, 0, 3, 4)

            def glu(c):
                if c == 0:
                    dve.wait_ge(pool_chain, 11)
                dve.wait_ge(sg_ready, c + 1)
                dve.tensor_tensor(upad[:, c, PAD0:PAD0 + T], ps[1 + c][:, 0:T], glu_sg[:, c, :], ALU.mult).then_inc(u_ready, 1)

            glu(0)
            dve.wait_ge(cum_ready, 1)
            dve.tensor_copy(S(7), ps[0][:, 16:16 + TT * H]).then_inc(cum_copied, 1)
            glu(1)
            glu(2)
            dve.wait_ge(cumT_ready, 1)
            dve.tensor_copy(cT[:, :], ps[0][0:H, 64:64 + T]).then_inc(cT_ready, 1)
            glu(3)
            dve.wait_ge(u_ready, NC4)

            def conv_taps(first, last):
                for n in range(first, last):
                    j, c = n // NC4, n % NC4
                    w = dww[:, n:n + 1]
                    if j == 0:
                        dve.tensor_scalar(conv[:, c, :], upad[:, c, 0:T], w, prm[:, C_DWB + c:C_DWB + c + 1],
                                          ALU.mult, ALU.add).then_inc(conv_tap, 1)
                    else:
                        dve.wait_ge(conv_tap, n - NC4 + 1)
                        dve.scalar_tensor_tensor(out=conv[:, c, :], in0=upad[:, c, j:j + T], scalar=w,
                                                 in1=conv[:, c, :], op0=ALU.mult, op1=ALU.add).then_inc(conv_tap, 1)

            LATE = 9
            conv_taps(0, NC4 * TAPS - 4 * LATE)

            def fox_max(h):
                dve.wait_ge(scores_ready, h + 1)
                b = (0, 5)[h % 2]
                dve.tensor_reduce(S3(5)[:, 0, h:h + 1], ps[b][:, 0:P], AX_X, ALU.max, negate=True).then_inc(dve_chain, 1)
                dve.tensor_reduce(S3(5)[:, 1, h:h + 1], ps[b][:, P:3 * P], AX_X, ALU.max, negate=True).then_inc(max_ready, 1)
                links[0] += 1

            def fox_pT(h):
                dve.wait_ge(pT_ready, h + 1)
                if h >= 2:
                    dve.wait_ge(pv_ready, h - 1)
                dve.tensor_copy(probsT[:, h % 2, :], ps[6 + h % 2][:, 0:3 * P]).then_inc(pT_copied, 1)

            for h in range(H + 1):
                if h < H:
                    fox_max(h)
                if h >= 1:
                    fox_pT(h - 1)
                if h < 4:
                    conv_taps(NC4 * TAPS - (4 - h) * LATE, NC4 * TAPS - (3 - h) * LATE)
                if h == 5:
                    dve.wait_ge(conv_tap, NC4 * TAPS)
                    dve.wait_ge(ln_mean, 1)
                    dve.tensor_tensor(lnc, conv, ps[3][:, 0:T].unsqueeze(1).broadcast_to([P, NC4, T]),
                                      ALU.subtract).then_inc(lnc_ready, 1)
                if h == 7:
                    dve.wait_ge(ln_var, 1)
                    dve.tensor_scalar(lnvar, ps[4][:, 0:T], EPS, None, ALU.add).then_inc(lnvar_ready, 1)
            dve.wait_ge(exp_ready, 2 * H)
            link(dve.reciprocal(S(8), S(6)))
            dve.wait_ge(lnstd_ready, 1)
            link(dve.reciprocal(lnvar, lnrstd))
            dve.tensor_tensor(conv, lnc, lnvar.unsqueeze(1).broadcast_to([P, NC4, T]), ALU.mult).then_inc(ln_scaled, 1)
            dve.wait_ge(pv_ready, H)
            for t in range(TT):
                dve.tensor_tensor(att[:, t, :].rearrange("p (h d) -> p h d", h=H),
                                  ps[1 + t][:, :].rearrange("p (h d) -> p h d", h=H), bc(S3(8)[:, t, :], DH),
                                  ALU.mult).then_inc(att_ready, 1)
            dve.wait_ge(attT_ready, 2)
            dve.tensor_copy(catT[:, 2:4, :].rearrange("p a b -> p (a b)"), ps[5][:, :]).then_inc(attT_copied, 1)
            add_residual(0, (0, 1, 2, 3))
            norm_scale(1)
            norm_gains(1)
            for c in range(NF):
                dve.wait_ge(dsg_ready, c + 1)
                dve.tensor_tensor(hid[:, c, :], ps[c % 4][:, T:2 * T], dsg[:, c % 4, :], ALU.mult).then_inc(hid_ready, 1)
            add_residual(1, (4, 5, 6, 7))
            norm_scale(2)
            norm_gains(2)
            dve.wait_ge(gate_pre, 2)
            gates = ps[0][:, 0:2 * TT * H].rearrange("p (t g) -> p t g", t=TT)
            link(dve.tensor_tensor(S3(9), gates[:, :, 0:H], both(bif1[:, 0:H]), ALU.add))
            link(dve.tensor_tensor(S3(10), gates[:, :, H:2 * H], both(bif1[:, H:2 * H]), ALU.add))
            neg_abs(1, 10, 11)
            for c in range(KD // 2):
                dve.wait_ge(u1_copied, c + 1)
            for j in range(TAPS1):
                for c in range(KD):
                    w = prm[:, C_CW1 + j * KD + c:C_CW1 + j * KD + c + 1]
                    if j == 0:
                        dve.tensor_scalar(uT[:, c, :], upad1[:, c, 0:T], w, None, ALU.mult).then_inc(conv1_tap, 1)
                    else:
                        dve.wait_ge(conv1_tap, KD * (j - 1) + c + 1)
                        dve.scalar_tensor_tensor(out=uT[:, c, :], in0=upad1[:, c, j:j + T], scalar=w,
                                                 in1=uT[:, c, :], op0=ALU.mult, op1=ALU.add).then_inc(conv1_tap, 1)
            log_f(1, 10, 13, 14)
            dve.wait_ge(cum_ready, 2)
            link(dve.tensor_copy(S(15), ps[0][:, 64:64 + TT * H]))
            dve.tensor_tensor(S(16), S(9), S(15), ALU.subtract).then_inc(cum_copied, 1)
            dve.wait_ge(cumT_ready, 2)
            link(dve.tensor_copy(aT[:, :], ps[0][0:H, 128:128 + T]))
            dve.tensor_tensor_scan(GT[:, :], aT[:, :], aT[:, :], 0.0, ALU.max, ALU.max).then_inc(gT_ready, 1)
            dve.wait_ge(gt_back, 1)
            dve.tensor_tensor(S(20), S(15), ps[0][:, 400:400 + TT * H], ALU.add).then_inc(m_ready, 1)
            for h in range(H):
                dve.wait_ge(dec_ready, h + 1)
                if h >= 2:
                    dve.wait_ge(num_ready, h - 1)
                dve.tensor_tensor(wts[:, h % 2, :], ps[1 + h % 2][:, 0:3 * P], dec[:, h % 2, :], ALU.mult).then_inc(w_ready, 1)
            dve.wait_ge(num_copied, H)
            dve.wait_ge(enm_ready, 1)
            nq = num[:, :, :, P:P + 1].rearrange("p t h o -> p t (h o)")
            link(dve.tensor_copy(S3(22), nq))
            link(dve.scalar_tensor_tensor(out=S(23), in0=S(22), scalar=-1.0, in1=S(22), op0=ALU.mult, op1=ALU.max))
            link(dve.tensor_tensor(S(24), S(23), S(21), ALU.max))
            link(dve.reciprocal(S(25), S(24)))
            dve.wait_ge(og_ready, 4)
            for t in range(TT):
                v = hc[:, t, :].rearrange("p (h d) -> p h d", h=H)
                link(dve.tensor_tensor(v, num[:, t, :, 0:P], bc(S3(25)[:, t, :], P), ALU.mult))
            dve.tensor_tensor(hc, hc, og, ALU.mult).then_inc(hc_ready, 1)
            dve.wait_ge(hsq_ready, 2)
            link(dve.tensor_reduce(S(31), hsq.rearrange("p t (h d) -> p (t h) d", h=H), AX_X, ALU.add))
            dve.tensor_scalar(S(32), S(31), 1.0 / P, EPS, ALU.mult, ALU.add).then_inc(hvar_ready, 1)
            dve.wait_ge(hrstd_ready, 1)
            dve.wait_ge(hc_ready, 1)
            for t in range(TT):
                v = hc[:, t, :].rearrange("p (h d) -> p h d", h=H)
                dve.tensor_tensor(v, v, bc(S3(33)[:, t, :], P), ALU.mult).then_inc(hn_ready, 1)
            for b in (1, 3):
                dve.wait_ge(hcT_ready, b + 1)
                for k in (2 * b, 2 * b + 1):
                    dve.tensor_scalar(catT1[:, k, :], ps[4 + b][:, (k % 2) * T:(k % 2 + 1) * T],
                                      prm[:, C_HN + k:C_HN + k + 1], None, ALU.mult).then_inc(hcT_dve, 1)
            add_residual(2, (0, 1, 2, 3))
            norm_scale(3)
            norm_gains(3)
            dve.tensor_copy(cur[:, 0, :], ss[:, 2, :]).then_inc(y_added, 4)
            dve.tensor_copy(cur[:, 1, :], ss[:, 2, :]).then_inc(lo_ready, 2 * RING)
            dve.wait_ge(logits_ready, 1)
            L, p1, oh1, l2, p2, oh2, t1, t2 = 0, 1, 2, 3, 4, 5, 6, 7
            link(dve.tensor_copy(S(L), ps[0][:, 0:TT * NE]))

            def first_max(l, p, oh, top):
                link(dve.tensor_reduce(top, S3(l), AX_X, ALU.max))
                link(dve.tensor_tensor(S3(p), S3(l), bc(top, NE), ALU.is_equal))
                link(dve.tensor_tensor(S3(p), S3(p), pick_order[:, :, :], ALU.mult))
                link(dve.tensor_reduce(ss[:, 7, :], S3(p), AX_X, ALU.max))
                link(dve.tensor_tensor(S3(oh), S3(p), bc(ss[:, 7, :], NE), ALU.is_equal))

            first_max(L, p1, oh1, ss[:, 5, :])
            link(dve.scalar_tensor_tensor(out=S(l2), in0=S(oh1), scalar=NEG, in1=S(L), op0=ALU.mult, op1=ALU.add))
            first_max(l2, p2, oh2, ss[:, 6, :])
            dve.tensor_tensor(S(8), S(oh1), S(oh2), ALU.add).then_inc(mask_ready, 1)
            dve.tensor_tensor(ss[:, 3, :], ss[:, 6, :], ss[:, 5, :], ALU.subtract).then_inc(diff_ready, 1)
            dve.wait_ge(e2_ready, 1)
            link(dve.tensor_scalar(ss[:, 5, :], ss[:, 4, :], 1.0, None, ALU.add))
            link(dve.reciprocal(ss[:, 6, :], ss[:, 5, :]))
            link(dve.tensor_tensor(ss[:, 7, :], ss[:, 4, :], ss[:, 6, :], ALU.mult))
            link(dve.tensor_tensor(S3(t1), S3(oh1), bc(ss[:, 6, :], NE), ALU.mult))
            link(dve.tensor_tensor(S3(t2), S3(oh2), bc(ss[:, 7, :], NE), ALU.mult))
            link(dve.tensor_tensor(S(9), S(t1), S(t2), ALU.add))
            dve.wait_ge(pos_ready, 1)
            link(dve.tensor_tensor(S(10), ps[0][:, 64:64 + TT * NE], S(8), ALU.mult))
            link(dve.tensor_scalar(S(11), S(10), -1.0, None, ALU.add))
            link(dve.tensor_reduce(ss[:, 3, 0:1], ps[0][:, 96:96 + NE], AX_X, ALU.max))
            dve.tensor_copy(flag[:, 0:1], ss[:, 3, 0:1]).then_inc(flag_ready, 1)

            def expert(pair, q, e, r=None):
                def count(sem, n, per):
                    dve.wait_ge(sem, pair * (2 * per) + (q * per + n))

                def lo(u):
                    s, _ = expert_tile(q, u // 2)
                    count(hi_ready, u + 1, 2 * NT)
                    dve.tensor_tensor(w_lo[:, u % SPLITS, :], half_tile(s, u % 2), w_hi[:, u % SPLITS, :].bitcast(F32),
                                      ALU.subtract).then_inc(lo_ready, 1)

                if r is not None:
                    dve.wait_ge(round_ready, r)
                dve.tensor_copy(cur[:, 0, :].unsqueeze(2), S3(11)[:, :, bass.ds(e, 1)]).then_inc(cur_ready, 1)
                dve.tensor_copy(cur[:, 1, :].unsqueeze(2), S3(9)[:, :, bass.ds(e, 1)]).then_inc(cur_ready, 1)
                count(cur_ready, 2, 2)
                for t in range(TT):
                    dve.tensor_scalar(disp[:, t, :], slot_no[:, :], cur[:, 0, t:t + 1], None,
                                      ALU.is_equal).then_inc(route_ready, 1)
                    dve.tensor_scalar(comb[:, t, :], slot_no[:, :], cur[:, 0, t:t + 1], cur[:, 1, t:t + 1],
                                      ALU.is_equal, ALU.mult).then_inc(route_ready, 1)
                for u in range(SPLITS - 1):
                    lo(u)
                for b in range(2):
                    count(disp_done, b + 1, 2)
                    g0 = G_NORM[3] + 4 * b
                    dve.tensor_tensor(xT[:, 4 * b:4 * b + 4, :], ps[5 + b][:, 0:4 * CAP].rearrange("p (k s) -> p k s", k=4),
                                      bc(prm[:, g0:g0 + 4], CAP), ALU.mult).then_inc(xTe_ready, 1)
                for b in range(2):
                    count(xhi_ready, b + 1, 2)
                    v = slice(4 * b, 4 * b + 4)
                    dve.tensor_tensor(x_lo[:, v, :], xT[:, v, :], x_hi[:, v, :].bitcast(F32), ALU.subtract).then_inc(xlo_ready, 1)
                for u in range(2 * NT):
                    if u + SPLITS - 1 < 2 * NT:
                        lo(u + SPLITS - 1)
                    kind, g = order[u // 2]
                    if kind == 1 and u % 2:
                        count(u_done, g + 1, GROUPS)
                        dve.wait_ge(sil_ready, pair * (2 * GROUPS) + (q * GROUPS + g + 1))
                        dve.tensor_tensor(htok, ps[1][:, :], sil, ALU.mult).then_inc(htok_ready, 1)
                    if u % 2 == 0 and u >= 4 and order[u // 2 - 1][0] == 1:
                        gt = order[u // 2 - 1][1]
                        count(hhi_ready, gt + 1, GROUPS)
                        dve.tensor_tensor(h_lo[:, gt % 2, :], ps[4][:, :], h_hi[:, gt % 2, :].bitcast(F32),
                                          ALU.subtract).then_inc(hlo_ready, 1)
                count(ysum_done, 1, 1)
                dve.tensor_copy(ye[0:CAP, 0:512], ps[2][0:CAP, :]).then_inc(ye_dve, 1)
                for n in range(4):
                    count(y_done, n + 1, 4)
                    t, half = n // 2, n % 2
                    v = xres[:, t, half * 512:(half + 1) * 512]
                    dve.tensor_tensor(v, v, ps[(5, 6, 0, 1)[n]][:, :], ALU.add).then_inc(y_added, 1)

            dve.wait_ge(dve_chain, links[0])
            with dve.Fori(0, NE // 2) as i:
                for q in range(2):
                    expert(i, q, i * 2 + q)
            dve.wait_ge(flag_ready, 1)
            most = dve.value_load(flag[0:1, 0:1], min_val=0, max_val=T)
            with dve.If(most > CAP):
                with dve.Fori(1, ROUNDS) as r:
                    dve.wait_ge(cur_ready, r * (2 * NE))
                    dve.tensor_scalar(S(11), S(11), -float(CAP), None, ALU.add).then_inc(round_ready, 1)
                    with dve.Fori(0, NE // 2) as i:
                        for q in range(2):
                            expert(r * (NE // 2) + i, q, i * 2 + q, r)
                dve.wait_ge(y_added, ROUNDS * NE * 4 + 4)
            dve.wait_ge(y_added, NE * 4 + 4)
            dve.tensor_copy(flag[:, 1:2], flag[:, 0:1]).then_inc(moe_done, 1)
            norm_scale(4)
            dve.wait_ge(gfin_in, 16)
            for t in range(TT):
                dve.scalar_tensor_tensor(out=xn[:, t, :], in0=xres[:, t, :], scalar=ss[:, 2, t:t + 1], in1=gfin[:, :],
                                         op0=ALU.mult, op1=ALU.mult).then_inc(fin_ready, 1)

        @block.tensor
        def _(pe):
            def arrived(t):
                pe.wait_ge(landed[slot(t)], landed_at[t])

            def turn(src, ready, i, done, frees=False):
                for b in range(4):
                    for k in (2 * b, 2 * b + 1):
                        for t in range(TT):
                            if b == 0 and k == 0:
                                pe.wait_ge(ready, 2 * i + t + 1)
                            last = pe.transpose(ps[4 + b][:, (k % 2) * T + t * P:(k % 2) * T + (t + 1) * P],
                                                src[:, t, k * P:(k + 1) * P], ident[:, :])
                            if frees and k == 0 and t == 0:
                                last.then_inc(tiles_used, 1)
                    last.then_inc(done, 1)

            def hT_wait(i):
                pe.wait_ge(hT_act, 4 * i + 4)
                pe.wait_ge(hT_dve, 4 * i + 4)

            def feature_major(o, w, c, frees=False):
                for k in range(KD):
                    last = pe.matmul(o, w[:, k, c * P:(c + 1) * P], hT[:, k, :], start=(k == 0), stop=(k == KD - 1))
                    if k == 0 and frees:
                        last.then_inc(tiles_used, 1)
                return last

            def token_major(o, w, t, src=hT, frees=False):
                for k in range(KD):
                    last = pe.matmul(o, src[:, k, t * P:(t + 1) * P], w[:, k, :], start=(k == 0), stop=(k == KD - 1))
                    if k == 0 and frees:
                        last.then_inc(tiles_used, 1)
                return last

            def cumulate(o, src):
                pe.matmul(o[:, 0:H], upper[:, :], src[:, 0, :], start=True, stop=True)
                pe.matmul(o[:, H:2 * H], ones[:, :], src[:, 0, :], start=True, stop=False)
                return pe.matmul(o[:, H:2 * H], upper[:, :], src[:, 1, :], start=False, stop=True)

            def out_proj(stage, t0, src, banks):
                for n in range(4):
                    half, t = n // 2, n % 2
                    if t == 0:
                        arrived(t0 + half)
                    w = tile(t0 + half, KD, TILE)
                    token_major(ps[banks[n]][:, :], w, t, src, frees=(n == 2)).then_inc(proj_ready, 1)

            pe.wait_ge(ident_ready, 1)
            pe.wait_ge(params_in, 16 * 11)
            pe.transpose(ps[7][:, 0:N_ROWS1], rows1[0:N_ROWS1, :], ident[0:N_ROWS1, 0:N_ROWS1])
            pe.transpose(ps[7][:, P:P + N_ROWS2], rows2[0:N_ROWS2, :], ident[0:N_ROWS2, 0:N_ROWS2]).then_inc(prm_T, 1)
            pe.wait_ge(prm_ready, 2)
            turn(xn, xn_ready, 0, xT_ready)
            pe.wait_ge(small_in, 16 * 6)
            hT_wait(0)
            token_major(ps[0][:, 0:H], wf, 0)
            token_major(ps[0][:, H:2 * H], wf, 1).then_inc(gate_pre, 1)
            arrived(T_GLU)
            arrived(T_GLU + 1)
            for c in range(NC4):
                feature_major(ps[1 + c][:, 0:T], tile(T_GLU, KD, TILE), c)
                feature_major(ps[1 + c][:, T:2 * T], tile(T_GLU + 1, KD, TILE), c,
                              frees=(c == NC4 - 1)).then_inc(glu_ready, 1)
                if c == 0:
                    pe.wait_ge(const_ready, 4)
                    pe.wait_ge(pool_chain, 11)
                    pe.wait_ge(logf_ready, 1)
                    cumulate(ps[0][:, 16:16 + 2 * H], S3(4)).then_inc(cum_ready, 1)
                if c == 2:
                    pe.wait_ge(cum_copied, 1)
                    pe.transpose(ps[0][0:H, 64:64 + P], S3(7)[:, 0, :], ident[:, :])
                    pe.transpose(ps[0][0:H, 64 + P:64 + T], S3(7)[:, 1, :], ident[:, :]).then_inc(cumT_ready, 1)
            arrived(T_Q)
            arrived(T_K)
            for c in range(NC4):
                b = (5, 6, 7, 0)[c]
                if b == 0:
                    pe.wait_ge(cT_ready, 1)
                feature_major(ps[b][:, 0:T], tile(T_Q, KD, TILE), c, frees=(c == 0))
                feature_major(ps[b][:, T:2 * T], tile(T_K, KD, TILE), c, frees=(c == NC4 - 1)).then_inc(qk_ready, 1)
            arrived(T_V)
            for t in range(TT):
                pe.wait_ge(u_ready, t + 1)
                token_major(ps[1 + t][:, :], tile(T_V, KD, TILE), t, frees=(t == 0)).then_inc(v_ready, 1)
            def scores(h):
                lo, c, b = DH * (h % 2), h // 2, (0, 5)[h % 2]
                if h >= 2:
                    pe.wait_ge(exp_ready, 2 * (h - 1))
                for t, o in ((0, ps[b][:, 0:P]), (1, ps[b][:, P:3 * P])):
                    n = (t + 1) * P
                    last = pe.matmul(o, qT0[lo:lo + DH, c, t * P:(t + 1) * P], kT0[lo:lo + DH, c, 0:n], start=True, stop=False)
                    if h == 0 and t == 0:
                        last.then_inc(tiles_used, 1)
                    pe.matmul(o, neg_sel[:, h, :], cT[:, 0:n], start=False, stop=False)
                    last = pe.matmul(o[:, n - P:n], ident[:, :], mask_qk[:, :], start=False, stop=True)
                last.then_inc(scores_ready, 1)

            def turn_probs(h):
                pe.wait_ge(exp_ready, 2 * h + 2)
                if h >= 2:
                    pe.wait_ge(pT_copied, h - 1)
                for j in range(3):
                    last = pe.transpose(ps[6 + h % 2][:, j * P:(j + 1) * P], probs[:, h % 2, j * P:(j + 1) * P], ident[:, :])
                last.then_inc(pT_ready, 1)

            def values(h):
                pe.wait_ge(pT_copied, h + 1)
                cols = slice(h * DH, (h + 1) * DH)
                pe.matmul(ps[1][:, cols], probsT[:, h % 2, 0:P], v0[:, 0, cols], start=True, stop=True)
                pe.matmul(ps[2][:, cols], probsT[:, h % 2, P:2 * P], v0[:, 0, cols], start=True, stop=False)
                pe.matmul(ps[2][:, cols], probsT[:, h % 2, 2 * P:3 * P], v0[:, 1, cols], start=False,
                          stop=True).then_inc(pv_ready, 1)

            pe.wait_ge(u_ready, NC4)
            pe.wait_ge(qk_copied, 2 * NC4)
            pe.wait_ge(v_copied, TT)
            for i in range(H + 2):
                if i < H:
                    scores(i)
                if i == 5:
                    pe.wait_ge(conv_tap, NC4 * TAPS)
                    for c in range(NC4):
                        last = pe.matmul(ps[3][:, 0:T], ch_mean[:, :], conv[:, c, :], start=(c == 0), stop=(c == NC4 - 1))
                    last.then_inc(ln_mean, 1)
                if i == 7:
                    pe.wait_ge(lnsq_ready, 1)
                    for c in range(NC4):
                        last = pe.matmul(ps[4][:, 0:T], ch_mean[:, :], lnsq[:, c, :], start=(c == 0), stop=(c == NC4 - 1))
                    last.then_inc(ln_var, 1)
                if 1 <= i <= H:
                    turn_probs(i - 1)
                if i >= 2:
                    values(i - 2)
            pe.wait_ge(att_ready, TT)
            for j in range(FW // P):
                for t in range(TT):
                    last = pe.transpose(ps[(0, 5)[j // 2]][:, (j % 2) * T + t * P:(j % 2) * T + (t + 1) * P],
                                        att[:, t, j * P:(j + 1) * P], ident[:, :])
                if j % 2:
                    last.then_inc(attT_ready, 1)
            pe.wait_ge(attT_copied, 2)
            pe.wait_ge(convT_ready, NC4)
            out_proj(0, T_OUT0, catT, (0, 1, 2, 3))
            turn(xn, xn_ready, 1, xT_ready, frees=True)
            hT_wait(1)
            for c in range(NF):
                t = T_PAIR + c // 2
                if c % 2 == 0:
                    arrived(t)
                if c >= 4:
                    pe.wait_ge(hid_ready, c - 3)
                w = tile(t, 2 * KD, 256)
                feature_major(ps[c % 4][:, 0:T], w[:, 0:KD, :], c % 2, frees=(c % 2 == 0 and c > 0))
                feature_major(ps[c % 4][:, T:2 * T], w[:, KD:2 * KD, :], c % 2).then_inc(gu_ready, 1)
            for f in range(NF):
                if f % 4 == 0:
                    arrived(T_DOWN + f // 4)
                pe.wait_ge(hid_ready, f + 1)
                w = tile(T_DOWN + f // 4, 4, D)
                for n in range(4):
                    half, t = n // 2, n % 2
                    last = pe.matmul(ps[4 + n][:, :], hid[:, f, t * P:(t + 1) * P], w[:, f % 4, half * 512:(half + 1) * 512],
                                     start=(f == 0), stop=(f == NF - 1))
                    if f % 4 == 0 and n == 0:
                        last.then_inc(tiles_used, 1)
                    if f == NF - 1:
                        last.then_inc(proj_ready, 1)
            turn(xn, xn_ready, 2, xT_ready, frees=True)
            hT_wait(2)
            token_major(ps[0][:, 0:2 * H], wif, 0)
            token_major(ps[0][:, 2 * H:4 * H], wif, 1).then_inc(gate_pre, 1)
            for c in range(KD):
                if c % 4 == 0:
                    arrived(T_U + c // 4)
                last = feature_major(ps[1 + c // 2][:, (c % 2) * T:(c % 2 + 1) * T], tile(T_U + c // 4, KD, TILE), c % 4,
                                     frees=(c == 4))
                if c % 2:
                    last.then_inc(u1_ready, 1)
            for n in range(4):
                half, t = n // 2, n % 2
                if t == 0:
                    arrived(T_V1 + half)
                if n == 3:
                    pe.wait_ge(u1_copied, 1)
                token_major(ps[(5, 6, 7, 1)[n]][:, :], tile(T_V1 + half, KD, TILE), t, frees=(t == 0)).then_inc(v1_ready, 1)
            pe.wait_ge(logf_ready, 2)
            cumulate(ps[0][:, 64:64 + 2 * H], S3(14)).then_inc(cum_ready, 1)
            for n in range(4):
                half, t = n // 2, n % 2
                if t == 0:
                    arrived(T_O1 + half)
                if n == 0:
                    pe.wait_ge(u1_copied, 4)
                if n == 3:
                    pe.wait_ge(v1_copied, 1)
                token_major(ps[2 + n][:, :], tile(T_O1 + half, KD, TILE), t, frees=(t == 0)).then_inc(o1_ready, 1)
                if n == 1:
                    pe.wait_ge(cum_copied, 2)
                    for tt in range(TT):
                        last = pe.transpose(ps[0][0:H, P + tt * P:P + (tt + 1) * P], S3(16)[:, tt, :], ident[:, :])
                    last.then_inc(cumT_ready, 1)
            pe.wait_ge(gT_ready, 1)
            for t in range(TT):
                last = pe.transpose(ps[0][:, 400 + t * H:400 + (t + 1) * H], GT[:, t * P:(t + 1) * P], ident[0:H, 0:H])
            last.then_inc(gt_back, 1)
            arrived(T_QK1)
            w = tile(T_QK1, 2 * H, P)
            pe.wait_ge(v1_copied, 4)
            for h in range(H):
                b = (6, 7, 1, 2)[h % 4]
                pe.wait_ge(uT_ready, h + 1)
                if h == 3:
                    pe.wait_ge(og_ready, 1)
                if h >= 4:
                    pe.wait_ge(qk1_copied, 2 * (h - 3))
                last = pe.matmul(ps[b][:, 0:T], w[:, h, :], uT[:, h, :], start=True, stop=True)
                if h == 0:
                    last.then_inc(tiles_used, 1)
                pe.matmul(ps[b][:, T:2 * T], w[:, H + h, :], uT[:, h, :], start=True, stop=True).then_inc(qk1_ready, 1)

            def decay_and_scores(h):
                s, e = ps[1 + h % 2], ps[3 + h % 2]
                if h >= 2:
                    pe.wait_ge(w_ready, h - 1)
                last = pe.matmul(s[:, 0:T], kT1[:, h, 0:P], qT1[:, h, :], start=True, stop=True)
                if h == 0:
                    last.then_inc(tiles_used, 1)
                pe.matmul(s[:, T:T + P], kT1[:, h, P:T], qT1[:, h, P:T], start=True, stop=True)
                pe.matmul(e[:, 0:T], neg_sel[:, h, :], GT[:, :], start=True, stop=False)
                pe.matmul(e[:, 0:P], ident[:, :], mask_kq[:, :], start=False, stop=True)
                pe.matmul(e[:, T:T + P], neg_sel[:, h, :], GT[:, P:T], start=True, stop=False)
                pe.matmul(e[:, T:T + P], ident[:, :], mask_kq[:, :], start=False, stop=True).then_inc(ex_ready, 1)

            def numerators(h):
                o = ps[5 + h % 2]
                pe.wait_ge(w_ready, h + 1)
                if h >= 2:
                    pe.wait_ge(num_copied, h - 1)
                pe.matmul(o[:, 0:P + 1], wts[:, h % 2, 0:P], v_aug[:, 0, h, :], start=True, stop=True)
                pe.matmul(o[:, T:T + P + 1], wts[:, h % 2, P:T], v_aug[:, 0, h, :], start=True, stop=False)
                pe.matmul(o[:, T:T + P + 1], wts[:, h % 2, T:T + P], v_aug[:, 1, h, :], start=False,
                          stop=True).then_inc(num_ready, 1)

            pe.wait_ge(qk1_copied, 2 * H)
            pe.wait_ge(og_ready, 4)
            for i in range(H + 1):
                if i < H:
                    decay_and_scores(i)
                if i >= 1:
                    numerators(i - 1)
            turn(hc, hn_ready, 0, hcT_ready)
            pe.wait_ge(hcT_act, 4)
            pe.wait_ge(hcT_dve, 4)
            out_proj(2, T_OUT1, catT1, (0, 1, 2, 3))
            turn(xn, xn_ready, 3, xT_ready, frees=True)
            hT_wait(3)
            token_major(ps[0][:, 0:NE], wr, 0)
            token_major(ps[0][:, NE:2 * NE], wr, 1).then_inc(logits_ready, 1)
            pe.wait_ge(mask_ready, 1)
            cumulate(ps[0][:, 64:64 + 2 * NE], S3(8)).then_inc(split_used, SPLITS - 1)
            pe.matmul(ps[0][:, 96:96 + NE], ones[:, :], S3(8)[:, 0, :], start=True, stop=False)
            pe.matmul(ps[0][:, 96:96 + NE], ones[:, :], S3(8)[:, 1, :], start=False, stop=True).then_inc(pos_ready, 1)

            def expert(pair, q):
                def count(sem, n, per):
                    pe.wait_ge(sem, pair * (2 * per) + (q * per + n))

                count(y_added, 4, 4)
                count(route_ready, 4, 4)
                for k in range(KD):
                    o = ps[5 + k // 4][:, (k % 4) * CAP:(k % 4 + 1) * CAP]
                    for t in range(TT):
                        last = pe.matmul(o, xn[:, t, k * P:(k + 1) * P], disp[:, t, :], start=(t == 0), stop=(t == TT - 1))
                        if k == 0 and t == 0:
                            last.then_inc(split_used, 1)
                    if k % 4 == 3:
                        last.then_inc(disp_done, 1)
                for t in range(TT):
                    last = pe.transpose(ps[7][0:CAP, t * P:(t + 1) * P], comb[:, t, :], ident[:, :])
                last.then_inc(combT_done, 1)
                count(xhi_ready, 2, 2)
                count(xlo_ready, 2, 2)
                for u in range(2 * NT):
                    kind, g = order[u // 2]
                    count(lo_ready, 2 * RING + u + 1, 2 * NT)
                    if kind < 2:
                        w = [v[:, u % SPLITS, :].rearrange("p (k n) -> p k n", k=KD // 2) for v in (w_hi, w_lo)]
                        o = ps[kind][:, :]
                        if kind == 1 and g > 0 and u % 2 == 0:
                            count(htok_ready, g, GROUPS)
                        if kind == 0 and g > 0 and u % 2 == 0:
                            count(sil_ready, g, GROUPS)
                        for kk in range(KD // 2):
                            k = (u % 2) * (KD // 2) + kk
                            last = pe.matmul(o, x_hi[:, k, :], w[0][:, kk, :], start=(k == 0), stop=False)
                            if u > 0 and kk == 0:
                                last.then_inc(split_used, 1)
                            pe.matmul(o, x_hi[:, k, :], w[1][:, kk, :], start=False, stop=False)
                            last = pe.matmul(o, x_lo[:, k, :], w[0][:, kk, :], start=False, stop=(k == KD - 1))
                        if u % 2:
                            last.then_inc((g_done, u_done)[kind], 1)
                    else:
                        w = [v[:, u % SPLITS, :].rearrange("p (k n) -> p k n", k=CPG // 2) for v in (w_hi, w_lo)]
                        if u % 2 == 0:
                            count(hlo_ready, g + 1, GROUPS)
                        for kk in range(CPG // 2):
                            f = (u % 2) * (CPG // 2) + kk
                            rows = slice(f * P, (f + 1) * P)
                            first, final = g == 0 and f == 0, g == GROUPS - 1 and f == CPG - 1
                            for a, b, st, en in ((h_hi, 0, first, False), (h_hi, 1, False, False), (h_lo, 0, False, final)):
                                for half in range(2):
                                    last = pe.matmul(ps[2 + half][:, :], a[:, g % 2, rows], w[b][:, kk, half * 512:(half + 1) * 512],
                                                     start=st, stop=en)
                                    if kk == 0 and a is h_hi and b == 0 and half == 0:
                                        last.then_inc(split_used, 1)
                        if final:
                            last.then_inc(ysum_done, 1)
                    if u % 2 == 0 and u >= 4 and order[u // 2 - 1][0] == 1:
                        gt = order[u // 2 - 1][1]
                        count(htok_ready, gt + 1, GROUPS)
                        for j in range(CPG):
                            last = pe.transpose(ps[4][:, j * P:(j + 1) * P], htok[:, j * P:(j + 1) * P], ident[:, :])
                        last.then_inc(hidT_done, 1)
                count(combT_ready, 1, 1)
                for n in range(4):
                    t, half = n // 2, n % 2
                    if n == 0:
                        count(ye_dve, 1, 1)
                    if n == 1:
                        count(ye_act, 1, 1)
                    pe.matmul(ps[(5, 6, 0, 1)[n]][:, :], combT[0:CAP, t * P:(t + 1) * P],
                              ye[0:CAP, half * 512:(half + 1) * 512], start=True, stop=True).then_inc(y_done, 1)

            with pe.Fori(0, NE // 2) as i:
                for q in range(2):
                    expert(i, q)
            pe.wait_ge(flag_ready, 1)
            most = pe.value_load(flag[0:1, 0:1], min_val=0, max_val=T)
            with pe.If(most > CAP):
                with pe.Fori(1, ROUNDS) as r:
                    with pe.Fori(0, NE // 2) as i:
                        for q in range(2):
                            expert(r * (NE // 2) + i, q)


_INS = ['x', 'l0_norm1_g', 'l0_w_in', 'l0_b_f', 'l0_dw_w', 'l0_dw_b', 'l0_cln_g', 'l0_cln_b', 'l0_w_out',
        'l0_norm2_g', 'l0_w_gate', 'l0_w_up', 'l0_w_down', 'l1_norm1_g', 'l1_w_in', 'l1_b_i', 'l1_b_f',
        'l1_conv_w', 'l1_conv_b', 'l1_wq_head', 'l1_wk_head', 'l1_hnorm_g', 'l1_w_out', 'l1_norm2_g',
        'l1_router', 'l1_e_gate', 'l1_e_up', 'l1_e_down', 'final_norm_g']


def kernel(**inputs):
    import numpy as _np
    import concourse.bacc as _bacc
    from concourse import mybir as _mybir
    from concourse.bass_utils import run_bass_kernel_spmd as _run

    nc = _bacc.Bacc("TRN2", target_bir_lowering=False, num_devices=1)
    arrays, args = {}, []
    for name in _INS:
        a = _np.ascontiguousarray(inputs[name])
        arrays[f"in_{name}_dram"] = a
        args.append(nc.dram_tensor(f"in_{name}_dram", a.shape, _mybir.dt.from_np(a.dtype), kind="ExternalInput").ap())
    out = nc.dram_tensor("out_dram", inputs["x"].shape, _mybir.dt.float32, kind="ExternalOutput").ap()
    bass_hybrid_trunk(nc, *args, out)
    r = _run(nc, [arrays], core_ids=[0])
    return r.results[0]["out_dram"]
```

```python
from contextlib import ExitStack

import concourse.bass as bass
from concourse import mybir

ALU = mybir.AluOpType
ACT = mybir.ActivationFunctionType
AX_X = mybir.AxisListType.X
F32 = mybir.dt.float32
F32R = mybir.dt.float32r
I32 = mybir.dt.int32

P = 128
EPS = 1e-6
NEG = -1e30
CAP = 128
LAYER_RING = 3
RING = 6
SPLITS = 3
TILE = 512
ARENA = 19200
COLS = 4096


def bass_hybrid_trunk(nc, x, l0_norm1_g, l0_w_in, l0_b_f, l0_dw_w, l0_dw_b, l0_cln_g, l0_cln_b, l0_w_out,
                      l0_norm2_g, l0_w_gate, l0_w_up, l0_w_down, l1_norm1_g, l1_w_in, l1_b_i, l1_b_f,
                      l1_conv_w, l1_conv_b, l1_wq_head, l1_wk_head, l1_hnorm_g, l1_w_out, l1_norm2_g,
                      l1_router, l1_e_gate, l1_e_up, l1_e_down, final_norm_g, out):
    _, T, D = x.shape
    TT = T // P
    KD = D // P
    H = l0_b_f.shape[0]
    DH = 64
    FW = H * DH
    CC = l0_dw_w.shape[1]
    NC4 = CC // P
    TAPS = l0_dw_w.shape[0]
    TAPS1 = l1_conv_w.shape[0]
    DFF = l0_w_gate.shape[1]
    NF = DFF // P
    NE, _, DFE = l1_e_gate.shape
    GROUPS = DFE // TILE
    CPG = TILE // P
    CH = GROUPS * CPG
    ROUNDS = -(-T // CAP)
    assert TT == 2 and KD == 8 and H == 8 and NE == 8 and 6 * GROUPS % RING == 0 and 6 * GROUPS % SPLITS == 0

    def wide(w, c0, n):
        return w[:, c0:c0 + n].rearrange("(k p) n -> p k n", p=P)

    front = []
    for a, b in ((3 * FW + H, 3 * FW + H + CC), (0, FW)):
        for c0 in (0, 256):
            front.append([(wide(l0_w_in, a + c0, 256), 0, 256), (wide(l0_w_in, b + c0, 256), KD * 256, 256)])
    front.append([(wide(l0_w_in, 2 * FW, TILE), 0, TILE)])
    for half in range(2):
        front.append([(wide(l0_w_out, half * TILE, TILE), 0, TILE)])
    PAIRS = DFF // 256
    for p in range(PAIRS):
        front.append([(wide(l0_w_gate, p * 256, 256), 0, 256), (wide(l0_w_up, p * 256, 256), KD * 256, 256)])
    DOWNS = -(-NF // 4)
    for t in range(DOWNS):
        n = min(4, NF - 4 * t)
        front.append([(l0_w_down[t * 512:t * 512 + n * P, :].rearrange("(k p) n -> p k n", p=P), 0, D)])
    for c0 in range(0, D, TILE):
        front.append([(wide(l1_w_in, c0, 256), 0, 256), (wide(l1_w_in, c0 + 256, 256), KD * 256, 256)])
    for c0 in range(D, 3 * D, TILE):
        front.append([(wide(l1_w_in, c0, TILE), 0, TILE)])
    front.append([(l1_wq_head.rearrange("h d e -> d h e"), 0, P), (l1_wk_head.rearrange("h d e -> d h e"), H * P, P)])
    for half in range(2):
        front.append([(wide(l1_w_out, half * TILE, TILE), 0, TILE)])
    T_OUT0, T_PAIR = 5, 7
    T_DOWN = T_PAIR + PAIRS
    T_U = T_DOWN + DOWNS
    T_V1, T_O1, T_QK1, T_OUT1 = T_U + 2, T_U + 4, T_U + 6, T_U + 7
    FRONT = T_OUT1 + 2
    assert FRONT == len(front) and NF % 2 == 0 and FRONT % RING == LAYER_RING

    halves = [(t, h) for t in range(T_OUT0) for h in range(2)]
    N_OUT0 = len(halves)
    halves += [(T_OUT0 + t, h) for h in range(2) for t in range(2)]
    N_PAIR = len(halves)
    halves += [(t, h) for t in range(T_PAIR, T_DOWN) for h in range(2)]
    N_DOWN = len(halves)
    halves += [(T_DOWN + f // 2, f % 2) for f in range(NF // 2)]
    N_IN1 = len(halves)
    halves += [(t, h) for t in range(T_U, T_QK1) for h in range(2)]
    HALVES = len(halves)

    with ExitStack() as ctx:
        def sb(name, shape, dt=F32):
            return ctx.enter_context(nc.sbuf_tensor(name, shape, dt))

        def sem(name):
            return ctx.enter_context(nc.semaphore(name))

        HALF = COLS // 2
        ring_at = -(-nc.sbuf_base // 32) * 32
        ring = sb("ring", [P, RING, COLS])
        assert nc.sbuf_base == ring_at + 4 * RING * COLS
        l_w = nc.alloc_sbuf_tensor_at("l_w", [P, SPLITS, 2, HALF], F32R, offset=ring_at + 4 * LAYER_RING * COLS)
        xres = sb("xres", [P, TT, D])
        xn = sb("xn", [P, TT, D])
        hT = sb("hT", [P, KD, T])
        arena_at = nc.sbuf_base
        arena = sb("arena", [P, ARENA])

        class Phase:
            def __init__(self):
                self.at = 0

            def __call__(self, name, shape, dt=F32):
                words = 1
                for n in shape[1:]:
                    words *= n
                t = nc.alloc_sbuf_tensor_at(name, shape, dt, offset=arena_at + 4 * self.at)
                self.at += words
                assert self.at <= ARENA, name
                return t

        layers, moe = Phase(), Phase()
        work = layers("work", [P, 13864])
        n_lo = layers("n_lo", [P, KD, T], F32R)
        ident = sb("ident", [P, P])
        upper = sb("upper", [P, P])
        ones = sb("ones", [P, P])
        ch_mean = layers("ch_mean", [P, P])
        mask_qk = layers("mask_qk", [P, P])
        mask_kq = layers("mask_kq", [P, P])
        neg_sel = layers("neg_sel", [H, H, P])
        slot_no = sb("slot_no", [P, CAP])
        pick_order = sb("pick_order", [P, TT, NE])
        minus_half = sb("minus_half", [P, TT * H])
        rows1 = layers("rows1", [P, P])
        rows2 = layers("rows2", [P, P])
        prm = sb("prm", [P, P])
        dww = layers("dww", [P, P])
        wf = layers("wf", [P, KD, H])
        wif = layers("wif", [P, KD, 2 * H])
        wr = sb("wr", [P, KD, NE])
        bf0 = sb("bf0", [P, H])
        bif1 = sb("bif1", [P, 2 * H])
        small = sb("small", [P, 40, TT * H])
        cT = layers("cT", [H, T])
        aT = layers("aT", [H, T])
        GT = layers("GT", [H, T])
        ss = sb("ss", [P, 8, TT])
        cur = sb("cur", [P, 2, TT])
        flag = sb("flag", [P, 2], I32)
        gateT = sb("gateT", [2 * H, T])

        def region(start, *dims):
            n = 1
            for d in dims:
                n *= d
            v = work[:, start:start + n]
            if len(dims) == 2:
                v = v.rearrange("p (a b) -> p a b", a=dims[0])
            if len(dims) == 3:
                v = v.rearrange("p (a b c) -> p a b c", a=dims[0], b=dims[1])
            return v

        qT0 = region(0, NC4, T)
        kT0 = region(1024, NC4, T)
        v0 = region(2048, TT, FW)
        PAD0 = TAPS - 1
        upad = region(3072, NC4, T + PAD0)
        conv = region(4216, NC4, T)
        lnc = region(5240, NC4, T)
        lnsq = region(6264, NC4, T)
        convs = region(6264, NC4, T)
        probs = region(9336, 2, 3 * P)
        probsT = region(10104, 2, 3 * P)
        att = region(10872, TT, FW)
        glu_sg = region(11896, NC4, T)
        lnvar = region(12920, T)
        lnrstd = region(13176, T)
        def rounded(name, start, *dims):
            return nc.alloc_sbuf_tensor_at(name, [P, *dims], F32R, offset=arena_at + 4 * start)

        n_hi = [rounded("n_hi0", 5240, KD, T), rounded("n_hi1", 2 * NF * T, KD, T), rounded("n_hi2", 4120, KD, T)]
        c_hi = rounded("c_hi", 7288, KD, T)
        c_lo = n_lo
        hid_hi = rounded("hid_hi", 0, NF, T)
        hid_lo = rounded("hid_lo", NF * T, NF, T)
        dsg = hT[:, 0:4, :].rearrange("p (b a) t -> p b (a t)", b=2)
        hidf = hT[:, 4:8, :].rearrange("p (b a) t -> p b (a t)", b=2)
        PAD1 = TAPS1 - 1
        upad1 = region(0, KD, T + PAD1)
        uT = region(2072, KD, T)
        qT1 = region(4120, KD, T)
        kT1 = region(6168, KD, T)
        v_aug = region(8216, TT, H, P + 1)
        og = region(10280, TT, D)
        dec = region(12328, 2, 3 * P)
        wts = region(13096, 2, 3 * P)
        hc = region(0, TT, D)
        catT1 = region(2072, KD, T)
        w_hi = moe("w_hi", [P, SPLITS, HALF], F32R)
        w_lo = moe("w_lo", [P, SPLITS, HALF], F32R)
        x_hi = moe("x_hi", [P, KD, CAP], F32R)
        x_lo = moe("x_lo", [P, KD, CAP], F32R)
        h_hi = moe("h_hi", [P, 2, TILE], F32R)
        h_lo = moe("h_lo", [P, 2, TILE], F32R)
        ye = moe("ye", [P, D])
        disp = moe("disp", [P, TT, CAP])
        comb = moe("comb", [P, TT, CAP])
        combT = moe("combT", [P, T])
        gfin = moe("gfin", [P, D])
        xT = hT[:, 0:4, :].rearrange("p a b -> p (a b)").rearrange("p (k s) -> p k s", k=KD)
        sil = hT[:, 4:6, :].rearrange("p a b -> p (a b)")
        htok = hT[:, 6:8, :].rearrange("p a b -> p (a b)")

        ps = [ctx.enter_context(nc.psum_tensor(f"bank{b}", [P, 512], F32)) for b in range(8)]

        G_NORM = [0, 8, 16, 24]
        C_DWB, C_CLNG, C_CLNB, C_CB1, C_HN, C_CW1 = 32, 36, 40, 44, 52, 60
        N_ROWS1 = C_CW1 + TAPS1 * KD
        N_ROWS2 = TAPS * NC4

        def S(i):
            return small[:, i, :]

        def S3(i):
            return small[:, i, :].rearrange("p (t h) -> p t h", t=TT)

        landed = [sem(f"landed{i}") for i in range(RING)]
        tiles_used = sem("tiles_used")
        x_in = sem("x_in")
        params_in = sem("params_in")
        small_in = sem("small_in")
        gfin_in = sem("gfin_in")
        ident_ready = sem("ident_ready")
        const_ready = sem("const_ready")
        pool_chain = sem("pool_chain")
        dve_chain = sem("dve_chain")
        act_chain = sem("act_chain")
        prm_T = sem("prm_T")
        prm_ready = sem("prm_ready")
        sq_done = sem("sq_done")
        var_ready = sem("var_ready")
        rstd_ready = sem("rstd_ready")
        xn_ready = sem("xn_ready")
        xT_ready = sem("xT_ready")
        hT_act = sem("hT_act")
        hT_dve = sem("hT_dve")
        nhi_ready = sem("nhi_ready")
        nlo_ready = sem("nlo_ready")
        hTf_ready = sem("hTf_ready")
        chi_ready = sem("chi_ready")
        clo_ready = sem("clo_ready")
        lhi_ready = sem("lhi_ready")
        llo_ready = sem("llo_ready")
        lsplit_used = sem("lsplit_used")
        gateT_ready = sem("gateT_ready")
        gateT_copied = sem("gateT_copied")
        gate_pre = sem("gate_pre")
        absz_ready = sem("absz_ready")
        ln_ready = sem("ln_ready")
        logf_ready = sem("logf_ready")
        cum_ready = sem("cum_ready")
        cum_copied = sem("cum_copied")
        cumT_ready = sem("cumT_ready")
        cT_ready = sem("cT_ready")
        glu_ready = sem("glu_ready")
        sg_ready = sem("sg_ready")
        u_ready = sem("u_ready")
        conv_tap = sem("conv_tap")
        qk_ready = sem("qk_ready")
        qk_copied = sem("qk_copied")
        v_ready = sem("v_ready")
        v_copied = sem("v_copied")
        ln_mean = sem("ln_mean")
        lnc_ready = sem("lnc_ready")
        lnsq_ready = sem("lnsq_ready")
        ln_var = sem("ln_var")
        lnvar_ready = sem("lnvar_ready")
        lnstd_ready = sem("lnstd_ready")
        ln_scaled = sem("ln_scaled")
        convT_ready = sem("convT_ready")
        scores_ready = sem("scores_ready")
        max_ready = sem("max_ready")
        exp_ready = sem("exp_ready")
        pT_ready = sem("pT_ready")
        pT_copied = sem("pT_copied")
        pv_ready = sem("pv_ready")
        att_ready = sem("att_ready")
        attT_ready = sem("attT_ready")
        proj_ready = sem("proj_ready")
        res_added = sem("res_added")
        gate_ready = sem("gate_ready")
        up_ready = sem("up_ready")
        dsg_ready = sem("dsg_ready")
        hidf_ready = sem("hidf_ready")
        hidhi_ready = sem("hidhi_ready")
        hidlo_ready = sem("hidlo_ready")
        pads_ready = sem("pads_ready")
        u1_ready = sem("u1_ready")
        u1_copied = sem("u1_copied")
        conv1_tap = sem("conv1_tap")
        uT_ready = sem("uT_ready")
        v1_ready = sem("v1_ready")
        v1_copied = sem("v1_copied")
        o1_ready = sem("o1_ready")
        og_ready = sem("og_ready")
        qk1_ready = sem("qk1_ready")
        qk1_copied = sem("qk1_copied")
        gT_ready = sem("gT_ready")
        gt_back = sem("gt_back")
        m_ready = sem("m_ready")
        enm_ready = sem("enm_ready")
        ex_ready = sem("ex_ready")
        dec_ready = sem("dec_ready")
        w_ready = sem("w_ready")
        num_ready = sem("num_ready")
        hc_ready = sem("hc_ready")
        hsq_ready = sem("hsq_ready")
        hvar_ready = sem("hvar_ready")
        hrstd_ready = sem("hrstd_ready")
        hn_ready = sem("hn_ready")
        hcT_ready = sem("hcT_ready")
        hcT_act = sem("hcT_act")
        hcT_dve = sem("hcT_dve")
        diff_ready = sem("diff_ready")
        e2_ready = sem("e2_ready")
        mask_ready = sem("mask_ready")
        pos_ready = sem("pos_ready")
        flag_ready = sem("flag_ready")
        cur_ready = sem("cur_ready")
        round_ready = sem("round_ready")
        route_ready = sem("route_ready")
        hi_ready = sem("hi_ready")
        lo_ready = sem("lo_ready")
        split_used = sem("split_used")
        disp_done = sem("disp_done")
        xTe_ready = sem("xTe_ready")
        xhi_ready = sem("xhi_ready")
        xlo_ready = sem("xlo_ready")
        combT_done = sem("combT_done")
        combT_ready = sem("combT_ready")
        g_done = sem("g_done")
        sil_ready = sem("sil_ready")
        u_done = sem("u_done")
        htok_ready = sem("htok_ready")
        hidT_done = sem("hidT_done")
        hhi_ready = sem("hhi_ready")
        hlo_ready = sem("hlo_ready")
        ysum_done = sem("ysum_done")
        ye_left = sem("ye_left")
        ye_right = sem("ye_right")
        y_done = sem("y_done")
        y_added = sem("y_added")
        moe_done = sem("moe_done")
        fin_ready = sem("fin_ready")
        stored = sem("stored")

        def slot(t):
            return t % LAYER_RING

        def tile(t, k, n):
            return ring[:, slot(t), 0:k * n].rearrange("p (k n) -> p k n", k=k)

        slot_count = [0] * RING
        landed_at = []
        for t, parts in enumerate(front):
            slot_count[slot(t)] += 16 * len(parts)
            landed_at.append(slot_count[slot(t)])
        NT = 3 * GROUPS
        PER_PAIR = 2 * NT * 16 // RING

        order = [(0, 0), (1, 0)]
        for g in range(1, GROUPS):
            order += [(0, g), (1, g), (2, g - 1)]
        order.append((2, GROUPS - 1))

        def expert_tile(q, n):
            j = q * NT + n
            s = (FRONT + j) % RING
            return s, slot_count[s] + 16 * (j // RING + 1)

        def half_tile(s, h):
            return ring[:, s, h * HALF:(h + 1) * HALF]

        U_ADD, U_COMB, U_ROUTE, U_GATHER, U_NEXT = 1, 7, 20, 33, 2 * NT - 5
        assert order[U_NEXT // 2][0] == 1 and U_NEXT % 2 and all(kind == 2 for kind, _ in order[U_NEXT // 2 + 1:])

        def passed(pair, q, n, per):
            return pair * (2 * per) + (q * per + n)

        def passed_adds(r, pair, q, n, per):
            return pair * (2 * per) + (q * per + n) if r is None else pair * (2 * per) + r * per + (q * per + n)

        def all_rounds(engine, one_round):
            one_round(None)
            engine.wait_ge(flag_ready, 1)
            most = engine.value_load(flag[0:1, 0:1], min_val=0, max_val=T)
            with engine.If(most > CAP):
                with engine.Fori(1, ROUNDS) as r:
                    one_round(r)

        def all_experts(engine, r, expert):
            base = 0 if r is None else r * (NE // 2)
            with engine.Fori(0, NE // 2 - 1) as i:
                for q in range(2):
                    expert(r, i if r is None else base + i, q, i * 2 + q, False)
            for q in range(2):
                expert(r, base + (NE // 2 - 1), q, NE - 2 + q, q == 1)

        def wait_split_input(engine, n):
            t, h = halves[n]
            if t not in [s for s, _ in halves[:n]]:
                engine.wait_ge(landed[slot(t)], landed_at[t])
            if n >= SPLITS:
                engine.wait_ge(lsplit_used, n - SPLITS + 1)

        block = ctx.enter_context(nc.Block())

        @block.sync
        def _(sp):
            for t in range(TT):
                sp.dma_start(xres[:, t, :], x[0, t * P:(t + 1) * P, :]).then_inc(x_in, 16)

            def row(dst, src):
                sp.dma_start(dst, src.rearrange("(r p) -> r p", p=P)).then_inc(params_in, 16)

            for i, g in enumerate((l0_norm1_g, l0_norm2_g, l1_norm1_g, l1_norm2_g)):
                row(rows1[G_NORM[i]:G_NORM[i] + KD, :], g)
            row(rows1[C_DWB:C_DWB + NC4, :], l0_dw_b)
            row(rows1[C_CLNG:C_CLNG + NC4, :], l0_cln_g)
            row(rows1[C_CLNB:C_CLNB + NC4, :], l0_cln_b)
            row(rows1[C_CB1:C_CB1 + KD, :], l1_conv_b)
            row(rows1[C_HN:C_HN + KD, :], l1_hnorm_g)
            row(rows1[C_CW1:N_ROWS1, :], l1_conv_w.rearrange("t c -> (t c)"))
            row(rows2[0:N_ROWS2, :], l0_dw_w.rearrange("t c -> (t c)"))
            for t, parts in enumerate(front):
                if t >= LAYER_RING:
                    sp.wait_ge(llo_ready, max(n for n, (s, _) in enumerate(halves) if s == t - LAYER_RING) + 1)
                for src, off, n in parts:
                    k = src.shape[1]
                    dst = ring[:, slot(t), off:off + k * n].rearrange("p (k n) -> p k n", k=k)
                    sp.dma_start(dst, src).then_inc(landed[slot(t)], 16)
                if t == 0:
                    for dst, w in ((wf, wide(l0_w_in, 3 * FW, H)), (wif, wide(l1_w_in, 3 * D, 2 * H)), (wr, wide(l1_router, 0, NE))):
                        sp.dma_start(dst[:, :, :], w).then_inc(small_in, 16)
                    sp.dma_start(bf0[:, :], l0_b_f.partition_broadcast(P)).then_inc(small_in, 16)
                    sp.dma_start(bif1[:, 0:H], l1_b_i.partition_broadcast(P)).then_inc(small_in, 16)
                    sp.dma_start(bif1[:, H:2 * H], l1_b_f.partition_broadcast(P)).then_inc(small_in, 16)

            def load_expert(r, pair, q, e, final):
                for n, (kind, g) in enumerate(order):
                    j = q * NT + n
                    s, _ = expert_tile(q, n)
                    if j < RING - LAYER_RING:
                        sp.wait_ge(lsplit_used, HALVES)
                    elif j < RING:
                        sp.wait_ge(tiles_used, j - LAYER_RING + 1)
                    sp.wait_ge(lo_ready, pair * (4 * NT) + (2 * j + 2))
                    w = (l1_e_gate, l1_e_up, l1_e_down)[kind]
                    row = w[bass.ds(e, 1), :, :].rearrange("a r c -> (a r) c")
                    if kind < 2:
                        src = row[:, g * TILE:(g + 1) * TILE]
                    else:
                        src = row[g * TILE:(g + 1) * TILE, :]
                    k = src.shape[0] // P
                    sp.dma_start(ring[:, s, :].rearrange("p (k n) -> p k n", k=k),
                                 src.rearrange("(k p) n -> p k n", p=P)).then_inc(landed[s], 16)

            all_rounds(sp, lambda r: all_experts(sp, r, load_expert))
            for t in range(TT):
                sp.wait_ge(fin_ready, t + 1)
                sp.dma_start(out[0, t * P:(t + 1) * P, :], xn[:, t, :]).then_inc(stored, 16)
            sp.wait_ge(stored, 16 * TT)

        @block.gpsimd
        def _(pool):
            pool.memset(ident[:, :], 0.0).then_inc(pool_chain, 1)
            pool.wait_ge(pool_chain, 1)
            pool.affine_select(out=ident[:, :], in_=ident[:, :], compare_op=ALU.not_equal, fill=1.0, base=0,
                               pattern=[[-1, P]], channel_multiplier=1).then_inc(ident_ready, 1)
            pool.memset(minus_half[:, :], -0.5).then_inc(pool_chain, 1)
            pool.memset(upper[:, :], 1.0).then_inc(pool_chain, 1)
            pool.memset(mask_qk[:, :], 0.0).then_inc(pool_chain, 1)
            pool.memset(mask_kq[:, :], 0.0).then_inc(pool_chain, 1)
            pool.memset(neg_sel[:, :, :], 0.0).then_inc(pool_chain, 1)
            pool.memset(ones[:, :], 1.0).then_inc(pool_chain, 1)
            pool.memset(ch_mean[:, :], 1.0 / CC).then_inc(pool_chain, 1)
            pool.memset(upad[:, :, 0:PAD0], 0.0).then_inc(pool_chain, 1)
            pool.iota(slot_no[:, :], pattern=[[1, CAP]], base=0, channel_multiplier=0,
                      allow_small_or_imprecise_dtypes=True).then_inc(pool_chain, 1)
            pool.iota(pick_order[:, :, :], pattern=[[0, TT], [-1, NE]], base=NE, channel_multiplier=0,
                      allow_small_or_imprecise_dtypes=True).then_inc(pool_chain, 1)
            pool.wait_ge(pool_chain, 11)
            pool.affine_select(out=upper[:, :], in_=upper[:, :], compare_op=ALU.is_ge, fill=0.0, base=0,
                               pattern=[[1, P]], channel_multiplier=-1).then_inc(const_ready, 1)
            pool.affine_select(out=mask_qk[:, :], in_=mask_qk[:, :], compare_op=ALU.is_ge, fill=NEG, base=0,
                               pattern=[[-1, P]], channel_multiplier=1).then_inc(const_ready, 1)
            pool.affine_select(out=mask_kq[:, :], in_=mask_kq[:, :], compare_op=ALU.is_ge, fill=NEG, base=0,
                               pattern=[[1, P]], channel_multiplier=-1).then_inc(const_ready, 1)
            pool.affine_select(out=neg_sel[:, :, :], in_=neg_sel[:, :, :], compare_op=ALU.not_equal, fill=-1.0,
                               base=0, pattern=[[-1, H], [0, P]], channel_multiplier=1).then_inc(const_ready, 1)

            def rstd_of_norm(i):
                for t in range(TT):
                    pool.wait_ge(var_ready, TT * i + t + 1)
                    pool.tensor_tensor(ss[:, 2, t:t + 1], ss[:, 1, t:t + 1], minus_half[:, 0:1], ALU.pow).then_inc(rstd_ready, 1)

            rstd_of_norm(0)
            rstd_of_norm(1)
            pool.wait_ge(res_added, 8)
            pool.memset(upad1[:, :, 0:PAD1], 0.0).then_inc(pads_ready, 1)
            pool.memset(v_aug[:, :, :, P:P + 1], 1.0).then_inc(pads_ready, 1)
            rstd_of_norm(2)
            for h in range(H):
                pool.wait_ge(hvar_ready, h + 1)
                pool.tensor_tensor(S3(33)[:, :, h], S3(32)[:, :, h], minus_half[:, 0:TT], ALU.pow).then_inc(hrstd_ready, 1)
            rstd_of_norm(3)
            rstd_of_norm(4)

        @block.scalar
        def _(act):
            def norm_squares(i):
                if i == 0:
                    act.wait_ge(x_in, 16 * TT)
                elif i == 4:
                    act.wait_ge(moe_done, 1)
                for t in range(TT):
                    if 0 < i < 4:
                        act.wait_ge(res_added, 4 * i - 1 + t)
                    act.activation(xn[:, t, :], xres[:, t, :], ACT.Square,
                                   accum_out=ss[:, 0, t:t + 1]).then_inc(sq_done, 1)

            def norm_gains(i):
                for b in (0, 2):
                    act.wait_ge(xT_ready, 4 * i + b + 1)
                    for k in (2 * b, 2 * b + 1):
                        act.activation(hT[:, k, :], ps[4 + b][:, (k % 2) * T:(k % 2 + 1) * T], ACT.Copy,
                                       scale=prm[:, G_NORM[i] + k:G_NORM[i] + k + 1]).then_inc(hT_act, 1)

            def norm_hi(i, chunks=range(KD)):
                for k in chunks:
                    if k % 2 == 0:
                        act.wait_ge(xT_ready, 4 * i + k // 2 + 1)
                    act.activation(n_hi[i][:, k, :], ps[4 + k // 2][:, (k % 2) * T:(k % 2 + 1) * T], ACT.Copy,
                                   scale=prm[:, G_NORM[i] + k:G_NORM[i] + k + 1]).then_inc(nhi_ready, 1)

            def norm_unsplit(i):
                for k in range(KD):
                    act.activation(hT[:, k, :], ps[4 + k // 2][:, (k % 2) * T:(k % 2 + 1) * T], ACT.Copy,
                                   scale=prm[:, G_NORM[i] + k:G_NORM[i] + k + 1]).then_inc(hTf_ready, 1)

            def hi(n):
                t, h = halves[n]
                wait_split_input(act, n)
                act.activation(l_w[:, n % SPLITS, 0, :], half_tile(slot(t), h), ACT.Copy).then_inc(lhi_ready, 1)

            def log_sigmoid_part(i, az, e, l):
                act.wait_ge(absz_ready, i + 1)
                act.activation(S(e), S(az), ACT.Exp).then_inc(act_chain, 1)
                act.wait_ge(act_chain, i + 1)
                act.activation(S(l), S(e), ACT.Ln, bias=1.0).then_inc(ln_ready, 1)

            norm_squares(0)
            act.wait_ge(prm_ready, 2)
            norm_hi(0, range(4))
            hi(0)
            norm_hi(0, range(4, KD))
            hi(1)
            for n in range(N_OUT0):
                hi(n + SPLITS - 1)
                if n == 0:
                    act.wait_ge(nlo_ready, KD)
                    norm_unsplit(0)
                if n in (1, 3):
                    act.wait_ge(glu_ready, n // 2 + 1)
                    act.activation(glu_sg[:, n - 1:n + 1, :].rearrange("p a t -> p (a t)"), ps[1 + n][:, :],
                                   ACT.Sigmoid).then_inc(sg_ready, 1)
                if n == 5:
                    log_sigmoid_part(0, 1, 2, 3)
                if 4 <= n < 8:
                    act.wait_ge(qk_ready, n - 3)
                    dst, c0 = (qT0, kT0)[n % 2], 2 * ((n - 4) // 2)
                    act.activation(dst[:, c0:c0 + 2, :].rearrange("p a t -> p (a t)"), ps[(5, 6, 7, 3)[n - 4]][:, :], ACT.Copy,
                                   scale=(DH ** -0.5, 1.0)[n % 2]).then_inc(qk_copied, 1)
            for t in range(TT):
                act.wait_ge(v_ready, t + 1)
                act.activation(v0[:, t, :], ps[1 + t][:, :], ACT.Copy).then_inc(v_copied, 1)
            hi(N_OUT0 + 2)
            def copy_turned(h):
                act.wait_ge(pT_ready, h + 1)
                if h >= 2:
                    act.wait_ge(pv_ready, h - 1)
                act.activation(probsT[:, h % 2, :], ps[6 + h % 2][:, 0:3 * P], ACT.Copy).then_inc(pT_copied, 1)

            for h in range(H):
                act.wait_ge(max_ready, h + 1)
                if h >= 2:
                    act.wait_ge(pT_ready, h - 1)
                b = (0, 5)[h % 2]
                act.activation(probs[:, h % 2, 0:P], ps[b][:, 0:P], ACT.Exp, bias=S3(5)[:, 0, h:h + 1],
                               accum_out=S3(6)[:, 0, h:h + 1]).then_inc(exp_ready, 1)
                act.activation(probs[:, h % 2, P:3 * P], ps[b][:, P:3 * P], ACT.Exp, bias=S3(5)[:, 1, h:h + 1],
                               accum_out=S3(6)[:, 1, h:h + 1]).then_inc(exp_ready, 1)
                if h >= 1:
                    copy_turned(h - 1)
                if h == 6:
                    act.wait_ge(lnc_ready, 1)
                    act.activation(lnsq, lnc, ACT.Square).then_inc(lnsq_ready, 1)
            copy_turned(H - 1)
            act.wait_ge(lnvar_ready, 1)
            act.activation(lnrstd, lnvar, ACT.Sqrt).then_inc(lnstd_ready, 1)
            for j in range(2):
                act.wait_ge(attT_ready, j + 1)
                act.activation(c_hi[:, 2 * j:2 * j + 2, :].rearrange("p a t -> p (a t)"), ps[5 + 2 * j][:, :],
                               ACT.Copy).then_inc(chi_ready, 1)
            act.wait_ge(ln_scaled, 1)
            for c in range(NC4):
                act.activation(convs[:, c, :], conv[:, c, :], ACT.Silu, scale=prm[:, C_CLNG + c:C_CLNG + c + 1],
                               bias=prm[:, C_CLNB + c:C_CLNB + c + 1]).then_inc(convT_ready, 1)
            act.wait_ge(convT_ready, NC4)
            act.activation(c_hi[:, NC4:KD, :], convs, ACT.Copy).then_inc(chi_ready, 1)
            for n in range(N_OUT0 + 3, N_PAIR + SPLITS - 1):
                hi(n)
            norm_squares(1)
            norm_hi(1)
            for n in range(N_PAIR, N_IN1):
                hi(n + SPLITS - 1)
                p = (n - N_PAIR) // 2
                if n < N_DOWN and n % 2 == 0:
                    act.wait_ge(gate_ready, p + 1)
                    if p >= 2:
                        act.wait_ge(hidf_ready, p - 1)
                    act.activation(dsg[:, p % 2, :], ps[(n - N_PAIR) % 4][:, :], ACT.Silu).then_inc(dsg_ready, 1)
                elif n < N_DOWN:
                    act.wait_ge(hidf_ready, p + 1)
                    act.activation(hid_hi[:, 2 * p:2 * p + 2, :].rearrange("p a t -> p (a t)"), hidf[:, p % 2, :],
                                   ACT.Copy).then_inc(hidhi_ready, 1)
            norm_squares(2)
            norm_hi(2)
            act.wait_ge(pads_ready, 2)
            for n in range(12):
                if n + SPLITS - 1 < 12:
                    hi(N_IN1 + n + SPLITS - 1)
                if n < 4:
                    act.wait_ge(u1_ready, n + 1)
                    act.activation(upad1[:, 2 * n:2 * n + 2, PAD1:PAD1 + T],
                                   ps[1 + n][:, :].rearrange("p (a b) -> p a b", a=2), ACT.Copy).then_inc(u1_copied, 1)
                if n == 0:
                    norm_unsplit(2)
                if n == 4:
                    log_sigmoid_part(1, 11, 12, 13)
                if n in (5, 7):
                    for m in (n - 5, n - 4):
                        act.wait_ge(v1_ready, m + 1)
                        half, t = m // 2, m % 2
                        act.activation(v_aug[:, t, 4 * half:4 * half + 4, 0:P],
                                       ps[(5, 6, 7, 1)[m]][:, :].rearrange("p (h d) -> p h d", h=4), ACT.Copy).then_inc(v1_copied, 1)
                if n == 8:
                    for c in range(KD):
                        act.wait_ge(conv1_tap, (TAPS1 - 1) * KD + c + 1)
                        act.activation(uT[:, c, :], uT[:, c, :], ACT.Silu,
                                       bias=prm[:, C_CB1 + c:C_CB1 + c + 1]).then_inc(uT_ready, 1)
                if n in (9, 11):
                    for m in (n - 9, n - 8):
                        act.wait_ge(o1_ready, m + 1)
                        half, t = m // 2, m % 2
                        act.activation(og[:, t, half * 512:half * 512 + 512], ps[2 + m][:, :], ACT.Sigmoid).then_inc(og_ready, 1)
            for h in range(H):
                act.wait_ge(qk1_ready, h + 1)
                b = (6, 7, 1, 2)[h % 4]
                act.activation(qT1[:, h, :], ps[b][:, 0:T], ACT.Copy).then_inc(qk1_copied, 1)
                act.activation(kT1[:, h, :], ps[b][:, T:2 * T], ACT.Copy, scale=P ** -0.5).then_inc(qk1_copied, 1)
            act.wait_ge(m_ready, 1)
            act.activation(S(21), S(20), ACT.Exp, scale=-1.0).then_inc(enm_ready, 1)

            for h in range(H + 2):
                if h < H:
                    act.wait_ge(ex_ready, h + 1)
                    if h >= 2:
                        act.wait_ge(w_ready, h - 1)
                    act.activation(dec[:, h % 2, 0:2 * P], ps[3 + h % 2][:, 0:2 * P], ACT.Exp,
                                   bias=S3(16)[:, 0, h:h + 1]).then_inc(act_chain, 1)
                    act.activation(dec[:, h % 2, 2 * P:3 * P], ps[3 + h % 2][:, 2 * P:3 * P], ACT.Exp,
                                   bias=S3(16)[:, 1, h:h + 1]).then_inc(dec_ready, 1)
                if h >= 2:
                    for t in range(TT):
                        act.wait_ge(hc_ready, TT * (h - 2) + t + 1)
                        cols = slice((h - 2) * P, (h - 1) * P)
                        act.activation(xn[:, t, cols], hc[:, t, cols], ACT.Square,
                                       accum_out=S3(31)[:, t, h - 2:h - 1]).then_inc(hsq_ready, 1)
                if h in (6, 8, 9):
                    p = (h - 5) // 2 if h < 9 else 2
                    act.wait_ge(hcT_ready, p + 1)
                    for k in (2 * p, 2 * p + 1):
                        act.activation(catT1[:, k, :], ps[(7, 0)[p % 2]][:, (k % 2) * T:(k % 2 + 1) * T], ACT.Copy,
                                       scale=prm[:, C_HN + k:C_HN + k + 1]).then_inc(hcT_act, 1)
            norm_squares(3)
            act.wait_ge(xn_ready, 8)
            act.dma_start(gfin[:, :], final_norm_g.partition_broadcast(P)).then_inc(gfin_in, 16)
            norm_gains(3)
            act.wait_ge(diff_ready, 1)
            act.activation(ss[:, 4, :], ss[:, 3, :], ACT.Exp).then_inc(e2_ready, 1)

            def hi_expert(pair, q, u):
                s, at = expert_tile(q, u // 2)
                if u % 2 == 0:
                    act.wait_ge(landed[s], pair * PER_PAIR + at)
                act.wait_ge(split_used, passed(pair, q, u + 1, 2 * NT))
                act.activation(w_hi[:, u % SPLITS, :], half_tile(s, u % 2), ACT.Copy).then_inc(hi_ready, 1)

            def gathered_gain(pair, q, ahead, b):
                act.wait_ge(disp_done, passed(pair, q, 2 * ahead + b + 1, 2))
                for k in range(4 * b, 4 * b + 4):
                    act.activation(xT[:, k, :], ps[5 + b][:, (k % 4) * CAP:(k % 4 + 1) * CAP], ACT.Copy,
                                   scale=prm[:, G_NORM[3] + k:G_NORM[3] + k + 1]).then_inc(xTe_ready, 1)

            def gathered_hi(pair, q, ahead, b):
                act.wait_ge(xTe_ready, passed(pair, q, KD * ahead + 4 * b + 4, KD))
                act.activation(x_hi[:, 4 * b:4 * b + 4, :], xT[:, 4 * b:4 * b + 4, :], ACT.Copy).then_inc(xhi_ready, 1)

            def expert(r, pair, q, e, final):
                for u in range(2 * NT):
                    if u + SPLITS - 1 < 2 * NT or not final:
                        hi_expert(pair, q, u + SPLITS - 1)
                    kind, g = order[u // 2]
                    if kind == 0 and u % 2:
                        act.wait_ge(g_done, passed(pair, q, g + 1, GROUPS))
                        if g > 0:
                            act.wait_ge(htok_ready, passed(pair, q, g, GROUPS))
                        act.activation(sil, ps[0][:, :], ACT.Silu).then_inc(sil_ready, 1)
                    if u % 2 == 0 and u >= 4 and order[u // 2 - 1][0] == 1:
                        gt = order[u // 2 - 1][1]
                        act.wait_ge(hidT_done, passed(pair, q, gt + 1, GROUPS))
                        act.activation(h_hi[:, gt % 2, :], ps[4][:, :], ACT.Copy).then_inc(hhi_ready, 1)
                    if u == U_COMB + 1:
                        act.wait_ge(y_done, passed_adds(r, pair, q, 4, 4))
                        act.wait_ge(combT_done, passed(pair, q, 1, 1))
                        act.activation(combT[0:CAP, :], ps[7][0:CAP, 0:T], ACT.Copy).then_inc(combT_ready, 1)
                    if u in (U_GATHER + 1, U_GATHER + 3) and not final:
                        gathered_gain(pair, q, 1, (u - U_GATHER) // 2)
                    if u in (U_NEXT + 1, U_NEXT + 3) and not final:
                        gathered_hi(pair, q, 1, (u - U_NEXT) // 2)
                act.wait_ge(ysum_done, passed(pair, q, 1, 1))
                act.activation(ye[0:CAP, 0:512], ps[2][0:CAP, :], ACT.Copy).then_inc(ye_left, 1)
                act.activation(ye[0:CAP, 512:1024], ps[3][0:CAP, :], ACT.Copy).then_inc(ye_right, 1)

            def one_round(r):
                first = 0 if r is None else r * (NE // 2)
                for u in range(SPLITS - 1):
                    hi_expert(first, 0, u)
                for b in range(2):
                    gathered_gain(first, 0, 0, b)
                    gathered_hi(first, 0, 0, b)
                all_experts(act, r, expert)

            all_rounds(act, one_round)
            norm_squares(4)

        @block.vector
        def _(dve):
            links = [0]

            def link(ins):
                links[0] += 1
                ins.then_inc(dve_chain, 1)
                dve.wait_ge(dve_chain, links[0])

            def bc(ap, n):
                return ap.unsqueeze(2).broadcast_to([ap.shape[0], ap.shape[1], n])

            def both(ap):
                return ap.unsqueeze(1).broadcast_to([ap.shape[0], TT, ap.shape[1]])

            def norm_scale(i, tiles=range(TT)):
                for t in tiles:
                    dve.wait_ge(sq_done, TT * i + t + 1)
                    dve.tensor_scalar(ss[:, 1, t:t + 1], ss[:, 0, t:t + 1], 1.0 / D, EPS, ALU.mult, ALU.add).then_inc(var_ready, 1)
                    dve.wait_ge(rstd_ready, TT * i + t + 1)
                    if i < 4:
                        dve.tensor_scalar(xn[:, t, :], xres[:, t, :], ss[:, 2, t:t + 1], None, ALU.mult).then_inc(xn_ready, 1)
                    else:
                        dve.scalar_tensor_tensor(out=xn[:, t, :], in0=xres[:, t, :], scalar=ss[:, 2, t:t + 1], in1=gfin[:, :],
                                                 op0=ALU.mult, op1=ALU.mult).then_inc(fin_ready, 1)

            def norm_gains(i):
                for b in (1, 3):
                    dve.wait_ge(xT_ready, 4 * i + b + 1)
                    for k in (2 * b, 2 * b + 1):
                        dve.tensor_scalar(hT[:, k, :], ps[4 + b][:, (k % 2) * T:(k % 2 + 1) * T],
                                          prm[:, G_NORM[i] + k:G_NORM[i] + k + 1], None, ALU.mult).then_inc(hT_dve, 1)

            def norm_lo(i, chunks=range(KD)):
                for k in chunks:
                    if k % 2 == 0:
                        dve.wait_ge(nhi_ready, KD * i + k + 2)
                    dve.scalar_tensor_tensor(out=n_lo[:, k, :], in0=ps[4 + k // 2][:, (k % 2) * T:(k % 2 + 1) * T],
                                             scalar=prm[:, G_NORM[i] + k:G_NORM[i] + k + 1],
                                             in1=n_hi[i][:, k, :].bitcast(F32), op0=ALU.mult, op1=ALU.subtract).then_inc(nlo_ready, 1)

            def lo(n):
                t, h = halves[n]
                dve.wait_ge(lhi_ready, n + 1)
                dve.tensor_tensor(l_w[:, n % SPLITS, 1, :], half_tile(slot(t), h), l_w[:, n % SPLITS, 0, :].bitcast(F32),
                                  ALU.subtract).then_inc(llo_ready, 1)

            def add_residual(stage, banks, part=range(4)):
                for n in part:
                    dve.wait_ge(proj_ready, 4 * stage + n + 1)
                    half, t = n // 2, n % 2
                    v = xres[:, t, half * 512:(half + 1) * 512]
                    dve.tensor_tensor(v, v, ps[banks[n]][:, :], ALU.add).then_inc(res_added, 1)

            def neg_abs(i, z, az):
                dve.scalar_tensor_tensor(out=S(az), in0=S(z), scalar=-1.0, in1=S(z), op0=ALU.mult,
                                         op1=ALU.min).then_inc(absz_ready, 1)

            def log_f(i, z, l, lf):
                dve.wait_ge(ln_ready, i + 1)
                dve.scalar_tensor_tensor(out=S(lf), in0=S(z), scalar=0.0, in1=S(l), op0=ALU.min,
                                         op1=ALU.subtract).then_inc(logf_ready, 1)

            norm_scale(0)
            dve.tensor_copy(cur[:, 1, :], ss[:, 2, :]).then_inc(lo_ready, 2 * RING)
            dve.wait_ge(prm_T, 1)
            dve.tensor_copy(prm[:, 0:N_ROWS1], ps[7][:, 0:N_ROWS1]).then_inc(prm_ready, 1)
            dve.tensor_copy(dww[:, 0:N_ROWS2], ps[7][:, P:P + N_ROWS2]).then_inc(prm_ready, 1)
            dve.wait_ge(prm_ready, 2)
            norm_lo(0, range(4))
            lo(0)
            norm_lo(0, range(4, KD))
            lo(1)

            def glu(p):
                if p == 0:
                    dve.wait_ge(pool_chain, 11)
                dve.wait_ge(sg_ready, p + 1)
                dve.tensor_tensor(upad[:, 2 * p:2 * p + 2, PAD0:PAD0 + T], ps[1 + 2 * p][:, :].rearrange("p (a t) -> p a t", a=2),
                                  glu_sg[:, 2 * p:2 * p + 2, :], ALU.mult).then_inc(u_ready, 1)

            def conv_taps(first, last):
                for n in range(first, last):
                    pair, j, c = n // (2 * TAPS), n // 2 % TAPS, n % 2 + 2 * (n // (2 * TAPS))
                    w = dww[:, j * NC4 + c:j * NC4 + c + 1]
                    if n % (2 * TAPS) == 0:
                        dve.wait_ge(u_ready, pair + 1)
                    if j == 0:
                        dve.tensor_scalar(conv[:, c, :], upad[:, c, 0:T], w, prm[:, C_DWB + c:C_DWB + c + 1],
                                          ALU.mult, ALU.add).then_inc(conv_tap, 1)
                    else:
                        dve.wait_ge(conv_tap, n - 1)
                        dve.scalar_tensor_tensor(out=conv[:, c, :], in0=upad[:, c, j:j + T], scalar=w,
                                                 in1=conv[:, c, :], op0=ALU.mult, op1=ALU.add).then_inc(conv_tap, 1)

            ATT_HEADS, LATE = 6, 10
            EARLY = NC4 * TAPS - ATT_HEADS * LATE
            for n in range(N_OUT0):
                lo(n + SPLITS - 1)
                if n == 2:
                    dve.wait_ge(gateT_ready, 1)
                    dve.tensor_copy(gateT[0:H, :], ps[0][0:H, 128:128 + T]).then_inc(gateT_copied, 1)
                if n == 4:
                    dve.wait_ge(small_in, 16 * 6)
                    dve.wait_ge(gate_pre, 1)
                    link(dve.tensor_tensor(S3(0), ps[0][:, 0:TT * H].rearrange("p (t h) -> p t h", t=TT), both(bf0[:, :]), ALU.add))
                    neg_abs(0, 0, 1)
                if n in (1, 3):
                    glu(n // 2)
                if n == 5:
                    dve.wait_ge(u_ready, 2)
                    log_f(0, 0, 3, 4)
                if n == 7:
                    dve.wait_ge(cum_ready, 1)
                    dve.tensor_copy(S(7), ps[0][:, 16:16 + TT * H]).then_inc(cum_copied, 1)
                if n == 8:
                    dve.wait_ge(cumT_ready, 1)
                    dve.tensor_copy(cT[:, :], ps[0][0:H, 64:64 + T]).then_inc(cT_ready, 1)
                if n >= 1:
                    conv_taps(EARLY * (n - 1) // 9, EARLY * n // 9)
            lo(N_OUT0 + 2)

            def fox_max(h):
                dve.wait_ge(scores_ready, h + 1)
                b = (0, 5)[h % 2]
                dve.tensor_reduce(S3(5)[:, 0, h:h + 1], ps[b][:, 0:P], AX_X, ALU.max, negate=True).then_inc(dve_chain, 1)
                dve.tensor_reduce(S3(5)[:, 1, h:h + 1], ps[b][:, P:3 * P], AX_X, ALU.max, negate=True).then_inc(max_ready, 1)
                links[0] += 1

            for h in range(H):
                fox_max(h)
                if h < ATT_HEADS:
                    conv_taps(EARLY + h * LATE, EARLY + (h + 1) * LATE)
                if h == 6:
                    dve.wait_ge(conv_tap, NC4 * TAPS)
                    dve.wait_ge(ln_mean, 1)
                    dve.tensor_tensor(lnc, conv, ps[3][:, 0:T].unsqueeze(1).broadcast_to([P, NC4, T]),
                                      ALU.subtract).then_inc(lnc_ready, 1)
                if h == H - 1:
                    dve.wait_ge(ln_var, 1)
                    dve.tensor_scalar(lnvar, ps[4][:, 0:T], EPS, None, ALU.add).then_inc(lnvar_ready, 1)
            dve.wait_ge(exp_ready, 2 * H)
            link(dve.reciprocal(S(8), S(6)))
            dve.wait_ge(pv_ready, H)
            for t in range(TT):
                dve.tensor_tensor(att[:, t, :].rearrange("p (h d) -> p h d", h=H),
                                  ps[1 + t][:, :].rearrange("p (h d) -> p h d", h=H), bc(S3(8)[:, t, :], DH),
                                  ALU.mult).then_inc(att_ready, 1)
            dve.wait_ge(lnstd_ready, 1)
            link(dve.reciprocal(lnvar, lnrstd))
            dve.tensor_tensor(conv, lnc, lnvar.unsqueeze(1).broadcast_to([P, NC4, T]), ALU.mult).then_inc(ln_scaled, 1)
            for j in range(2):
                dve.wait_ge(chi_ready, j + 1)
                v = slice(2 * j, 2 * j + 2)
                dve.tensor_tensor(c_lo[:, v, :].rearrange("p a t -> p (a t)"), ps[5 + 2 * j][:, :],
                                  c_hi[:, v, :].bitcast(F32).rearrange("p a t -> p (a t)"), ALU.subtract).then_inc(clo_ready, 1)
            dve.wait_ge(chi_ready, 3)
            dve.tensor_tensor(c_lo[:, NC4:KD, :], convs, c_hi[:, NC4:KD, :].bitcast(F32), ALU.subtract).then_inc(clo_ready, 1)
            lo(N_OUT0 + 3)
            lo(N_PAIR)
            add_residual(0, (0, 3, 1, 2), range(2))
            lo(N_PAIR + 1)
            add_residual(0, (0, 3, 1, 2), range(2, 4))
            norm_scale(1)
            norm_lo(1)
            for n in range(N_PAIR, N_IN1):
                lo(n + SPLITS - 1)
                p = (n - N_PAIR) // 2
                if n < N_DOWN and n % 2:
                    dve.wait_ge(up_ready, p + 1)
                    dve.wait_ge(dsg_ready, p + 1)
                    if p >= 2:
                        dve.wait_ge(hidlo_ready, p - 1)
                    dve.tensor_tensor(hidf[:, p % 2, :], ps[(n - N_PAIR) % 4][:, :], dsg[:, p % 2, :], ALU.mult).then_inc(hidf_ready, 1)
                elif N_PAIR < n <= N_DOWN:
                    dve.wait_ge(hidhi_ready, p)
                    v = slice(2 * p - 2, 2 * p)
                    dve.tensor_tensor(hid_lo[:, v, :].rearrange("p a t -> p (a t)"), hidf[:, (p - 1) % 2, :],
                                      hid_hi[:, v, :].bitcast(F32).rearrange("p a t -> p (a t)"), ALU.subtract).then_inc(hidlo_ready, 1)
            add_residual(1, (4, 5, 6, 7))
            norm_scale(2)
            norm_lo(2)

            def conv1_taps(first, last):
                for n in range(first, last):
                    j, c = n // KD, n % KD
                    w = prm[:, C_CW1 + n:C_CW1 + n + 1]
                    if j == 0:
                        dve.tensor_scalar(uT[:, c, :], upad1[:, c, 0:T], w, None, ALU.mult).then_inc(conv1_tap, 1)
                    else:
                        dve.wait_ge(conv1_tap, KD * (j - 1) + c + 1)
                        dve.scalar_tensor_tensor(out=uT[:, c, :], in0=upad1[:, c, j:j + T], scalar=w,
                                                 in1=uT[:, c, :], op0=ALU.mult, op1=ALU.add).then_inc(conv1_tap, 1)

            for n in range(12):
                if n + SPLITS - 1 < 12:
                    lo(N_IN1 + n + SPLITS - 1)
                if n == 1:
                    dve.wait_ge(gateT_ready, 2)
                    dve.tensor_copy(gateT[:, :], ps[0][0:2 * H, 128:128 + T]).then_inc(gateT_copied, 1)
                if n == 3:
                    dve.wait_ge(gate_pre, 2)
                    gates = ps[0][:, 0:2 * TT * H].rearrange("p (t g) -> p t g", t=TT)
                    link(dve.tensor_tensor(S3(9), gates[:, :, 0:H], both(bif1[:, 0:H]), ALU.add))
                    link(dve.tensor_tensor(S3(10), gates[:, :, H:2 * H], both(bif1[:, H:2 * H]), ALU.add))
                    neg_abs(1, 10, 11)
                    for c in range(KD // 2):
                        dve.wait_ge(u1_copied, c + 1)
                if 4 <= n < 8:
                    conv1_taps(KD * TAPS1 * (n - 4) // 4, KD * TAPS1 * (n - 3) // 4)
                if n == 5:
                    log_f(1, 10, 13, 14)
            dve.wait_ge(cum_ready, 2)
            link(dve.tensor_copy(S(15), ps[0][:, 64:64 + TT * H]))
            dve.tensor_tensor(S(16), S(9), S(15), ALU.subtract).then_inc(cum_copied, 1)
            dve.wait_ge(cumT_ready, 2)
            link(dve.tensor_copy(aT[:, :], ps[0][0:H, 128:128 + T]))
            dve.tensor_tensor_scan(GT[:, :], aT[:, :], aT[:, :], 0.0, ALU.max, ALU.max).then_inc(gT_ready, 1)
            dve.wait_ge(gt_back, 1)
            dve.tensor_tensor(S(20), S(15), ps[0][:, 400:400 + TT * H], ALU.add).then_inc(m_ready, 1)
            dve.wait_ge(enm_ready, 1)
            dve.wait_ge(og_ready, 4)
            for i in range(H + 3):
                if i < H:
                    dve.wait_ge(dec_ready, i + 1)
                    if i >= 2:
                        dve.wait_ge(num_ready, i - 1)
                    dve.tensor_tensor(wts[:, i % 2, :], ps[1 + i % 2][:, 0:3 * P], dec[:, i % 2, :], ALU.mult).then_inc(w_ready, 1)
                if 1 <= i <= H:
                    h = i - 1
                    dve.wait_ge(num_ready, h + 1)
                    o = ps[5 + h % 2][:, :].rearrange("p (t d) -> p t d", t=TT)
                    nq = o[:, :, P]
                    link(dve.tensor_copy(S3(22)[:, :, h], nq))
                    link(dve.scalar_tensor_tensor(out=S3(23)[:, :, h], in0=S3(22)[:, :, h], scalar=-1.0, in1=S3(22)[:, :, h],
                                                  op0=ALU.mult, op1=ALU.max))
                    link(dve.tensor_tensor(S3(24)[:, :, h], S3(23)[:, :, h], S3(21)[:, :, h], ALU.max))
                    link(dve.reciprocal(S3(25)[:, :, h], S3(24)[:, :, h]))
                    for t in range(TT):
                        cols = slice(h * P, (h + 1) * P)
                        dve.scalar_tensor_tensor(out=hc[:, t, cols], in0=o[:, t, 0:P], scalar=S3(25)[:, t, h:h + 1],
                                                 in1=og[:, t, cols], op0=ALU.mult, op1=ALU.mult).then_inc(hc_ready, 1)
                if 2 <= i < H + 2:
                    h = i - 2
                    dve.wait_ge(hsq_ready, TT * h + TT)
                    dve.tensor_scalar(S3(32)[:, :, h], S3(31)[:, :, h], 1.0 / P, EPS, ALU.mult, ALU.add).then_inc(hvar_ready, 1)
                if i >= 3:
                    h = i - 3
                    dve.wait_ge(hrstd_ready, h + 1)
                    for t in range(TT):
                        v = hc[:, t, h * P:(h + 1) * P]
                        dve.tensor_scalar(v, v, S3(33)[:, t, h:h + 1], None, ALU.mult).then_inc(hn_ready, 1)
            dve.wait_ge(hcT_ready, 4)
            for k in (6, 7):
                dve.tensor_scalar(catT1[:, k, :], ps[0][:, (k % 2) * T:(k % 2 + 1) * T],
                                  prm[:, C_HN + k:C_HN + k + 1], None, ALU.mult).then_inc(hcT_dve, 1)
            add_residual(2, (3, 1, 2, 0), range(3))
            norm_scale(3, (0,))
            add_residual(2, (3, 1, 2, 0), (3,))
            norm_scale(3, (1,))
            norm_gains(3)
            dve.wait_ge(gateT_ready, 3)
            dve.tensor_copy(gateT[0:NE, :], ps[0][0:NE, 128:128 + T]).then_inc(gateT_copied, 1)
            dve.wait_ge(gate_pre, 3)
            L, p1, oh1, l2, p2, oh2, t1, t2 = 0, 1, 2, 3, 4, 5, 6, 7
            link(dve.tensor_copy(S(L), ps[0][:, 0:TT * NE]))

            def first_max(l, p, oh, top):
                link(dve.tensor_reduce(top, S3(l), AX_X, ALU.max))
                link(dve.tensor_tensor(S3(p), S3(l), bc(top, NE), ALU.is_equal))
                link(dve.tensor_tensor(S3(p), S3(p), pick_order[:, :, :], ALU.mult))
                link(dve.tensor_reduce(ss[:, 7, :], S3(p), AX_X, ALU.max))
                link(dve.tensor_tensor(S3(oh), S3(p), bc(ss[:, 7, :], NE), ALU.is_equal))

            first_max(L, p1, oh1, ss[:, 5, :])
            link(dve.scalar_tensor_tensor(out=S(l2), in0=S(oh1), scalar=NEG, in1=S(L), op0=ALU.mult, op1=ALU.add))
            first_max(l2, p2, oh2, ss[:, 6, :])
            dve.tensor_tensor(S(8), S(oh1), S(oh2), ALU.add).then_inc(mask_ready, 1)
            dve.tensor_tensor(ss[:, 3, :], ss[:, 6, :], ss[:, 5, :], ALU.subtract).then_inc(diff_ready, 1)
            dve.wait_ge(e2_ready, 1)
            link(dve.tensor_scalar(ss[:, 5, :], ss[:, 4, :], 1.0, None, ALU.add))
            link(dve.reciprocal(ss[:, 6, :], ss[:, 5, :]))
            link(dve.tensor_tensor(ss[:, 7, :], ss[:, 4, :], ss[:, 6, :], ALU.mult))
            link(dve.tensor_tensor(S3(t1), S3(oh1), bc(ss[:, 6, :], NE), ALU.mult))
            link(dve.tensor_tensor(S3(t2), S3(oh2), bc(ss[:, 7, :], NE), ALU.mult))
            link(dve.tensor_tensor(S(9), S(t1), S(t2), ALU.add))
            dve.wait_ge(pos_ready, 1)
            link(dve.tensor_tensor(S(10), ps[0][:, 64:64 + TT * NE], S(8), ALU.mult))
            link(dve.tensor_scalar(S(11), S(10), -1.0, None, ALU.add))

            def lo_expert(pair, q, u):
                s, _ = expert_tile(q, u // 2)
                dve.wait_ge(hi_ready, passed(pair, q, u + 1, 2 * NT))
                dve.tensor_tensor(w_lo[:, u % SPLITS, :], half_tile(s, u % 2), w_hi[:, u % SPLITS, :].bitcast(F32),
                                  ALU.subtract).then_inc(lo_ready, 1)

            def route_columns(pair, q, e):
                dve.tensor_copy(cur[:, 0, :].unsqueeze(2), S3(11)[:, :, bass.ds(e, 1)]).then_inc(cur_ready, 1)
                dve.tensor_copy(cur[:, 1, :].unsqueeze(2), S3(9)[:, :, bass.ds(e, 1)]).then_inc(cur_ready, 1)

            def route_slots(pair, q, ahead):
                dve.wait_ge(cur_ready, passed(pair, q, 2 * ahead + 2, 2))
                for t in range(TT):
                    dve.tensor_scalar(disp[:, t, :], slot_no[:, :], cur[:, 0, t:t + 1], None,
                                      ALU.is_equal).then_inc(route_ready, 1)

            def route_gates(pair, q, ahead):
                if ahead:
                    dve.wait_ge(combT_done, passed(pair, q, 1, 1))
                for t in range(TT):
                    dve.tensor_scalar(comb[:, t, :], slot_no[:, :], cur[:, 0, t:t + 1], cur[:, 1, t:t + 1],
                                      ALU.is_equal, ALU.mult).then_inc(route_ready, 1)

            def gathered_lo(pair, q, ahead, b):
                dve.wait_ge(xhi_ready, passed(pair, q, 2 * ahead + b + 1, 2))
                v = slice(4 * b, 4 * b + 4)
                dve.tensor_tensor(x_lo[:, v, :], xT[:, v, :], x_hi[:, v, :].bitcast(F32), ALU.subtract).then_inc(xlo_ready, 1)

            def add_rows(r, pair, q, ahead, t):
                for n in (2 * t, 2 * t + 1):
                    dve.wait_ge(y_done, passed_adds(r, pair, q, 4 * ahead + n + 1, 4))
                    t, half = n // 2, n % 2
                    v = xres[:, t, half * 512:(half + 1) * 512]
                    dve.tensor_tensor(v, v, ps[(5, 6, 7, 5)[n]][:, :], ALU.add).then_inc(y_added, 1)

            def expert(r, pair, q, e, final):
                for u in range(2 * NT):
                    if u + SPLITS - 1 < 2 * NT or not final:
                        lo_expert(pair, q, u + SPLITS - 1)
                    kind, g = order[u // 2]
                    if kind == 1 and u % 2:
                        dve.wait_ge(u_done, passed(pair, q, g + 1, GROUPS))
                        dve.wait_ge(sil_ready, passed(pair, q, g + 1, GROUPS))
                        dve.tensor_tensor(htok, ps[1][:, :], sil, ALU.mult).then_inc(htok_ready, 1)
                    if u % 2 == 0 and u >= 4 and order[u // 2 - 1][0] == 1:
                        gt = order[u // 2 - 1][1]
                        dve.wait_ge(hhi_ready, passed(pair, q, gt + 1, GROUPS))
                        dve.tensor_tensor(h_lo[:, gt % 2, :], ps[4][:, :], h_hi[:, gt % 2, :].bitcast(F32),
                                          ALU.subtract).then_inc(hlo_ready, 1)
                    if u in (U_ADD, U_ADD + 2):
                        add_rows(r, pair, q, 0, u // 2)
                    if not final:
                        if u == U_ROUTE:
                            route_columns(pair, q, e + 1)
                        if u == U_ROUTE + 2:
                            route_slots(pair, q, 1)
                        if u == U_ROUTE + 8:
                            route_gates(pair, q, 1)
                        if u in (U_NEXT + 2, U_NEXT + 4):
                            gathered_lo(pair, q, 1, (u - U_NEXT) // 2 - 1)

            def one_round(r):
                first = 0 if r is None else r * (NE // 2)
                if r is not None:
                    dve.wait_ge(cur_ready, r * (2 * NE))
                    dve.tensor_scalar(S(11), S(11), -float(CAP), None, ALU.add).then_inc(round_ready, 1)
                    dve.wait_ge(round_ready, r)
                dve.memset(ye[:, :], 0.0).then_inc(ye_left, 1)
                dve.memset(combT[:, 0:P], 0.0).then_inc(ye_right, 1)
                dve.memset(combT[:, P:T], 0.0).then_inc(combT_ready, 1)
                route_columns(first, 0, 0)
                route_slots(first, 0, 0)
                route_gates(first, 0, 0)
                if r is None:
                    link(dve.tensor_reduce(ss[:, 3, 0:1], ps[0][:, 96:96 + NE], AX_X, ALU.max))
                    dve.tensor_copy(flag[:, 0:1], ss[:, 3, 0:1]).then_inc(flag_ready, 1)
                for u in range(SPLITS - 1):
                    lo_expert(first, 0, u)
                for b in range(2):
                    gathered_lo(first, 0, 0, b)
                all_experts(dve, r, expert)
                for t in range(TT):
                    add_rows(r, first + (NE // 2 - 1), 1, 1, t)
                dve.wait_ge(y_added, 4 * (NE + 1) if r is None else r * (4 * (NE + 1)) + 4 * (NE + 1))

            dve.wait_ge(dve_chain, links[0])
            all_rounds(dve, one_round)
            dve.tensor_copy(flag[:, 1:2], flag[:, 0:1]).then_inc(moe_done, 1)
            dve.wait_ge(gfin_in, 16)
            norm_scale(4)

        @block.tensor
        def _(pe):
            def arrived(t):
                pe.wait_ge(landed[slot(t)], landed_at[t])

            def turn(src, ready, i, done, frees=False):
                for t in range(TT):
                    pe.wait_ge(ready, 2 * i + t + 1)
                    for k in range(KD):
                        last = pe.transpose(ps[4 + k // 2][:, (k % 2) * T + t * P:(k % 2) * T + (t + 1) * P],
                                            src[:, t, k * P:(k + 1) * P], ident[:, :])
                        if frees and k == 0 and t == 0:
                            last.then_inc(tiles_used, 1)
                        if t == TT - 1 and k % 2:
                            last.then_inc(done, 1)

            def hT_wait(i):
                pe.wait_ge(hT_act, 4 * i + 4)
                pe.wait_ge(hT_dve, 4 * i + 4)

            def small_feature_major(w, n):
                for k in range(KD):
                    last = pe.matmul(ps[0][0:n, 128:128 + T], w[:, k, :], hT[:, k, :], start=(k == 0), stop=(k == KD - 1))
                last.then_inc(gateT_ready, 1)

            def turn_gates(i, n):
                pe.wait_ge(gateT_copied, i + 1)
                for t in range(TT):
                    last = pe.transpose(ps[0][:, t * n:(t + 1) * n], gateT[0:n, t * P:(t + 1) * P], ident[0:n, 0:n])
                last.then_inc(gate_pre, 1)

            def cumulate(o, src):
                pe.matmul(o[:, 0:H], upper[:, :], src[:, 0, :], start=True, stop=True)
                pe.matmul(o[:, H:2 * H], ones[:, :], src[:, 0, :], start=True, stop=False)
                return pe.matmul(o[:, H:2 * H], upper[:, :], src[:, 1, :], start=False, stop=True)

            def turn_heads(p):
                pe.wait_ge(hn_ready, 2 * TT * (p + 1))
                if p >= 2:
                    pe.wait_ge(hcT_act, 2 * (p - 1))
                for k in (2 * p, 2 * p + 1):
                    for t in range(TT):
                        last = pe.transpose(ps[(7, 0)[p % 2]][:, (k % 2) * T + t * P:(k % 2) * T + (t + 1) * P],
                                            hc[:, t, k * P:(k + 1) * P], ident[:, :])
                last.then_inc(hcT_ready, 1)

            def out_proj(t0, src, banks):
                for n in range(4):
                    half, t = n // 2, n % 2
                    if t == 0:
                        arrived(t0 + half)
                    w = tile(t0 + half, KD, TILE)
                    for k in range(KD):
                        if n == 0 and k == 0:
                            turn_heads(2)
                            pe.wait_ge(hcT_act, 6)
                        if n == 0 and k == 6:
                            turn_heads(3)
                            pe.wait_ge(hcT_dve, 2)
                        last = pe.matmul(ps[banks[n]][:, :], src[:, k, t * P:(t + 1) * P], w[:, k, :], start=(k == 0), stop=(k == KD - 1))
                        if k == 0 and n == 2:
                            last.then_inc(tiles_used, 1)
                    last.then_inc(proj_ready, 1)

            def three(o, aw, start, stop):
                (a, b) = aw
                first = pe.matmul(o, a[0], b[0], start=start, stop=False)
                pe.matmul(o, a[0], b[1], start=False, stop=False)
                return first, pe.matmul(o, a[1], b[0], start=False, stop=stop)

            def norm_chunk(i, k):
                pe.wait_ge(nlo_ready, KD * i + k + 1)

            def half_feature(n, o, i, first_of_norm=False):
                w = [l_w[:, n % SPLITS, part, :].rearrange("p (k n) -> p k n", k=KD) for part in range(2)]
                pe.wait_ge(llo_ready, n + 1)
                for c in range(2):
                    for k in range(KD):
                        if first_of_norm and c == 0:
                            norm_chunk(i, k)
                        cols = slice(c * P, (c + 1) * P)
                        first, last = three(o[:, c * T:(c + 1) * T], ([v[:, k, cols] for v in w], [n_hi[i][:, k, :], n_lo[:, k, :]]),
                                            k == 0, k == KD - 1)
                        if n > 0 and c == 0 and k == 0:
                            first.then_inc(lsplit_used, 1)
                return last

            def half_tokens(n, banks, a, ready, frees=True):
                w = [l_w[:, n % SPLITS, part, :].rearrange("p (k n) -> p k n", k=KD // 2) for part in range(2)]
                pe.wait_ge(llo_ready, n + 1)
                h = halves[n][1]
                opens = halves[n][0] not in [t for t, _ in halves[:n]]
                for t in range(TT):
                    for kk in range(KD // 2):
                        k = h * (KD // 2) + kk
                        first, last = three(ps[banks[t]][:, :], ([v[:, k, t * P:(t + 1) * P] for v in a],
                                                                 [v[:, kk, :] for v in w]), opens and kk == 0, not opens and kk == KD // 2 - 1)
                        if frees and t == 0 and kk == 0:
                            first.then_inc(lsplit_used, 1)
                    if not opens:
                        last.then_inc(ready, 1)

            pe.wait_ge(ident_ready, 1)
            pe.wait_ge(params_in, 16 * 11)
            pe.transpose(ps[7][:, 0:N_ROWS1], rows1[0:N_ROWS1, :], ident[0:N_ROWS1, 0:N_ROWS1])
            pe.transpose(ps[7][:, P:P + N_ROWS2], rows2[0:N_ROWS2, :], ident[0:N_ROWS2, 0:N_ROWS2]).then_inc(prm_T, 1)
            pe.wait_ge(prm_ready, 2)
            turn(xn, xn_ready, 0, xT_ready)
            for n in range(4):
                last = half_feature(n, ps[1 + n], 0, n == 0)
                if n % 2:
                    last.then_inc(glu_ready, 1)
                if n == 1:
                    pe.wait_ge(small_in, 16 * 6)
                    pe.wait_ge(hTf_ready, KD)
                    small_feature_major(wf, H)
            for n in range(4, 8):
                if n == 7:
                    pe.wait_ge(u_ready, 2)
                half_feature(n, ps[(5, 6, 7, 3)[n - 4]], 0).then_inc(qk_ready, 1)
                if n == 4:
                    turn_gates(0, H)
                if n == 6:
                    pe.wait_ge(const_ready, 4)
                    pe.wait_ge(pool_chain, 11)
                    pe.wait_ge(logf_ready, 1)
                    cumulate(ps[0][:, 16:16 + 2 * H], S3(4)).then_inc(cum_ready, 1)
            half_tokens(8, (1, 2), (n_hi[0], n_lo), v_ready)
            pe.wait_ge(cum_copied, 1)
            pe.transpose(ps[0][0:H, 64:64 + P], S3(7)[:, 0, :], ident[:, :])
            pe.transpose(ps[0][0:H, 64 + P:64 + T], S3(7)[:, 1, :], ident[:, :]).then_inc(cumT_ready, 1)
            half_tokens(9, (1, 2), (n_hi[0], n_lo), v_ready)
            def scores(h):
                lo, c, b = DH * (h % 2), h // 2, (0, 5)[h % 2]
                if h >= 2:
                    pe.wait_ge(exp_ready, 2 * (h - 1))
                for t, o in ((0, ps[b][:, 0:P]), (1, ps[b][:, P:3 * P])):
                    n = (t + 1) * P
                    last = pe.matmul(o, qT0[lo:lo + DH, c, t * P:(t + 1) * P], kT0[lo:lo + DH, c, 0:n], start=True, stop=False)
                    if h == 0 and t == 0:
                        last.then_inc(lsplit_used, 1)
                    pe.matmul(o, neg_sel[:, h, :], cT[:, 0:n], start=False, stop=False)
                    last = pe.matmul(o[:, n - P:n], ident[:, :], mask_qk[:, :], start=False, stop=True)
                last.then_inc(scores_ready, 1)

            def turn_probs(h):
                pe.wait_ge(exp_ready, 2 * h + 2)
                if h >= 2:
                    pe.wait_ge(pT_copied, h - 1)
                for j in range(3):
                    last = pe.transpose(ps[6 + h % 2][:, j * P:(j + 1) * P], probs[:, h % 2, j * P:(j + 1) * P], ident[:, :])
                last.then_inc(pT_ready, 1)

            def values(h):
                pe.wait_ge(pT_copied, h + 1)
                cols = slice(h * DH, (h + 1) * DH)
                pe.matmul(ps[1][:, cols], probsT[:, h % 2, 0:P], v0[:, 0, cols], start=True, stop=True)
                pe.matmul(ps[2][:, cols], probsT[:, h % 2, P:2 * P], v0[:, 0, cols], start=True, stop=False)
                pe.matmul(ps[2][:, cols], probsT[:, h % 2, 2 * P:3 * P], v0[:, 1, cols], start=False,
                          stop=True).then_inc(pv_ready, 1)

            pe.wait_ge(cT_ready, 1)
            pe.wait_ge(qk_copied, 4)
            pe.wait_ge(v_copied, TT)
            for i in range(H + 2):
                if i < H:
                    scores(i)
                if i == 6:
                    pe.wait_ge(conv_tap, NC4 * TAPS)
                    for c in range(NC4):
                        last = pe.matmul(ps[3][:, 0:T], ch_mean[:, :], conv[:, c, :], start=(c == 0), stop=(c == NC4 - 1))
                    last.then_inc(ln_mean, 1)
                if i == 8:
                    pe.wait_ge(lnsq_ready, 1)
                    for c in range(NC4):
                        last = pe.matmul(ps[4][:, 0:T], ch_mean[:, :], lnsq[:, c, :], start=(c == 0), stop=(c == NC4 - 1))
                    last.then_inc(ln_var, 1)
                if 1 <= i <= H:
                    turn_probs(i - 1)
                if i >= 2:
                    values(i - 2)
            pe.wait_ge(att_ready, TT)
            for j in range(FW // P):
                for t in range(TT):
                    last = pe.transpose(ps[5 + 2 * (j // 2)][:, (j % 2) * T + t * P:(j % 2) * T + (t + 1) * P],
                                        att[:, t, j * P:(j + 1) * P], ident[:, :])
                if j % 2:
                    last.then_inc(attT_ready, 1)
            c_split = (c_hi, c_lo)
            pe.wait_ge(clo_ready, 2)
            half_tokens(N_OUT0, (0, 3), c_split, proj_ready, frees=False)
            half_tokens(N_OUT0 + 1, (1, 2), c_split, proj_ready)
            pe.wait_ge(clo_ready, 3)
            half_tokens(N_OUT0 + 2, (0, 3), c_split, proj_ready)
            half_tokens(N_OUT0 + 3, (1, 2), c_split, proj_ready)
            turn(xn, xn_ready, 1, xT_ready)
            for n in range(N_PAIR, N_DOWN):
                m = n - N_PAIR
                if m >= 4:
                    pe.wait_ge((dsg_ready, hidf_ready)[m % 2], m // 2 - 1)
                half_feature(n, ps[m % 4], 1, m == 0).then_inc((gate_ready, up_ready)[m % 2], 1)
            for n in range(N_DOWN, N_IN1):
                pe.wait_ge(hidlo_ready, n - N_DOWN + 1)
                pe.wait_ge(llo_ready, n + 1)
                w = [l_w[:, n % SPLITS, part, :].rearrange("p (k n) -> p k n", k=2) for part in range(2)]
                for m in range(4):
                    half, t = m // 2, m % 2
                    for kk in range(2):
                        f = 2 * (n - N_DOWN) + kk
                        cols = slice(half * 512, (half + 1) * 512)
                        first, last = three(ps[4 + m][:, :], ([v[:, f, t * P:(t + 1) * P] for v in (hid_hi, hid_lo)],
                                                              [v[:, kk, cols] for v in w]), f == 0, f == NF - 1)
                        if m == 0 and kk == 0:
                            first.then_inc(lsplit_used, 1)
                    if n == N_IN1 - 1:
                        last.then_inc(proj_ready, 1)
            turn(xn, xn_ready, 2, xT_ready)
            for c in range(KD // 2):
                half_feature(N_IN1 + c, ps[1 + c], 2, c == 0).then_inc(u1_ready, 1)
                if c == 1:
                    pe.wait_ge(hTf_ready, 2 * KD)
                    small_feature_major(wif, 2 * H)
                if c == 3:
                    turn_gates(1, 2 * H)

            half_tokens(N_IN1 + 4, (5, 6), (n_hi[2], n_lo), v1_ready)
            half_tokens(N_IN1 + 5, (5, 6), (n_hi[2], n_lo), v1_ready)
            pe.wait_ge(u1_copied, 1)
            half_tokens(N_IN1 + 6, (7, 1), (n_hi[2], n_lo), v1_ready)
            half_tokens(N_IN1 + 7, (7, 1), (n_hi[2], n_lo), v1_ready)
            pe.wait_ge(logf_ready, 2)
            cumulate(ps[0][:, 64:64 + 2 * H], S3(14)).then_inc(cum_ready, 1)
            pe.wait_ge(u1_copied, 4)
            half_tokens(N_IN1 + 8, (2, 3), (n_hi[2], n_lo), o1_ready)
            half_tokens(N_IN1 + 9, (2, 3), (n_hi[2], n_lo), o1_ready)
            pe.wait_ge(cum_copied, 2)
            for tt in range(TT):
                last = pe.transpose(ps[0][0:H, P + tt * P:P + (tt + 1) * P], S3(16)[:, tt, :], ident[:, :])
            last.then_inc(cumT_ready, 1)
            pe.wait_ge(v1_copied, 1)
            half_tokens(N_IN1 + 10, (4, 5), (n_hi[2], n_lo), o1_ready)
            half_tokens(N_IN1 + 11, (4, 5), (n_hi[2], n_lo), o1_ready)
            pe.wait_ge(gT_ready, 1)
            for t in range(TT):
                last = pe.transpose(ps[0][:, 400 + t * H:400 + (t + 1) * H], GT[:, t * P:(t + 1) * P], ident[0:H, 0:H])
            last.then_inc(gt_back, 1)
            arrived(T_QK1)
            w = tile(T_QK1, 2 * H, P)
            pe.wait_ge(v1_copied, 4)
            for h in range(H):
                b = (6, 7, 1, 2)[h % 4]
                pe.wait_ge(uT_ready, h + 1)
                if h == 3:
                    pe.wait_ge(og_ready, 1)
                if h >= 4:
                    pe.wait_ge(qk1_copied, 2 * (h - 3))
                last = pe.matmul(ps[b][:, 0:T], w[:, h, :], uT[:, h, :], start=True, stop=True)
                if h == 0:
                    last.then_inc(lsplit_used, 1)
                pe.matmul(ps[b][:, T:2 * T], w[:, H + h, :], uT[:, h, :], start=True, stop=True).then_inc(qk1_ready, 1)

            def decay_and_scores(h):
                s, e = ps[1 + h % 2], ps[3 + h % 2]
                if h >= 2:
                    pe.wait_ge(w_ready, h - 1)
                last = pe.matmul(s[:, 0:T], kT1[:, h, 0:P], qT1[:, h, :], start=True, stop=True)
                if h == 0:
                    last.then_inc(tiles_used, 1)
                pe.matmul(s[:, T:T + P], kT1[:, h, P:T], qT1[:, h, P:T], start=True, stop=True)
                pe.matmul(e[:, 0:T], neg_sel[:, h, :], GT[:, :], start=True, stop=False)
                pe.matmul(e[:, 0:P], ident[:, :], mask_kq[:, :], start=False, stop=True)
                pe.matmul(e[:, T:T + P], neg_sel[:, h, :], GT[:, P:T], start=True, stop=False)
                pe.matmul(e[:, T:T + P], ident[:, :], mask_kq[:, :], start=False, stop=True).then_inc(ex_ready, 1)

            def numerators(h):
                o = ps[5 + h % 2]
                pe.wait_ge(w_ready, h + 1)
                if h >= 2:
                    pe.wait_ge(hc_ready, TT * (h - 1))
                pe.matmul(o[:, 0:P + 1], wts[:, h % 2, 0:P], v_aug[:, 0, h, :], start=True, stop=True)
                pe.matmul(o[:, T:T + P + 1], wts[:, h % 2, P:T], v_aug[:, 0, h, :], start=True, stop=False)
                pe.matmul(o[:, T:T + P + 1], wts[:, h % 2, T:T + P], v_aug[:, 1, h, :], start=False,
                          stop=True).then_inc(num_ready, 1)

            pe.wait_ge(m_ready, 1)
            pe.wait_ge(qk1_copied, 2 * H)
            pe.wait_ge(og_ready, 4)
            for i in range(H + 1):
                if i < H:
                    decay_and_scores(i)
                if i >= 1:
                    numerators(i - 1)
                if i in (5, 7):
                    turn_heads((i - 5) // 2)
            out_proj(T_OUT1, catT1, (3, 1, 2, 0))
            turn(xn, xn_ready, 3, xT_ready, frees=True)
            hT_wait(0)
            small_feature_major(wr, NE)
            turn_gates(2, NE)
            pe.wait_ge(mask_ready, 1)
            cumulate(ps[0][:, 64:64 + 2 * NE], S3(8)).then_inc(split_used, SPLITS - 1)
            pe.matmul(ps[0][:, 96:96 + NE], ones[:, :], S3(8)[:, 0, :], start=True, stop=False)
            pe.matmul(ps[0][:, 96:96 + NE], ones[:, :], S3(8)[:, 1, :], start=False, stop=True).then_inc(pos_ready, 1)

            def gather(pair, q, ahead):
                pe.wait_ge(route_ready, passed(pair, q, 4 * ahead + 4, 4))
                for k in range(KD):
                    o = ps[5 + k // 4][:, (k % 4) * CAP:(k % 4 + 1) * CAP]
                    for t in range(TT):
                        last = pe.matmul(o, xn[:, t, k * P:(k + 1) * P], disp[:, t, :], start=(t == 0), stop=(t == TT - 1))
                    if k % 4 == 3:
                        last.then_inc(disp_done, 1)

            def back_to_tokens(r, pair, q, ahead, t):
                pe.wait_ge(combT_ready, passed_adds(r, pair, q, ahead + 1, 1))
                pe.wait_ge(ye_left, passed_adds(r, pair, q, ahead + 1, 1))
                pe.wait_ge(ye_right, passed_adds(r, pair, q, ahead + 1, 1))
                for n in (2 * t, 2 * t + 1):
                    half = n % 2
                    if n == 3:
                        pe.wait_ge(y_added, passed_adds(r, pair, q, 4 * ahead + 1, 4))
                    pe.matmul(ps[(5, 6, 7, 5)[n]][:, :], combT[0:CAP, t * P:(t + 1) * P],
                              ye[0:CAP, half * 512:(half + 1) * 512], start=True, stop=True).then_inc(y_done, 1)

            def expert(r, pair, q, e, final):
                for u in range(2 * NT):
                    if u < 2:
                        pe.wait_ge(xlo_ready, passed(pair, q, u + 1, 2))
                    kind, g = order[u // 2]
                    pe.wait_ge(lo_ready, passed(pair, q, 2 * RING + u + 1, 2 * NT))
                    if kind < 2:
                        w = [v[:, u % SPLITS, :].rearrange("p (k n) -> p k n", k=KD // 2) for v in (w_hi, w_lo)]
                        o = ps[kind][:, :]
                        if kind == 1 and g > 0 and u % 2 == 0:
                            pe.wait_ge(htok_ready, passed(pair, q, g, GROUPS))
                        if kind == 0 and g > 0 and u % 2 == 0:
                            pe.wait_ge(sil_ready, passed(pair, q, g, GROUPS))
                        for kk in range(KD // 2):
                            k = (u % 2) * (KD // 2) + kk
                            last = pe.matmul(o, x_hi[:, k, :], w[0][:, kk, :], start=(k == 0), stop=False)
                            if kk == 0:
                                last.then_inc(split_used, 1)
                            pe.matmul(o, x_hi[:, k, :], w[1][:, kk, :], start=False, stop=False)
                            last = pe.matmul(o, x_lo[:, k, :], w[0][:, kk, :], start=False, stop=(k == KD - 1))
                        if u % 2:
                            last.then_inc((g_done, u_done)[kind], 1)
                    else:
                        w = [v[:, u % SPLITS, :].rearrange("p (k n) -> p k n", k=CPG // 2) for v in (w_hi, w_lo)]
                        if u % 2 == 0:
                            pe.wait_ge(hlo_ready, passed(pair, q, g + 1, GROUPS))
                        for kk in range(CPG // 2):
                            f = (u % 2) * (CPG // 2) + kk
                            rows = slice(f * P, (f + 1) * P)
                            first, last_f = g == 0 and f == 0, g == GROUPS - 1 and f == CPG - 1
                            for a, b, st, en in ((h_hi, 0, first, False), (h_hi, 1, False, False), (h_lo, 0, False, last_f)):
                                for half in range(2):
                                    last = pe.matmul(ps[2 + half][:, :], a[:, g % 2, rows], w[b][:, kk, half * 512:(half + 1) * 512],
                                                     start=st, stop=en)
                                    if kk == 0 and a is h_hi and b == 0 and half == 0:
                                        last.then_inc(split_used, 1)
                        if last_f:
                            last.then_inc(ysum_done, 1)
                    if u in (U_ADD, U_ADD + 2):
                        back_to_tokens(r, pair, q, 0, u // 2)
                    if u % 2 == 0 and u >= 4 and order[u // 2 - 1][0] == 1:
                        gt = order[u // 2 - 1][1]
                        pe.wait_ge(htok_ready, passed(pair, q, gt + 1, GROUPS))
                        for j in range(CPG):
                            last = pe.transpose(ps[4][:, j * P:(j + 1) * P], htok[:, j * P:(j + 1) * P], ident[:, :])
                        last.then_inc(hidT_done, 1)
                    if u == U_COMB:
                        pe.wait_ge(y_added, passed_adds(r, pair, q, 4, 4))
                        for t in range(TT):
                            last = pe.transpose(ps[7][0:CAP, t * P:(t + 1) * P], comb[:, t, :], ident[:, :])
                        last.then_inc(combT_done, 1)
                    if u == U_GATHER and not final:
                        gather(pair, q, 1)

            def one_round(r):
                first = 0 if r is None else r * (NE // 2)
                if r is not None:
                    pe.wait_ge(y_added, r * (4 * (NE + 1)))
                gather(first, 0, 0)
                all_experts(pe, r, expert)
                for t in range(TT):
                    back_to_tokens(r, first + (NE // 2 - 1), 1, 1, t)

            all_rounds(pe, one_round)


_INS = ['x', 'l0_norm1_g', 'l0_w_in', 'l0_b_f', 'l0_dw_w', 'l0_dw_b', 'l0_cln_g', 'l0_cln_b', 'l0_w_out',
        'l0_norm2_g', 'l0_w_gate', 'l0_w_up', 'l0_w_down', 'l1_norm1_g', 'l1_w_in', 'l1_b_i', 'l1_b_f',
        'l1_conv_w', 'l1_conv_b', 'l1_wq_head', 'l1_wk_head', 'l1_hnorm_g', 'l1_w_out', 'l1_norm2_g',
        'l1_router', 'l1_e_gate', 'l1_e_up', 'l1_e_down', 'final_norm_g']


def kernel(**inputs):
    import numpy as _np
    import concourse.bacc as _bacc
    from concourse import mybir as _mybir
    from concourse.bass_utils import run_bass_kernel_spmd as _run

    nc = _bacc.Bacc("TRN2", target_bir_lowering=False, num_devices=1)
    arrays, args = {}, []
    for name in _INS:
        a = _np.ascontiguousarray(inputs[name])
        arrays[f"in_{name}_dram"] = a
        args.append(nc.dram_tensor(f"in_{name}_dram", a.shape, _mybir.dt.from_np(a.dtype), kind="ExternalInput").ap())
    out = nc.dram_tensor("out_dram", inputs["x"].shape, _mybir.dt.float32, kind="ExternalOutput").ap()
    bass_hybrid_trunk(nc, *args, out)
    r = _run(nc, [arrays], core_ids=[0])
    return r.results[0]["out_dram"]
```
